# Optimizing a Trainium2 kernel written in Bass

```python
import math
import jax
import jax.numpy as jnp
from jax import lax
import numpy as np

D_MODEL = 2048
BATCH = 1
SEQ = 256
DEPTH = 1

MLSTM_HEADS = 4
MLSTM_HEAD_DIM = 256
MLSTM_WIDTH = MLSTM_HEADS * MLSTM_HEAD_DIM
MLSTM_CHUNK = 64
CONV_WIDTH = 4
ATTN_GROUPS = ((128, 1), (512, 4), (2048, 16))
ATTN_HEADS = 8
ATTN_HEAD_DIM = 128
ATTN_WIDTH = ATTN_HEADS * ATTN_HEAD_DIM
ATTN_HEADS_TOTAL = len(ATTN_GROUPS) * ATTN_HEADS
ATTN_BLOCK = 128
REL_BUCKETS = 32
REL_MAX_DISTANCE = 2048
S5_WIDTH = 1024
S5_GROUP = 16
S5_GROUPS = S5_WIDTH // S5_GROUP
S5_STATE = 64
FF_HIDDEN = 4 * D_MODEL
N_BRANCHES = 3
NORM_EPS = 1e-6

IN_SPLITS = (
    MLSTM_WIDTH, MLSTM_WIDTH, MLSTM_WIDTH, MLSTM_WIDTH,
    MLSTM_HEADS, MLSTM_HEADS,
    3 * ATTN_HEADS_TOTAL * ATTN_HEAD_DIM,
    S5_WIDTH,
    N_BRANCHES * D_MODEL,
)
N_IN = sum(IN_SPLITS)
IN_OFFSETS = tuple(int(o) for o in np.cumsum(IN_SPLITS)[:-1])

kernel_name = "hybrid_mlstm_dilated_s5_trunk"

def rms_norm(x, g):
    xf = x.astype(jnp.float32)
    y = xf * lax.rsqrt(jnp.mean(xf * xf, axis=-1, keepdims=True) + NORM_EPS)
    return (y * g.astype(jnp.float32)).astype(x.dtype)

def split_heads(t, h):
    return t.reshape(t.shape[:-1] + (h, t.shape[-1] // h))

def causal_depthwise_conv(x, w, b):
    k = w.shape[0]
    s = x.shape[1]
    xp = jnp.pad(x, ((0, 0), (k - 1, 0), (0, 0)))
    y = b
    for j in range(k):
        y = y + w[j] * xp[:, j:j + s]
    return y

def mlstm_chunkwise(q, k, v, ig, lf):
    b, s, h, e = q.shape
    L = MLSTM_CHUNK
    nc = s // L
    k = k * (e ** -0.5)

    def chunks(t):
        t = t.reshape((b, nc, L) + t.shape[2:])
        return jnp.moveaxis(t, 1, 0).swapaxes(2, 3)

    causal = jnp.tril(jnp.ones((L, L), dtype=bool))

    def step(carry, inp):
        c_state, n_state, m_state = carry
        qc, kc, vc, igc, lfc = inp
        bcum = jnp.cumsum(lfc, axis=-1)
        dlog = bcum[..., :, None] - bcum[..., None, :] + igc[..., None, :]
        dlog = jnp.where(causal, dlog, -jnp.inf)
        m_inter = bcum + m_state[..., None]
        m_t = jnp.maximum(m_inter, jnp.max(dlog, axis=-1))
        w_intra = jnp.exp(dlog - m_t[..., None])
        w_inter = jnp.exp(m_inter - m_t)
        sc = jnp.einsum('bhtd,bhsd->bhts', qc, kc) * w_intra
        num = (jnp.einsum('bhts,bhse->bhte', sc, vc)
               + w_inter[..., None] * jnp.einsum('bhtd,bhed->bhte', qc, c_state))
        den = jnp.sum(sc, axis=-1) + w_inter * jnp.einsum('bhtd,bhd->bht', qc, n_state)
        h_out = num / jnp.maximum(jnp.abs(den), jnp.exp(-m_t))[..., None]
        b_last = bcum[..., -1]
        g = b_last[..., None] - bcum + igc
        m_new = jnp.maximum(b_last + m_state, jnp.max(g, axis=-1))
        w_s = jnp.exp(g - m_new[..., None])
        decay = jnp.exp(b_last + m_state - m_new)
        c_new = decay[..., None, None] * c_state + jnp.einsum('bhs,bhse,bhsd->bhed', w_s, vc, kc)
        n_new = decay[..., None] * n_state + jnp.einsum('bhs,bhsd->bhd', w_s, kc)
        return (c_new, n_new, m_new), h_out

    init = (jnp.zeros((b, h, e, e), jnp.float32), jnp.zeros((b, h, e), jnp.float32),
            jnp.zeros((b, h), jnp.float32))
    _, hs = lax.scan(step, init, (chunks(q), chunks(k), chunks(v), chunks(ig), chunks(lf)))
    hs = jnp.moveaxis(hs.swapaxes(2, 3), 0, 1)
    return hs.reshape(b, s, h, e)

def t5_bucket(n):
    max_exact = REL_BUCKETS // 2
    nf = jnp.maximum(n, max_exact).astype(jnp.float32)
    large = max_exact + (jnp.log(nf / max_exact) / math.log(REL_MAX_DISTANCE / max_exact)
                         * (REL_BUCKETS - max_exact)).astype(jnp.int32)
    large = jnp.minimum(large, REL_BUCKETS - 1)
    return jnp.where(n < max_exact, n, large)

def band_bias(table, dilation):
    i = jnp.arange(ATTN_BLOCK)[:, None]
    j = jnp.arange(2 * ATTN_BLOCK)[None, :]
    dist = jnp.maximum(ATTN_BLOCK + i - j, 0) * dilation
    return jnp.transpose(table[t5_bucket(dist)], (2, 0, 1)).astype(jnp.float32)

def dilated_group_attention(q, k, v, bias, window, dilation):
    b, s, h, e = q.shape
    r = dilation
    span = window // dilation
    l = s // r
    nb = -(-l // ATTN_BLOCK)
    lp = nb * ATTN_BLOCK

    def to_blocks(t):
        t = t.reshape(b, l, r, h, e).swapaxes(1, 2)
        t = jnp.pad(t, ((0, 0), (0, 0), (0, lp - l), (0, 0), (0, 0)))
        return t.reshape(b, r, nb, ATTN_BLOCK, h, e)

    def with_prev(t):
        prev = jnp.pad(t, ((0, 0), (0, 0), (1, 0), (0, 0), (0, 0), (0, 0)))[:, :, :-1]
        return jnp.concatenate([prev, t], axis=3)

    qb = to_blocks(q)
    kk = with_prev(to_blocks(k))
    vv = with_prev(to_blocks(v))
    logits = jnp.einsum('bcnqhe,bcnkhe->bcnhqk', qb, kk) * (e ** -0.5) + bias
    i = jnp.arange(ATTN_BLOCK)[:, None]
    j = jnp.arange(2 * ATTN_BLOCK)[None, :]
    rel = ATTN_BLOCK + i - j
    band = (rel >= 0) & (rel <= span)
    has_prev = (jnp.arange(nb) > 0)[:, None, None] | (j >= ATTN_BLOCK)[None]
    valid = band[None] & has_prev
    logits = jnp.where(valid[None, None, :, None], logits, -jnp.inf)
    mx = jnp.max(logits, axis=-1, keepdims=True)
    p = jnp.exp(logits - mx)
    den = jnp.sum(p, axis=-1)
    out = jnp.einsum('bcnhqk,bcnkhe->bcnqhe', p, vv) / den.swapaxes(-1, -2)[..., None]
    lse = (mx[..., 0] + jnp.log(den)).swapaxes(-1, -2)
    out = out.reshape(b, r, lp, h, e)[:, :, :l].swapaxes(1, 2).reshape(b, s, h, e)
    lse = lse.reshape(b, r, lp, h)[:, :, :l].swapaxes(1, 2).reshape(b, s, h)
    return out, lse

def dilated_attention(q, k, v, rel_bias):
    outs, lses = [], []
    for g, (window, dilation) in enumerate(ATTN_GROUPS):
        hs = slice(g * ATTN_HEADS, (g + 1) * ATTN_HEADS)
        o, lse = dilated_group_attention(q[:, :, hs], k[:, :, hs], v[:, :, hs],
                                         band_bias(rel_bias[:, hs], dilation), window, dilation)
        outs.append(o)
        lses.append(lse)
    wts = jax.nn.softmax(jnp.stack(lses), axis=0)
    return jnp.sum(wts[..., None] * jnp.stack(outs), axis=0)

def s5_combine(e1, e2):
    a1r, a1i, b1r, b1i = e1
    a2r, a2i, b2r, b2i = e2
    return (a2r * a1r - a2i * a1i, a2r * a1i + a2i * a1r,
            a2r * b1r - a2i * b1i + b2r, a2r * b1i + a2i * b1r + b2i)

def s5_ssm(u, lam_re, lam_im, log_dt, b_re, b_im, c_re, c_im, d_skip):
    bsz, s, _ = u.shape
    ug = u.reshape(bsz, s, S5_GROUPS, S5_GROUP)
    dt = jnp.exp(log_dt)[:, None]
    mag = jnp.exp(lam_re * dt)
    ab_re = mag * jnp.cos(lam_im * dt)
    ab_im = mag * jnp.sin(lam_im * dt)
    nr = ab_re - 1.0
    ni = ab_im
    den = lam_re * lam_re + lam_im * lam_im
    f_re = (nr * lam_re + ni * lam_im) / den
    f_im = (ni * lam_re - nr * lam_im) / den
    bb_re = f_re[..., None] * b_re - f_im[..., None] * b_im
    bb_im = f_re[..., None] * b_im + f_im[..., None] * b_re
    bu_re = jnp.einsum('bsgi,gpi->bsgp', ug, bb_re)
    bu_im = jnp.einsum('bsgi,gpi->bsgp', ug, bb_im)
    a_re = jnp.broadcast_to(ab_re, (1, s) + ab_re.shape)
    a_im = jnp.broadcast_to(ab_im, (1, s) + ab_im.shape)
    _, _, xr, xi = lax.associative_scan(s5_combine, (a_re, a_im, bu_re, bu_im), axis=1)
    y = (jnp.einsum('bsgp,gop->bsgo', xr, c_re) - jnp.einsum('bsgp,gop->bsgo', xi, c_im)
         + d_skip * ug)
    return y.reshape(bsz, s, S5_WIDTH)

def setup_inputs(seed: int = 0) -> dict:
    key = jax.random.key(seed)
    ks = jax.random.split(key, 26)
    f32 = jnp.float32
    L, D = DEPTH, D_MODEL

    def normal(k, shape, scale):
        return jax.random.normal(k, shape, f32) * scale

    return {
        "x": normal(ks[0], (BATCH, SEQ, D), 1.0),
        "norm1_g": 1.0 + normal(ks[1], (L, D), 0.02),
        "w_in": normal(ks[2], (L, D, N_IN), D ** -0.5),
        "conv_w": normal(ks[3], (L, CONV_WIDTH, 2 * MLSTM_WIDTH), CONV_WIDTH ** -0.5),
        "conv_b": normal(ks[4], (L, 2 * MLSTM_WIDTH), 0.02),
        "b_igate": normal(ks[5], (L, MLSTM_HEADS), 0.1),
        "b_fgate": jnp.linspace(3.0, 6.0, MLSTM_HEADS, dtype=f32) + normal(ks[6], (L, MLSTM_HEADS), 0.1),
        "mh_norm_g": 1.0 + normal(ks[7], (L, MLSTM_WIDTH), 0.02),
        "rel_bias": normal(ks[8], (REL_BUCKETS, ATTN_HEADS_TOTAL), 0.5),
        "lam_re": -0.5 + normal(ks[9], (L, S5_GROUPS, S5_STATE), 0.01),
        "lam_im": math.pi * jnp.arange(S5_STATE, dtype=f32) + normal(ks[10], (L, S5_GROUPS, S5_STATE), 0.01),
        "log_dt": jax.random.uniform(ks[11], (L, S5_GROUPS), f32, math.log(1e-3), math.log(1e-1)),
        "b_re": normal(ks[12], (L, S5_GROUPS, S5_STATE, S5_GROUP), (2 * S5_GROUP) ** -0.5),
        "b_im": normal(ks[13], (L, S5_GROUPS, S5_STATE, S5_GROUP), (2 * S5_GROUP) ** -0.5),
        "c_re": normal(ks[14], (L, S5_GROUPS, S5_GROUP, S5_STATE), S5_STATE ** -0.5),
        "c_im": normal(ks[15], (L, S5_GROUPS, S5_GROUP, S5_STATE), S5_STATE ** -0.5),
        "d_skip": normal(ks[16], (L, S5_GROUPS, S5_GROUP), 1.0),
        "w_glu": normal(ks[17], (L, S5_WIDTH, 2 * S5_WIDTH), S5_WIDTH ** -0.5),
        "w_br_a": normal(ks[18], (L, MLSTM_WIDTH, D), MLSTM_WIDTH ** -0.5),
        "w_br_b": normal(ks[19], (L, ATTN_WIDTH, D), ATTN_WIDTH ** -0.5),
        "w_br_c": normal(ks[20], (L, S5_WIDTH, D), S5_WIDTH ** -0.5),
        "w_out": normal(ks[21], (L, D, D), D ** -0.5),
        "norm2_g": 1.0 + normal(ks[22], (L, D), 0.02),
        "w_ff1": normal(ks[23], (L, D, FF_HIDDEN), D ** -0.5),
        "w_ff2": normal(ks[24], (L, FF_HIDDEN, D), FF_HIDDEN ** -0.5),
        "final_g": 1.0 + normal(ks[25], (D,), 0.02),
    }

def reference(x, norm1_g, w_in, conv_w, conv_b, b_igate, b_fgate, mh_norm_g, rel_bias,
              lam_re, lam_im, log_dt, b_re, b_im, c_re, c_im, d_skip, w_glu,
              w_br_a, w_br_b, w_br_c, w_out, norm2_g, w_ff1, w_ff2, final_g):
    dt = x.dtype
    f32 = jnp.float32
    bsz, s, _ = x.shape
    for l in range(DEPTH):
        xn = rms_norm(x, norm1_g[l])
        proj = xn @ w_in[l]
        q_m, k_m, v_m, o_m, i_m, f_m, qkv_att, u_s5, gates = jnp.split(proj, IN_OFFSETS, axis=-1)

        qk = jax.nn.silu(causal_depthwise_conv(jnp.concatenate([q_m, k_m], axis=-1),
                                               conv_w[l], conv_b[l]).astype(f32))
        q_a, k_a = jnp.split(qk, 2, axis=-1)
        h_m = mlstm_chunkwise(split_heads(q_a, MLSTM_HEADS), split_heads(k_a, MLSTM_HEADS),
                              split_heads(v_m.astype(f32), MLSTM_HEADS),
                              i_m.astype(f32) + b_igate[l].astype(f32),
                              jax.nn.log_sigmoid(f_m.astype(f32) + b_fgate[l].astype(f32)))
        h_m = h_m * lax.rsqrt(jnp.mean(h_m * h_m, axis=-1, keepdims=True) + NORM_EPS)
        h_m = h_m.reshape(bsz, s, MLSTM_WIDTH) * mh_norm_g[l].astype(f32)
        y_a = (jax.nn.sigmoid(o_m.astype(f32)) * h_m).astype(dt)

        qkv = qkv_att.astype(f32).reshape(bsz, s, 3, ATTN_HEADS_TOTAL, ATTN_HEAD_DIM)
        y_b = dilated_attention(qkv[:, :, 0], qkv[:, :, 1], qkv[:, :, 2], rel_bias)
        y_b = y_b.reshape(bsz, s, ATTN_WIDTH).astype(dt)

        y_s = s5_ssm(u_s5.astype(f32), lam_re[l].astype(f32), lam_im[l].astype(f32),
                     log_dt[l].astype(f32), b_re[l].astype(f32), b_im[l].astype(f32),
                     c_re[l].astype(f32), c_im[l].astype(f32), d_skip[l].astype(f32))
        z = jax.nn.gelu(y_s.astype(dt))
        z_lin, z_gate = jnp.split(z @ w_glu[l], 2, axis=-1)
        y_c = z_lin * jax.nn.sigmoid(z_gate)

        g_a, g_b, g_c = jnp.split(jax.nn.sigmoid(gates), 3, axis=-1)
        mix = g_a * (y_a @ w_br_a[l]) + g_b * (y_b @ w_br_b[l]) + g_c * (y_c @ w_br_c[l])
        x = x + mix @ w_out[l]

        hn = rms_norm(x, norm2_g[l])
        x = x + jnp.square(jax.nn.relu(hn @ w_ff1[l])) @ w_ff2[l]
    return rms_norm(x, final_g)


_drawn_inputs = setup_inputs


def setup_inputs(seed=0):
    import zlib

    import numpy as np

    out = dict(_drawn_inputs(seed))
    spreads = {}
    factors = {'norm1_g': 4.776,
     'conv_b': 64.0,
     'b_igate': 200.0,
     'mh_norm_g': 76.066,
     'lam_re': 64.0,
     'lam_im': 30.072,
     'log_dt': 30.456,
     'b_re': 42.84,
     'b_im': 41.784,
     'c_re': 41.824,
     'c_im': 42.032,
     'norm2_g': 10.927,
     'final_g': 20.376}
    for name, (base, spread) in spreads.items():
        noise = np.random.default_rng([zlib.crc32(name.encode()), seed]).standard_normal(out[name].shape)
        drawn = base * np.exp(spread * noise) if base else spread * noise
        out[name] = jnp.asarray(drawn.astype(out[name].dtype))
    for name, factor in factors.items():
        out[name] = (out[name] * factor).astype(out[name].dtype)
    return out
```

```python
import math
from contextlib import ExitStack

import concourse.bass as bass
from concourse import mybir

F32 = mybir.dt.float32
F32R = mybir.dt.float32r
ACT = mybir.ActivationFunctionType
ALU = mybir.AluOpType
AX_X = mybir.AxisListType.X

P = 128
TOK = 256
TT = TOK // P
D = 2048
KD = D // P
EPS = 1e-6
MH, MW = 4, 1024
NG, AH = 3, 8
GW = 64
ST = 64
FF = 4 * D
Q_M, K_M, V_M, O_M, IF_M = 0, 1024, 2048, 3072, 4096
Q_A, K_A, V_A = 4104, 4104 + 3072, 4104 + 6144
U_S, GATE = 13320, 14344

LOADW, PIECEW, AHEAD = 2048, 1024, 4
C_LOADS = 16 * 10
SLOTS = 4
C_N1, C_N2, C_CW, C_CB, C_MH, C_DS = 0, 16, 32, 96, 112, 120
PK_B, PK_C, PK_U, PK_FH, PK_FL, PK_MAG, PK_D, PKW = 0, 256, 512, 768, 772, 776, 780, 784
NEG = -1.0e30
ROUND = 12582912.0
GRID16 = 192.0


def inv_two_pi():
    rest, parts = 1.0 / (2.0 * math.pi), []
    for _ in range(3):
        m, e = math.frexp(rest)
        part = math.ldexp(math.floor(m * 4096.0), e - 12)
        parts.append(part)
        rest -= part
    return parts


class Phase:
    def __init__(self, load, block):
        self.load, self.piece, self.block = load, 2 * load, block


LOADS_U, BLOCKS_U = 8, 2
LOADS_A, BLOCKS_A = 16, 4
LOADS_B, BLOCKS_B = 36, 18
LOADS_C, BLOCKS_C = 4, 2
LOADS_D, BLOCKS_D = 36, 12
LOADS_W, BLOCKS_W = 8, 2
LOADS_F1, BLOCKS_F1 = 8, 2
LOADS_F2, BLOCKS_F2 = 16, 2
HALF_LOADS, HALF_BLOCKS = 4 * LOADS_F1 + 2 * LOADS_F2, 4 * BLOCKS_F1 + 2 * BLOCKS_F2
PU = Phase(0, 0)
PI = Phase(PU.load + LOADS_U, PU.block + BLOCKS_U)
PA = Phase(PI.load + 1, PI.block + 1)
PB = Phase(PA.load + 2 * LOADS_A, PA.block + 2 * BLOCKS_A)
PC = Phase(PB.load + 2 * LOADS_B, PB.block + 2 * BLOCKS_B)
PD = Phase(PC.load + 2 * LOADS_C, PC.block + 2 * BLOCKS_C)
PW = Phase(PD.load + 2 * LOADS_D, PD.block + 2 * BLOCKS_D)
PF = Phase(PW.load + 2 * LOADS_W, PW.block + 2 * BLOCKS_W)
TOTAL_LOADS = PF.load + 2 * HALF_LOADS
TOTAL_PIECES = 2 * TOTAL_LOADS


def trunk(nc, x, norm1_g, w_in, conv_w, conv_b, b_igate, b_fgate, mh_norm_g, rel_bias, lam_re, lam_im,
          log_dt, b_re, b_im, c_re, c_im, d_skip, w_glu, w_br_a, w_br_b, w_br_c, w_out, norm2_g,
          w_ff1, w_ff2, final_g, ident_c, consts_c, onehot_c, relmask_c, out):
    ctx = ExitStack()
    with ctx:
        def sem(name):
            return ctx.enter_context(nc.semaphore(name))

        top = [(nc.sbuf_base + 31) // 32 * 32]

        def at(name, shape, off, dt=F32):
            return nc.alloc_sbuf_tensor_at(name, shape, dt, offset=off)

        def size(shape):
            n = 4
            for s in shape[1:]:
                n *= s
            return (n + 31) // 32 * 32

        def take(name, shape, dt=F32):
            t = at(name, shape, top[0], dt)
            top[0] += size(shape)
            return t

        def region(start, items):
            got = []
            for name, shape, dt in items:
                got.append(at(name, shape, start, dt))
                start += size(shape)
            assert start <= nc.sbuf_usable_end, (items[-1][0], start, nc.sbuf_usable_end)
            return got

        raw = take("raw", [P, SLOTS, LOADW])
        w_hi = take("w_hi", [P, SLOTS, PIECEW], F32R)
        w_lo = take("w_lo", [P, SLOTS, PIECEW], F32R)
        x_hi = take("x_hi", [P, KD, TOK], F32R)
        x_lo = take("x_lo", [P, KD, TOK], F32R)
        ident = take("ident", [P, P])
        vec = take("vec_cols", [P, P])
        consts = take("consts", [P, 384 + 256 + 8])
        masks = consts[:, 0:384]
        iota_t = consts[:, 384:640]
        par = consts[:, 640:648]
        half_pi = par[:, 5:6]
        runmax_bc = take("runmax_bc", [P, MH, TOK])
        acols = take("acols", [P, 4, MH])
        small = take("small", [P, 48])
        gate_bias = take("gate_bias", [8, 1])
        ldt = take("log_dt_pairs", [96, 2])
        conv_s = take("conv_s", [P, 48])
        y_base = top[0]
        y_a = take("y_a", [P, 8, TOK])
        y_b = take("y_b", [P, 8, TOK])
        y_s = take("y_s", [P, 8, TOK])
        r0 = top[0]
        pack, s5s, psi, kk2, c2, s2, m1, m2, zin, n1, n2 = region(r0, [
            ("pack", [P, 8, PKW], F32), ("s5_now", [P, PKW], F32), ("psi", [P, 4, TOK], F32),
            ("kk2", [P, 2, TOK], F32), ("cos2", [P, 2, TOK], F32), ("sin2", [P, 2, TOK], F32),
            ("m1", [P, 2, TOK], F32), ("m2", [P, 2, TOK], F32), ("zin", [P, 2, TOK], F32),
            ("n1", [P, 2, TOK], F32), ("n2", [P, 2, TOK], F32)])
        r_s5now = r0 + size([P, 8, PKW])
        r1 = r_s5now + size([P, PKW]) + 4096 + 8 * 2048
        (xf,) = region(r0, [("xf", [P, KD, TOK], F32)])
        (s5p,) = region(r_s5now, [("s5p", [P, 30, 32], F32)])
        (b_raw, c_raw, bb_t) = region(r_s5now + 3840, [
            ("b_raw", [P, 2, 32, 16], F32), ("c_raw", [P, 2, 8, 64], F32), ("bb_t", [P, 2, 32, 16], F32)])
        xs, b_pad, c_pad = region(r1, [("xs", [P, TT, D], F32), ("b_pad", [P, 2, 32, 32], F32),
                                       ("c_pad", [P, 2, 8, P], F32)])
        (vrows, srows, table, onehot, relmask, relval) = region(r_s5now + 3840 + 12288, [
            ("vrows", [P, P], F32), ("srows", [96, P], F32), ("table", [32, 24], F32),
            ("onehot", [32, 384], F32), ("relmask", [24, 384], F32), ("relval", [24, 384], F32)])
        (gates8, gtmp, fcum, gaf, gr, neg_sel, neg_bc) = region(r1, [
            ("gates8", [8, TOK], F32), ("gtmp", [8, 3, TOK], F32), ("fcum", [8, TOK], F32),
            ("gaf", [MH, 2, TOK], F32), ("gr", [MH, 2, TOK], F32), ("neg_sel", [8, MH], F32),
            ("neg_bc", [MH, MH, P], F32)])
        (qk_raw, acc, qT, kT, v_ext, o_sig, wexp, pT) = region(r1, [
            ("qk_raw", [P, 4, TOK], F32), ("acc", [P, 4, TOK], F32), ("qT", [P, 4, TOK], F32),
            ("kT", [P, 4, TOK], F32), ("v_ext", [P, TT, 2, 257], F32), ("o_sig", [P, 4, TOK], F32),
            ("wexp", [P, 2, 384], F32), ("pT", [P, 2, 384], F32)])
        (hn,) = region(r1 + 4096, [("hn", [P, TT, TOK], F32)])
        (aq, ak, av, rel, prob, probT) = region(r1, [
            ("aq", [P, 6, TOK], F32), ("ak", [P, 6, TOK], F32), ("av", [P, TT, NG, 2 * P], F32),
            ("rel", [P, NG, TOK], F32), ("prob", [P, NG * TOK + NG * P], F32), ("probT", [P, NG, 384], F32)])
        (mix_hi, mix_lo) = region(y_base, [("mix_hi", [P, KD, TOK], F32R), ("mix_lo", [P, KD, TOK], F32R)])
        r2 = y_base + 32768
        (y_hi, y_lo) = region(r2, [("y_hi", [P, 3, 8, TOK], F32R), ("y_lo", [P, 3, 8, TOK], F32R)])
        r3 = r2 + 49152
        (z_hi, z_lo) = region(r3, [("z_hi", [P, 8, TOK], F32R), ("z_lo", [P, 8, TOK], F32R)])
        (z_lin, z_sig) = region(y_base + 24576, [("z_lin", [P, 4, TOK], F32), ("z_sig", [P, 4, TOK], F32)])
        (gate_sig, mix, mix_t) = region(r3, [
            ("gate_sig", [P, NG, 4, TOK], F32), ("mix", [P, 4, TOK], F32), ("mix_t", [P, 4, TOK], F32)])
        (x1,) = region(r3, [("x1", [P, TT, D], F32)])
        (h_hi, h_lo) = region(y_base, [("h_hi", [P, 32, TOK], F32R), ("h_lo", [P, 32, TOK], F32R)])
        (xf2,) = region(y_base, [("xf2", [P, KD, TOK], F32)])
        (hs,) = region(y_base + 65536, [("hs", [P, TT, D], F32)])
        (relu, relu2) = region(y_base + 65536, [("relu", [P, PIECEW], F32), ("relu2", [P, PIECEW], F32)])
        (sq_junk,) = region(y_base, [("sq_junk", [P, TT, D], F32)])
        (fg_bc,) = region(y_base + 65536 + 8192, [("fg_bc", [P, D], F32)])
        assert y_base + 65536 + 16384 <= r3

        ps = ctx.enter_context(nc.psum_tensor("ps", [P, 8, 512], F32))
        SPARE = 4
        B_SC1, B_SC0, B_PV = 2, 4, 5
        B_H = (4, 5)
        B_Y, B_BU = 6, 7

        rel_rows = nc.dram_tensor("rel_rows", (24, 384), F32).ap()
        rel_tiles = nc.dram_tensor("rel_tiles", (AH, P, NG, TOK), F32).ap()

        raw_loaded = [sem(f"raw_loaded{i}") for i in range(SLOTS)]
        hi_ready, lo_ready_v, lo_ready_g = sem("hi_ready"), sem("lo_ready_v"), sem("lo_ready_g")
        piece_done = sem("piece_done")
        psum_free = [sem("psum_free0"), sem("psum_free1")]
        x_loaded, vrows_loaded, c_loaded, s5_loaded, srows_ready = (
            sem("x_loaded"), sem("vrows_loaded"), sem("c_loaded"), sem("s5_loaded"), sem("srows_ready"))
        rel_stored, rel_spread = sem("rel_stored"), sem("rel_spread")
        sumsq_ready, inv_ready, root_ready, xs_ready = sem("sumsq_ready"), sem("inv_ready"), sem("root_ready"), sem("xs_ready")
        trans_ready, xf_ready, xhi_ready, xlo_ready = sem("trans_ready"), sem("xf_ready"), sem("xhi_ready"), sem("xlo_ready")
        cols_ready, cols_copied, relval_ready, relval_copied = sem("cols_ready"), sem("cols_copied"), sem("relval_ready"), sem("relval_copied")
        par_v, par_a = sem("par_v"), sem("par_a")
        bpad_ready, btr_ready, pack_ready = sem("bpad_ready"), sem("btr_ready"), sem("pack_ready")
        g8_a, g8_v, g8_p = sem("g8_a"), sem("g8_v"), sem("g8_p")
        phase_done = sem("phase_done")
        conv_in, conv_acc, conv_sig, qk_ready = sem("conv_in"), sem("conv_acc"), sem("conv_sig"), sem("qk_ready")
        v_ready, o_ready, wexp_in, wexp_ready = sem("v_ready"), sem("o_ready"), sem("wexp_in"), sem("wexp_ready")
        sT_ready, pT_ready, num_ready, rec_ready, hss_ready, hinv_ready = (
            sem("sT_ready"), sem("pT_ready"), sem("num_ready"), sem("rec_ready"), sem("hss_ready"), sem("hinv_ready"))
        hroot_ready, hn_ready, hT_ready, hT_copied = sem("hroot_ready"), sem("hn_ready"), sem("hT_ready"), sem("hT_copied")
        s5_staged, psi_ready, sins_ready, s2_ready = sem("s5_staged"), sem("psi_ready"), sem("sins_ready"), sem("s2_ready")
        bu_ready, bu_free, z_ready, rot_done, xr_ready, y_done = (
            sem("bu_ready"), sem("bu_free"), sem("z_ready"), sem("rot_done"), sem("xr_ready"), sem("y_done"))
        ys_ready, gelu_in, gelu_sig, unit_done = sem("ys_ready"), sem("gelu_in"), sem("gelu_sig"), sem("unit_done")
        aq_ready, ak_ready, av_ready, rel_loaded = sem("aq_ready"), sem("ak_ready"), sem("av_ready"), sem("rel_loaded")
        scored, logits_ready, exps_ready, prob_ready = sem("scored"), sem("logits_ready"), sem("exps_ready"), sem("prob_ready")
        probT_made, probT_ready, att_out, att_copied = sem("probT_made"), sem("probT_ready"), sem("att_out"), sem("att_copied")
        z_split_a, z_split_v = sem("z_split_a"), sem("z_split_v")
        glu_in, glu_out, y_split_a, y_split_v = sem("glu_in"), sem("glu_out"), sem("y_split_a"), sem("y_split_v")
        gsig_ready, mix_ready, mixhi_ready, mix_done = sem("gsig_ready"), sem("mix_ready"), sem("mixhi_ready"), sem("mix_done")
        x1_loaded, x1_done = sem("x1_loaded"), sem("x1_done")
        relu_ready, hhi_ready, h_ready = sem("relu_ready"), sem("hhi_ready"), sem("h_ready")
        fg_loaded, out_ready, stored = sem("fg_loaded"), sem("out_ready"), sem("stored")

        def bcast(ap, pos, n):
            dims = [list(d) for d in ap.ap]
            return bass.AP(ap.tensor, ap.offset, dims[:pos] + [[0, n]] + dims[pos:])

        def f(ap):
            return ap.bitcast(F32)

        def barrier(eng, n):
            eng.drain()
            eng.sem_inc(phase_done, 1)
            eng.wait_ge(phase_done, n * 4)

        def split_hi(act, s, o8):
            s += AHEAD
            if not isinstance(o8, int) or s + 8 * o8 < TOTAL_PIECES:
                load = s // 2
                act.wait_ge(raw_loaded[load % SLOTS], 16 * (load // SLOTS + 1) + 16 * o8)
                if s >= SLOTS:
                    act.wait_ge(piece_done, s - SLOTS + 1 + 8 * o8)
                act.activation(w_hi[:, s % SLOTS, :], raw[:, load % SLOTS, s % 2 * PIECEW:(s % 2 + 1) * PIECEW],
                               ACT.Copy).then_inc(hi_ready, 1)

        def split_lo(eng, s, o8):
            s += AHEAD
            mine = (s % SLOTS == 3) == (eng is nc.gpsimd)
            if mine and (not isinstance(o8, int) or s + 8 * o8 < TOTAL_PIECES):
                eng.wait_ge(hi_ready, s + 1 + 8 * o8)
                if eng is nc.gpsimd:
                    eng.wait_ge(lo_ready_v, s - s // SLOTS + 6 * o8)
                load = s // 2
                eng.tensor_tensor(w_lo[:, s % SLOTS, :], raw[:, load % SLOTS, s % 2 * PIECEW:(s % 2 + 1) * PIECEW],
                                  f(w_hi[:, s % SLOTS, :]), ALU.subtract).then_inc(
                    lo_ready_g if eng is nc.gpsimd else lo_ready_v, 1)

        def split_first(do, eng):
            for s in range(AHEAD):
                do(eng, s - AHEAD, 0)

        def split_unless_last(do, eng, h, i):
            with eng.If(h * 2 + i < 3):
                for s in range(32 - AHEAD, 32):
                    do(eng, PF.piece + 64 + s, h * 16 + i * 4)

        def block_done(eng, s, n, o8):
            eng.wait_ge(piece_done, s + n + 8 * o8)

        def gemm(pe, s, o8, block, o2, cols, tokens, hi, lo, kk0=0, npieces=8, narrow=False, after=None, xs_wait=None):
            kts = PIECEW // cols
            free = block // 2
            if free > 0:
                pe.wait_ge(psum_free[block % 2], free + o2)
            bank0 = block % 2 if narrow else 2 * (block % 2)
            for q in range(npieces):
                n = s + q + 1
                if (s + q) % SLOTS == 3:
                    pe.wait_ge(lo_ready_g, n // SLOTS + 2 * o8)
                else:
                    pe.wait_ge(lo_ready_v, n - n // SLOTS + 6 * o8)
                if xs_wait is not None:
                    xs_wait(q)
                slot = (s + q) % SLOTS
                whi = w_hi[:, slot, :].rearrange("p (k n) -> p k n", k=kts)
                wlo = w_lo[:, slot, :].rearrange("p (k n) -> p k n", k=kts)
                for k in range(kts):
                    kk = q * kts + k
                    first, last = kk == 0, (q == npieces - 1 and k == kts - 1)
                    if tokens:
                        for t in range(TT):
                            o = ps[:, bank0, t * cols:(t + 1) * cols] if narrow else ps[:, bank0 + t, 0:cols]
                            tk = slice(t * P, (t + 1) * P)
                            st = first and (t == 0 or not narrow)
                            pe.matmul(o, hi[:, kk0 + kk, tk], whi[:, k, :], start=st, stop=False, skip_group_check=True)
                            pe.matmul(o, hi[:, kk0 + kk, tk], wlo[:, k, :], start=False, stop=False, skip_group_check=True)
                            mm = pe.matmul(o, lo[:, kk0 + kk, tk], whi[:, k, :], start=False, stop=last, skip_group_check=True)
                    else:
                        for c in range(cols // P):
                            o = ps[:, bank0 + c // 2, c % 2 * TOK:(c % 2 + 1) * TOK]
                            cs = slice(c * P, (c + 1) * P)
                            st = first and c % 2 == 0
                            pe.matmul(o, whi[:, k, cs], hi[:, kk0 + kk, :], start=st, stop=False, skip_group_check=True)
                            pe.matmul(o, whi[:, k, cs], lo[:, kk0 + kk, :], start=False, stop=False, skip_group_check=True)
                            mm = pe.matmul(o, wlo[:, k, cs], hi[:, kk0 + kk, :], start=False, stop=last, skip_group_check=True)
                mm.then_inc(piece_done, 1)
                if after is not None:
                    after(q)

        block = ctx.enter_context(nc.Block())

        @block.sync
        def _(sp):
            def load(s, o4, src):
                if s >= SLOTS:
                    n = 2 * (s - SLOTS) + 2
                    if n % SLOTS == 0:
                        sp.wait_ge(lo_ready_g, n // SLOTS + 2 * o4)
                    else:
                        sp.wait_ge(lo_ready_v, n - n // SLOTS + 6 * o4)
                sp.dma_start(raw[:, s % SLOTS, :].rearrange("p (k n) -> p k n", k=src.shape[1]),
                             src).then_inc(raw_loaded[s % SLOTS], 16)

            w_in_k = w_in[0].rearrange("(k p) n -> p k n", p=P)

            def cols(w, k0, kt, c0, n, turn=0):
                return w[:, k0:k0 + kt, c0:][:, :, bass.ds(turn, n)]

            sp.dma_start(xs[:], x[0].rearrange("(t p) n -> p t n", p=P)).then_inc(x_loaded, 16)
            for j in range(2):
                for m in range(4):
                    load(4 * j + m, 0, cols(w_in_k, 4 * m, 4, U_S + 512 * j, 512))
            load(PI.load, 0, cols(w_in_k, 0, KD, IF_M, P))
            with sp.Fori(0, 2) as i:
                n = PA.load
                for base in (Q_M, K_M, V_M, O_M):
                    for m in range(4):
                        load(n, 4 * i, cols(w_in_k, 4 * m, 4, base, 512, i * 512))
                        n += 1
            with sp.Fori(0, 2) as i:
                n = PB.load
                for u in range(2):
                    for base in (Q_A, K_A, V_A):
                        for g in range(NG):
                            for m in range(2):
                                load(n, 9 * i, cols(w_in_k, 8 * m, 8, base + g * AH * P + u * 256, 256, i * 512))
                                n += 1
            w_glu_k = w_glu[0].rearrange("(k p) n -> p k n", p=P)
            with sp.Fori(0, 2) as i:
                n = PC.load
                for base in (0, 1024):
                    for m in range(2):
                        load(n, i, cols(w_glu_k, 4 * m, 4, base, 512, i * 512))
                        n += 1
            br_k = [w[0].rearrange("(k p) n -> p k n", p=P) for w in (w_br_a, w_br_b, w_br_c)]
            with sp.Fori(0, 2) as i:
                n = PD.load
                for u in range(2):
                    for b in range(3):
                        for m in range(4):
                            load(n, 9 * i, cols(w_in_k, 4 * m, 4, GATE + b * D + u * 512, 512, i * 1024))
                            n += 1
                        for m in range(2):
                            load(n, 9 * i, cols(br_k[b], 4 * m, 4, u * 512, 512, i * 512 * 2))
                            n += 1
            w_out_k = w_out[0].rearrange("(k p) n -> p k n", p=P)
            with sp.Fori(0, 2) as i:
                n = PW.load
                for u in range(2):
                    for m in range(4):
                        load(n, 2 * i, cols(w_out_k, 4 * m, 4, u * 512, 512, i * 1024))
                        n += 1
            ff1_k = w_ff1[0].rearrange("(k p) n -> p k n", p=P)
            ff2_k = w_ff2[0].rearrange("(h k p) n -> p h k n", p=P, h=2)
            with sp.Fori(0, 2) as h:
                with sp.Fori(0, 4) as i:
                    n = PF.load
                    for u in range(2):
                        for m in range(4):
                            load(n, 16 * h + 2 * i, cols(ff1_k, 4 * m, 4, u * 512, 512, h * 4096 + i * 1024))
                            n += 1
                with sp.Fori(0, 2) as i:
                    n = PF.load + 4 * LOADS_F1
                    for u in range(2):
                        for m in range(8):
                            load(n, 16 * h + 4 * i,
                                 ff2_k[:, :, :, u * 512:][:, bass.ds(h, 1), 4 * m:4 * m + 4, bass.ds(i * 1024, 512)].rearrange(
                                     "p h k n -> p (h k) n"))
                            n += 1
            sp.wait_ge(out_ready, 1)
            sp.dma_start(out[0].rearrange("(t p) n -> p t n", p=P), x1[:]).then_inc(stored, 16)
            sp.wait_ge(stored, 16)

        @block.tensor
        def _(pe):
            def transposes(src, n0):
                for b in range(8):
                    if b >= 4:
                        pe.wait_ge(xf_ready, n0 + b - 3)
                    for k in range(2):
                        for t in range(TT):
                            mm = pe.transpose(ps[:, SPARE + b % 4, k * TOK + t * P:k * TOK + (t + 1) * P],
                                              src[:, t, (2 * b + k) * P:(2 * b + k + 1) * P], ident[:])
                    mm.then_inc(trans_ready, 1)

            pe.wait_ge(vrows_loaded, 96)
            pe.wait_ge(srows_ready, 1)
            pe.transpose(ps[:, 0, 0:P], vrows[:], ident[:])
            pe.transpose(ps[:, 0, P:P + 96], srows[:], ident[0:96, 0:96])
            pe.matmul(ps[0:24, 1, 0:384], table[:], onehot[:], start=True, stop=True).then_inc(cols_ready, 1)
            pe.wait_ge(xs_ready, 2)
            transposes(xs, 0)
            pe.wait_ge(cols_copied, 2)

            def xn_wait(q):
                pe.wait_ge(xlo_ready, q + 1)
            gemm(pe, 0, 0, 0, 0, 512, False, x_hi, x_lo, xs_wait=xn_wait)
            gemm(pe, 8, 0, 1, 0, 512, False, x_hi, x_lo)
            for which, padded in enumerate((b_pad, c_pad)):
                pe.wait_ge(bpad_ready, which + 1)
                for b in range(4):
                    pe.wait_ge(xf_ready, 8)
                    if which:
                        pe.wait_ge(pack_ready, b + 1)
                    for h in range(2):
                        for ri in range(2):
                            t = 2 * b + h
                            src = (padded[:, ri, 4 * t:4 * t + 4, :].rearrange("p j c -> p (j c)") if which == 0
                                   else padded[:, ri, t, :])
                            mm = pe.transpose(ps[:, SPARE + b, h * 256 + ri * P:h * 256 + (ri + 1) * P], src, ident[:])
                    mm.then_inc(btr_ready, 1)
            gemm(pe, PI.piece, 0, PI.block, 0, P, False, x_hi, x_lo, npieces=2)
            pe.wait_ge(pack_ready, 8)
            pe.wait_ge(g8_v, 1)
            pe.matmul(ps[0:MH, SPARE, 0:TOK], ident[0:8, 0:MH], gates8[:], start=True, stop=False, skip_group_check=True)
            pe.matmul(ps[0:MH, SPARE, 0:TOK], neg_sel[:], fcum[:], start=False, stop=True, skip_group_check=True)
            pe.matmul(ps[0:MH, SPARE, TOK:2 * TOK], ident[0:8, MH:2 * MH], fcum[:], start=False, stop=True,
                      skip_group_check=True).then_inc(g8_p, 1)
            pe.wait_ge(g8_v, 2)
            pe.wait_ge(g8_a, 3)
            for h in range(MH):
                pe.matmul(ps[:, SPARE + h // 2, h % 2 * TOK:(h % 2 + 1) * TOK], neg_bc[:, h, :], gr[:, 0, :],
                          start=h % 2 == 0, stop=True, skip_group_check=True)
            for t in range(TT):
                pe.transpose(ps[:, SPARE + 2, t * MH:(t + 1) * MH], gaf[:, 0, t * P:(t + 1) * P], ident[0:MH, 0:MH])
                mm = pe.transpose(ps[:, SPARE + 2, (2 + t) * MH:(3 + t) * MH], gr[:, 1, t * P:(t + 1) * P],
                                  ident[0:MH, 0:MH])
            mm.then_inc(g8_p, 1)
            barrier(pe, 1)

            def s5_unit(n, q):
                if q in (3, 6, 10, 13):
                    j = (3, 6, 10, 13).index(q)
                    if j == 0:
                        pe.wait_ge(s5_staged, n + 1)
                    pe.wait_ge(bu_free, n * 4 + j + 1)
                    rows = slice(32 * j, 32 * j + 32)
                    for ri in range(2):
                        mm = pe.matmul(ps[:, B_BU, ri * TOK:(ri + 1) * TOK],
                                       s5s[rows, PK_B + ri * P:PK_B + (ri + 1) * P], s5s[rows, PK_U:PK_U + TOK],
                                       start=ri == 0, stop=True, skip_group_check=True)
                    mm.then_inc(bu_ready, 1)
                if q in (6, 10, 13, 16):
                    j = (6, 10, 13, 16).index(q)
                    if j == 0:
                        pe.wait_ge(ys_ready, n + 1)
                    pe.wait_ge(xr_ready, n * 4 + j + 1)
                    for ri in range(2):
                        mm = pe.matmul(ps[32 * j:32 * j + 32, B_Y, 0:TOK],
                                       s5s[:, PK_C + ri * P + 32 * j:PK_C + ri * P + 32 * j + 32], n1[:, ri, :],
                                       start=ri == 0, stop=ri == 1, skip_group_check=True)
                    mm.then_inc(y_done, 1)

            with pe.Fori(0, 2) as i:
                def after(pos):
                    s5_unit(i, pos)
                    if pos in (19, 20):
                        h = pos - 19
                        if h == 0:
                            pe.wait_ge(qk_ready, i * 2 + 2)
                        for e in range(2):
                            pe.matmul(ps[:, B_H[h], 0:TOK], kT[:, 2 * h + e, 0:P], qT[:, 2 * h + e, :],
                                      start=e == 0, stop=e == 1, skip_group_check=True)
                        for e in range(2):
                            mm = pe.matmul(ps[:, B_H[h], TOK:TOK + P], kT[:, 2 * h + e, P:TOK],
                                           qT[:, 2 * h + e, P:TOK], start=False, stop=e == 1,
                                           skip_group_check=True)
                        mm.then_inc(sT_ready, 1)
                    if pos in (25, 29):
                        h = (25, 29).index(pos)
                        if h == 0:
                            pe.wait_ge(v_ready, i + 1)
                        pe.wait_ge(pT_ready, i * 2 + 2)
                        if h == 1:
                            pe.wait_ge(hT_copied, i * 2 + 1)
                        pe.matmul(ps[:, B_H[0], 0:257], pT[:, h, 0:P], v_ext[:, 0, h, :], start=True, stop=True)
                        pe.matmul(ps[:, B_H[1], 0:257], pT[:, h, P:TOK], v_ext[:, 0, h, :], start=True, stop=False)
                        pe.matmul(ps[:, B_H[1], 0:257], pT[:, h, TOK:384], v_ext[:, 1, h, :], start=False,
                                  stop=True).then_inc(num_ready, 1)
                    if pos in (27, 31):
                        h = (27, 31).index(pos)
                        pe.wait_ge(hn_ready, i * 2 + h + 1)
                        for e in range(2):
                            for t in range(TT):
                                mm = pe.transpose(ps[:, B_H[0], e * TOK + t * P:e * TOK + (t + 1) * P],
                                                  hn[:, t, e * P:(e + 1) * P], ident[:])
                        mm.then_inc(hT_ready, 1)
                for b in range(BLOCKS_A):
                    gemm(pe, PA.piece + 8 * b, 4 * i, PA.block + b, 2 * i, 512, b == 2, x_hi, x_lo,
                         after=lambda q, b=b: after(8 * b + q))
            barrier(pe, 2)
            with pe.Fori(0, 2) as i:
                for u in range(2):
                    def after(pos):
                        if u == 0 or pos < 18:
                            s5_unit(i * 3 + (2 + u), pos)
                        else:
                            s5_unit(i * 3 + 4, pos - 18)
                        slot = i * 4 + 2 * u
                        if pos in (24, 29):
                            a = (24, 29).index(pos)
                            if a == 0:
                                pe.wait_ge(aq_ready, i * 6 + 3 * u + 3)
                                pe.wait_ge(ak_ready, i * 6 + 3 * u + 3)
                            else:
                                pe.wait_ge(probT_ready, slot + 1)
                            for g in range(NG):
                                c = 2 * g + a
                                o1 = ps[:, B_SC1 + g // 2, g % 2 * TOK:(g % 2 + 1) * TOK]
                                pe.matmul(o1, aq[:, c, P:TOK], ak[:, c, :], start=True, stop=True)
                                mm = pe.matmul(ps[:, B_SC0, g * P:(g + 1) * P], aq[:, c, 0:P], ak[:, c, 0:P],
                                               start=True, stop=True)
                            mm.then_inc(scored, 1)
                        if pos == 27:
                            prob_transposes(slot)
                        if pos == 35:
                            pe.wait_ge(av_ready, i * 6 + 3 * u + 3)
                            head_out(slot, 0)
                            prob_transposes(slot + 1)
                            head_out(slot + 1, 1)

                    def prob_transposes(slot):
                        pe.wait_ge(prob_ready, slot + 1)
                        for g in range(NG):
                            bank = B_SC1 + g
                            pe.transpose(ps[:, bank, 0:P], prob[:, NG * TOK + g * P:NG * TOK + (g + 1) * P], ident[:])
                            pe.transpose(ps[:, bank, P:2 * P], prob[:, g * TOK:g * TOK + P], ident[:])
                            mm = pe.transpose(ps[:, bank, 2 * P:3 * P], prob[:, g * TOK + P:(g + 1) * TOK], ident[:])
                        mm.then_inc(probT_made, 1)

                    def head_out(slot, a):
                        pe.wait_ge(probT_ready, slot + 1)
                        pe.wait_ge(att_copied, slot + 1)
                        for g in range(NG):
                            pe.matmul(ps[:, B_PV, 0:TOK], av[:, 0, g, a * P:(a + 1) * P], probT[:, g, 0:TOK],
                                      start=g == 0, stop=False, skip_group_check=True)
                            mm = pe.matmul(ps[:, B_PV, P:TOK], av[:, 1, g, a * P:(a + 1) * P], probT[:, g, TOK:384],
                                           start=False, stop=g == 2, skip_group_check=True)
                        mm.then_inc(att_out, 1)
                    for b in range(9):
                        n = 9 * u + b
                        gemm(pe, PB.piece + n * 4, 9 * i, PB.block + n, 9 * i, 256, b >= 6, x_hi, x_lo, npieces=4,
                             narrow=True, after=lambda q, b=b: after(4 * b + q))
            barrier(pe, 3)
            pe.wait_ge(z_split_v, 1)
            with pe.Fori(0, 2) as i:
                for b in range(2):
                    gemm(pe, PC.piece + 4 * b, i, PC.block + b, i, 512, False, z_hi, z_lo, npieces=4)
            pe.wait_ge(y_split_v, 2)
            with pe.Fori(0, 2) as i:
                for u in range(2):
                    for b in range(3):
                        s, n = PD.piece + 36 * u + 12 * b, PD.block + 6 * u + 2 * b
                        gemm(pe, s, 9 * i, n, 6 * i, 512, False, x_hi, x_lo)
                        if b == 2:
                            pe.wait_ge(y_split_v, 3)
                        gemm(pe, s + 8, 9 * i, n + 1, 6 * i, 512, False, y_hi[:, b], y_lo[:, b], npieces=4)
            pe.wait_ge(mix_done, 4)
            with pe.Fori(0, 2) as i:
                for u in range(2):
                    gemm(pe, PW.piece + 8 * u, 2 * i, PW.block + u, i, 512, True, mix_hi, mix_lo)
            pe.wait_ge(xs_ready, 4)
            transposes(hs, 8)
            pe.wait_ge(xlo_ready, 16)
            with pe.Fori(0, 2) as h:
                with pe.Fori(0, 4) as i:
                    for u in range(2):
                        gemm(pe, PF.piece + 8 * u, h * 16 + i * 2, PF.block + u, h * 6 + i, 512, False, x_hi, x_lo)
                with pe.Fori(0, 2) as i:
                    pe.wait_ge(h_ready, h * 8 + 9)
                    for u in range(2):
                        gemm(pe, PF.piece + 64 + 16 * u, h * 16 + i * 4, PF.block + 8 + u, h * 6 + i, 512, True,
                             h_hi, h_lo, npieces=16)

        @block.scalar
        def _(act):
            def out_of_psum(dst, block, func=ACT.Copy, banks=2, width=512):
                act.activation(dst, ps[:, 2 * (block % 2):2 * (block % 2) + banks, 0:width], func).then_inc(
                    psum_free[block % 2], 1)

            def sums_of_squares(src, junk):
                for t in range(TT):
                    last = act.activation(junk[:, t, :], src[:, t, :], ACT.Square, accum_out=small[:, t:t + 1])
                last.then_inc(sumsq_ready, 1)

            def root(n):
                act.wait_ge(inv_ready, n)
                act.activation(small[:, 6:8], small[:, 4:6], ACT.Sqrt).then_inc(root_ready, 1)

            act.dma_start(ident[:], ident_c).then_inc(c_loaded, 16)
            act.dma_start(vrows[C_N1:C_N1 + 16, :], norm1_g.rearrange("a (k p) -> (a k) p", p=P)).then_inc(vrows_loaded, 16)
            act.dma_start(vrows[C_N2:C_N2 + 16, :], norm2_g.rearrange("a (k p) -> (a k) p", p=P)).then_inc(vrows_loaded, 16)
            act.dma_start(vrows[C_CW:C_CW + 64, :], conv_w[0].rearrange("j (k p) -> (j k) p", p=P)).then_inc(vrows_loaded, 16)
            act.dma_start(vrows[C_CB:C_CB + 16, :], conv_b.rearrange("a (k p) -> (a k) p", p=P)).then_inc(vrows_loaded, 16)
            act.dma_start(vrows[C_MH:C_MH + 8, :], mh_norm_g.rearrange("a (k p) -> (a k) p", p=P)).then_inc(vrows_loaded, 16)
            act.dma_start(vrows[C_DS:C_DS + 8, :], d_skip[0].rearrange("(k g) c -> k (g c)", k=8)).then_inc(vrows_loaded, 16)
            act.dma_start(consts[:], consts_c).then_inc(c_loaded, 16)
            act.dma_start(srows[0:32, :], lam_re[0].rearrange("(j q) s -> j (q s)", q=2)).then_inc(c_loaded, 16)
            act.dma_start(srows[32:64, :], lam_im[0].rearrange("(j q) s -> j (q s)", q=2)).then_inc(c_loaded, 16)
            act.dma_start(ldt[64:96, :], log_dt[0].rearrange("(j q) -> j q", q=2)).then_inc(c_loaded, 16)
            act.dma_start(gate_bias[0:4, :], b_igate[0].rearrange("(h a) -> h a", a=1)).then_inc(c_loaded, 16)
            act.dma_start(gate_bias[4:8, :], b_fgate[0].rearrange("(h a) -> h a", a=1)).then_inc(c_loaded, 16)
            act.dma_start(table[:], rel_bias).then_inc(c_loaded, 16)
            act.dma_start(onehot[:], onehot_c).then_inc(c_loaded, 16)
            act.dma_start(relmask[:], relmask_c).then_inc(c_loaded, 16)
            for ri, w in enumerate((b_re, b_im)):
                act.dma_start(b_raw[:, ri], w[0].rearrange("(j q) s c -> (q s) j c", q=2)).then_inc(s5_loaded, 16)
            for ri, w in enumerate((c_re, c_im)):
                act.dma_start(c_raw[:, ri], w[0].rearrange("(t g) c s -> (g c) t s", t=8)).then_inc(s5_loaded, 16)
            act.wait_ge(x_loaded, 16)
            sums_of_squares(xs, xf[:].rearrange("p (a k) t -> p a (k t)", a=TT))
            root(1)
            split_first(split_hi, act)
            for b in range(8):
                act.wait_ge(xf_ready, b + 1)
                act.activation(x_hi[:, 2 * b:2 * b + 2, :], xf[:, 2 * b:2 * b + 2, :], ACT.Copy).then_inc(xhi_ready, 1)
            for s in range(4):
                split_hi(act, s, 0)
            act.wait_ge(c_loaded, C_LOADS)
            act.wait_ge(par_v, 1)
            act.activation(s5p[:, 3, :], s5p[:, 2, :], ACT.Exp).then_inc(par_a, 1)
            act.wait_ge(par_v, 2)
            act.activation(s5p[:, 5, :], s5p[:, 4, :], ACT.Exp).then_inc(par_a, 1)
            act.wait_ge(par_v, 3)
            act.activation(s5p[:, 7, :].bitcast(F32R), s5p[:, 6, :], ACT.Copy).then_inc(par_a, 1)
            act.wait_ge(par_v, 4)
            act.activation(s5p[:, 20, :], s5p[:, 19, :], ACT.Sin, scale=math.pi)
            act.activation(s5p[:, 21, :], s5p[:, 19, :], ACT.Abs).then_inc(par_a, 1)
            act.wait_ge(par_a, 4)
            act.activation(s5p[:, 22, :], s5p[:, 21, :], ACT.Sin, bias=half_pi, scale=-math.pi)
            act.activation(s5p[:, 23, :], s5p[:, 21, :], ACT.Sin, bias=half_pi, scale=-2.0 * math.pi).then_inc(par_a, 1)
            for s in range(4, 8):
                split_hi(act, s, 0)
            block_done(act, 0, 8, 0)
            act.wait_ge(xlo_ready, 8)
            pack_u = pack[:, :, PK_U:PK_U + TOK]
            act.activation(pack_u[:, 0:4, :], ps[:, 0:2, :].rearrange("p b (c t) -> p (b c) t", t=TOK),
                           ACT.Copy).then_inc(psum_free[0], 1)
            for s in range(8, 16):
                split_hi(act, s, 0)
            block_done(act, 8, 8, 0)
            act.activation(pack_u[:, 4:8, :], ps[:, 2:4, :].rearrange("p b (c t) -> p (b c) t", t=TOK),
                           ACT.Copy).then_inc(psum_free[1], 1)
            for which in range(2):
                for b in range(4):
                    act.wait_ge(btr_ready, 4 * which + b + 1)
                    act.activation(pack[:, 2 * b:2 * b + 2, 256 * which:256 * which + 256],
                                   ps[:, SPARE + b, :].rearrange("p (t c) -> p t c", t=2), ACT.Copy).then_inc(pack_ready, 1)
            for s in range(16, 18):
                split_hi(act, s, 0)
            block_done(act, PI.piece, 2, 0)
            act.activation(gates8[:], ps[0:8, 0, 0:TOK], ACT.Identity, bias=gate_bias[:]).then_inc(psum_free[0], 1)
            act.drain()
            act.activation(gtmp[:, 0, :], gates8[:], ACT.Abs)
            act.drain()
            act.activation(gtmp[:, 1, :], gtmp[:, 0, :], ACT.Exp, scale=-1.0)
            act.drain()
            act.activation(gtmp[:, 2, :], gtmp[:, 1, :], ACT.Ln, bias=1.0).then_inc(g8_a, 2)
            act.wait_ge(g8_v, 2)
            act.activation(gr[:, 1, :], gaf[:, 1, :], ACT.Exp, scale=-1.0).then_inc(g8_a, 1)
            barrier(act, 1)

            def s5_unit(n, q):
                if q == 0:
                    act.wait_ge(unit_done, n + 1)
                    act.activation(s5s[:], pack[:, bass.ds(n, 1), :].rearrange("p a c -> p (a c)"), ACT.Copy).then_inc(
                        s5_staged, 1)
                if q in (2, 9):
                    h = (2, 9).index(q)
                    act.wait_ge(psi_ready, n * 2 + h + 1)
                    act.wait_ge(rot_done, n * 4 + 2 * h + 1)
                    ph = psi[:, 2 * h:2 * h + 2, :]
                    act.activation(s2[:], ph, ACT.Sin, scale=math.pi)
                    act.drain()
                    act.activation(ph, ph, ACT.Abs)
                    act.drain()
                    act.activation(c2[:], ph, ACT.Sin, bias=half_pi, scale=-2.0 * math.pi)
                    act.activation(ph, ph, ACT.Sin, bias=half_pi, scale=-math.pi).then_inc(sins_ready, 1)
                if q == 17:
                    act.wait_ge(gelu_in, n + 1)
                    act.activation(m2[:, 1, :], m2[:, 0, :], ACT.Sigmoid, scale=2.0 * math.sqrt(2.0 / math.pi)).then_inc(
                        gelu_sig, 1)

            with act.Fori(0, 2) as i:
                def conv_copy(b):
                    s = PA.piece + 8 * b
                    block_done(act, s, 8, 4 * i)
                    if b:
                        act.wait_ge(qk_ready, i * 2 + 1)
                    act.activation(qk_raw[:], ps[:, 2 * ((PA.block + b) % 2):2 * ((PA.block + b) % 2) + 2, :],
                                   ACT.Copy).then_inc(psum_free[(PA.block + b) % 2], 1)
                    act.drain()
                    act.sem_inc(conv_in, 1)
                for pos in range(32):
                    split_hi(act, PA.piece + pos, 4 * i)
                    s5_unit(i, pos)
                    if pos == 7:
                        conv_copy(0)
                    if pos in (10, 18):
                        b = (10, 18).index(pos)
                        act.wait_ge(conv_acc, i * 2 + b + 1)
                        act.activation(qk_raw[:], acc[:], ACT.Sigmoid).then_inc(conv_sig, 1)
                    if pos == 15:
                        conv_copy(1)
                    if pos == 12:
                        for h in range(2):
                            act.wait_ge(wexp_in, i * 2 + h + 1)
                            act.activation(wexp[:, h, 0:TOK], wexp[:, h, 0:TOK], ACT.Exp, bias=conv_s[:, 44 + h:45 + h])
                            act.activation(wexp[:, h, TOK:384], wexp[:, h, TOK:384], ACT.Exp,
                                           bias=conv_s[:, 46 + h:47 + h]).then_inc(wexp_ready, 1)
                    if pos == 23:
                        s, blk = PA.piece + 16, PA.block + 2
                        block_done(act, s, 8, 4 * i)
                        act.wait_ge(num_ready, i * 2 + 1)
                        act.activation(v_ext[:, :, :, 0:TOK],
                                       ps[:, 2 * (blk % 2):2 * (blk % 2) + 2, :].rearrange("p t (h e) -> p t h e", h=2),
                                       ACT.Copy).then_inc(psum_free[blk % 2], 1)
                        act.drain()
                        act.sem_inc(v_ready, 1)
                    if pos in (26, 30):
                        act.wait_ge(rec_ready, i * 2 + (26, 30).index(pos) + 1)
                        for t in range(TT):
                            last = act.activation(qk_raw[:, t, :], ps[:, B_H[t], 0:TOK], ACT.Square,
                                                  scale=small[:, 10 + t:11 + t], accum_out=small[:, 12 + t:13 + t])
                        last.then_inc(hss_ready, 1)
                        act.wait_ge(hinv_ready, i * 2 + (26, 30).index(pos) + 1)
                        act.activation(small[:, 18:20], small[:, 16:18], ACT.Sqrt).then_inc(hroot_ready, 1)
                s, blk = PA.piece + 24, PA.block + 3
                block_done(act, s, 8, 4 * i)
                act.activation(o_sig[:], ps[:, 2 * (blk % 2):2 * (blk % 2) + 2, :], ACT.Sigmoid).then_inc(
                    psum_free[blk % 2], 1)
                act.drain()
                act.sem_inc(o_ready, 1)
            barrier(act, 2)

            with act.Fori(0, 2) as i:
                for u in range(2):
                    for pos in range(36):
                        split_hi(act, PB.piece + 36 * u + pos, 9 * i)
                        if u == 0 or pos < 18:
                            s5_unit(i * 3 + (2 + u), pos)
                        else:
                            s5_unit(i * 3 + 4, pos - 18)
                        slot = i * 4 + 2 * u
                        if pos in (25, 30):
                            a = (25, 30).index(pos)
                            act.wait_ge(logits_ready, slot + a + 2)
                            act.activation(prob[:, 0:NG * TOK], prob[:, 0:NG * TOK], ACT.Exp, bias=small[:, 22:23],
                                           accum_out=small[:, 24:25])
                            act.activation(prob[:, NG * TOK:], prob[:, NG * TOK:], ACT.Exp, bias=small[:, 23:24],
                                           accum_out=small[:, 25:26]).then_inc(exps_ready, 1)
                        if pos == 28:
                            act.wait_ge(probT_made, slot + 2)
                            act.wait_ge(att_out, slot + 1)
                            act.activation(probT[:], ps[:, B_SC1:B_SC1 + 3, 0:384], ACT.Copy).then_inc(probT_ready, 1)
                        if pos % 4 == 3:
                            b = pos // 4
                            blk = PB.block + 9 * u + b
                            block_done(act, PB.piece + 36 * u + 4 * b, 4, 9 * i)
                            src = ps[:, blk % 2, :].rearrange("p (a t) -> p a t", a=2)
                            if b < 6:
                                dst = (aq if b < 3 else ak)[:, 2 * (b % 3):2 * (b % 3) + 2, :]
                                act.wait_ge(scored, slot + 1)
                            else:
                                dst = av[:, :, b - 6, :]
                                act.wait_ge(att_out, slot + 1)
                            act.activation(dst, src, ACT.Copy).then_inc(psum_free[blk % 2], 1)
                            act.drain()
                            act.sem_inc((aq_ready, ak_ready, av_ready)[b // 3], 1)
                    act.wait_ge(probT_made, slot + 3)
                    act.wait_ge(att_out, slot + 2)
                    act.activation(probT[:], ps[:, B_SC1:B_SC1 + 3, 0:384], ACT.Copy).then_inc(probT_ready, 1)
            barrier(act, 3)

            act.wait_ge(unit_done, 9)
            act.activation(z_hi[:], y_s[:], ACT.Copy).then_inc(z_split_a, 1)
            for b, y in enumerate((y_a, y_b)):
                act.activation(y_hi[:, b], y[:], ACT.Copy).then_inc(y_split_a, 1)
            with act.Fori(0, 2) as i:
                for b in range(2):
                    s, blk = PC.piece + 4 * b, PC.block + b
                    for q in range(4):
                        split_hi(act, s + q, i)
                    block_done(act, s, 4, i)
                    act.wait_ge(glu_out, i + 1)
                    act.activation((z_lin, z_sig)[b][:], ps[:, 2 * (blk % 2):2 * (blk % 2) + 2, :],
                                   (ACT.Copy, ACT.Sigmoid)[b]).then_inc(psum_free[blk % 2], 1)
                    act.drain()
                    act.sem_inc(glu_in, 1)
            act.wait_ge(glu_out, 3)
            act.activation(y_hi[:, 2], y_s[:], ACT.Copy).then_inc(y_split_a, 1)

            with act.Fori(0, 2) as i:
                for u in range(2):
                    for b in range(3):
                        s, blk = PD.piece + 36 * u + 12 * b, PD.block + 6 * u + 2 * b
                        for q in range(8):
                            split_hi(act, s + q, 9 * i)
                        block_done(act, s, 8, 9 * i)
                        act.wait_ge(mix_ready, i * 2 + u + 1)
                        act.activation(gate_sig[:, b], ps[:, 2 * (blk % 2):2 * (blk % 2) + 2, :],
                                       ACT.Sigmoid).then_inc(psum_free[blk % 2], 1)
                        act.drain()
                        act.sem_inc(gsig_ready, 1)
                        for q in range(4):
                            split_hi(act, s + 8 + q, 9 * i)
                    act.wait_ge(mix_ready, i * 2 + u + 2)
                    act.activation(mix_hi[:, bass.ds(i * 8 + 4 * u, 4), :], mix[:], ACT.Copy).then_inc(mixhi_ready, 1)

            with act.Fori(0, 2) as i:
                for s in range(16):
                    split_hi(act, PW.piece + s, 2 * i)
            act.wait_ge(x1_done, 4)
            sums_of_squares(x1, hs)
            root(2)
            for b in range(8):
                act.wait_ge(xf_ready, 8 + b + 1)
                act.activation(x_hi[:, 2 * b:2 * b + 2, :], xf2[:, 2 * b:2 * b + 2, :], ACT.Copy).then_inc(xhi_ready, 1)

            def ff1(h, i):
                for u in range(2):
                    s, blk = PF.piece + 8 * u, PF.block + u
                    for q in range(8):
                        split_hi(act, s + q, 16 * h + 2 * i)
                    block_done(act, s, 8, 16 * h + 2 * i)
                    act.wait_ge(h_ready, h * 8 + i * 2 + u + 1)
                    act.activation(relu[:].rearrange("p (b n) -> p b n", b=2),
                                   ps[:, 2 * (blk % 2):2 * (blk % 2) + 2, :], ACT.Relu).then_inc(psum_free[blk % 2], 1)
                    act.drain()
                    act.sem_inc(relu_ready, 1)
                    act.activation(h_hi[:, bass.ds(i * 8 + 4 * u, 4), :], relu[:], ACT.Square).then_inc(hhi_ready, 1)
            with act.Fori(0, 2) as h:
                with act.Fori(0, 4) as i:
                    ff1(h, i)
                with act.Fori(0, 2) as i:
                    for s in range(28):
                        split_hi(act, PF.piece + 64 + s, 16 * h + 4 * i)
                    split_unless_last(split_hi, act, h, i)
            act.wait_ge(x1_done, 12)
            sums_of_squares(x1, sq_junk)
            root(3)

        @block.vector
        def _(dve):
            def chain(*ops):
                for op in ops:
                    op()
                    dve.drain()

            def inverse_rms(n, width):
                dve.wait_ge(sumsq_ready, n)
                dve.tensor_scalar(small[:, 2:4], small[:, 0:2], 1.0 / width, EPS, ALU.mult, ALU.add)
                dve.drain()
                dve.reciprocal(small[:, 4:6], small[:, 2:4]).then_inc(inv_ready, 1)
                dve.wait_ge(root_ready, n)
                newton(small[:, 2:4], small[:, 6:8], small[:, 8:10], small[:, 20:22])

            def newton(v, r, dst, tmp):
                dve.tensor_tensor(tmp, r, r, ALU.mult)
                dve.drain()
                dve.tensor_tensor(tmp, tmp, v, ALU.mult)
                dve.drain()
                dve.tensor_scalar(tmp, tmp, -0.5, 1.5, ALU.mult, ALU.add)
                dve.drain()
                dve.tensor_tensor(dst, r, tmp, ALU.mult)
                dve.drain()

            def features(n0, xft, gcol):
                def lo(b):
                    dve.wait_ge(xhi_ready, n0 + b + 1)
                    dve.tensor_tensor(x_lo[:, 2 * b:2 * b + 2, :], xft[:, 2 * b:2 * b + 2, :],
                                      f(x_hi[:, 2 * b:2 * b + 2, :]), ALU.subtract).then_inc(xlo_ready, 1)
                for b in range(8):
                    dve.wait_ge(trans_ready, n0 + b + 1)
                    for k in range(2):
                        kk = 2 * b + k
                        last = dve.tensor_scalar(xft[:, kk, :], ps[:, SPARE + b % 4, k * TOK:(k + 1) * TOK],
                                                 vec[:, gcol + kk:gcol + kk + 1], None, ALU.mult)
                    last.then_inc(xf_ready, 1)
                    if b:
                        lo(b - 1)
                lo(7)

            for s in (bu_free, ys_ready, unit_done, att_copied, glu_out, mix_ready, h_ready, rot_done, att_out,
                      scored, num_ready, s2_ready, y_done, logits_ready, probT_made):
                dve.sem_inc(s, 1)
            dve.wait_ge(c_loaded, C_LOADS)
            dve.tensor_copy(srows[64:96, :].rearrange("p (q s) -> p q s", q=2), bcast(ldt[64:96, :], 2, ST)).then_inc(
                srows_ready, 1)
            inverse_rms(1, D)
            split_first(split_lo, dve)
            for t in range(TT):
                dve.tensor_scalar(xs[:, t, :], xs[:, t, :], small[:, 8 + t:9 + t], None, ALU.mult).then_inc(xs_ready, 1)
            dve.wait_ge(cols_ready, 1)
            dve.tensor_copy(vec[:], ps[:, 0, 0:P])
            dve.tensor_copy(s5p[:, 0:3, :], ps[:, 0, P:P + 96].rearrange("p (a b) -> p a b", a=3)).then_inc(par_v, 1)
            dve.tensor_tensor(relval[:], ps[0:24, 1, 0:384], relmask[:], ALU.add).then_inc(cols_copied, 2)
            dve.drain()
            features(0, xf, C_N1)

            def split_range(a, b):
                for s in range(a, b):
                    split_lo(dve, s, 0)
            split_range(0, 4)

            def pp(n):
                return s5p[:, n, :]

            def mul(o, a, b):
                dve.tensor_tensor(pp(o), pp(a), pp(b), ALU.mult)
                dve.drain()

            def add(o, a, b, op=ALU.add):
                dve.tensor_tensor(pp(o), pp(a), pp(b), op)
                dve.drain()

            def scaled(o, a, c):
                dve.tensor_scalar(pp(o), pp(a), c, None, ALU.mult)
                dve.drain()

            def whole(o, a, big=ROUND):
                dve.tensor_scalar(pp(o), pp(a), big, big, ALU.add, ALU.subtract)
                dve.drain()
            inv1, inv2, inv3 = inv_two_pi()
            dve.wait_ge(par_a, 1)
            mul(4, 0, 3)
            dve.sem_inc(par_v, 1)
            mul(6, 1, 3)
            dve.sem_inc(par_v, 1)
            dve.wait_ge(par_a, 3)
            add(8, 6, 7, ALU.subtract)
            scaled(9, 7, inv1)
            whole(10, 9)
            add(9, 9, 10, ALU.subtract)
            scaled(11, 7, inv2)
            whole(10, 11)
            add(11, 11, 10, ALU.subtract)
            scaled(12, 8, inv1)
            whole(10, 12)
            add(12, 12, 10, ALU.subtract)
            scaled(13, 8, inv2)
            scaled(14, 7, inv3)
            add(13, 13, 14)
            add(14, 9, 11)
            add(14, 14, 12)
            add(14, 14, 13)
            whole(10, 14)
            add(9, 9, 10, ALU.subtract)
            add(14, 14, 10, ALU.subtract)
            whole(17, 14, GRID16)
            add(15, 9, 17, ALU.subtract)
            add(15, 15, 11)
            add(15, 15, 12)
            add(15, 15, 13)
            scaled(18, 15, -1.0)
            add(19, 17, 15)
            dve.sem_inc(par_v, 1)
            dve.wait_ge(par_a, 5)
            mul(24, 20, 22)
            scaled(24, 24, 2.0)
            mul(25, 5, 23)
            dve.tensor_scalar(pp(25), pp(25), -1.0, None, ALU.add)
            dve.drain()
            mul(26, 5, 24)
            mul(20, 0, 0)
            mul(21, 1, 1)
            add(20, 20, 21)
            dve.reciprocal(pp(20), pp(20))
            dve.drain()
            mul(21, 25, 0)
            mul(22, 26, 1)
            add(21, 21, 22)
            mul(27, 21, 20)
            mul(21, 26, 0)
            mul(22, 25, 1)
            add(21, 21, 22, ALU.subtract)
            mul(28, 21, 20)
            split_range(4, 8)
            dve.wait_ge(s5_loaded, 64)
            bt = [bb_t[:, n] for n in range(2)]
            fre, fim = bcast(pp(27), 2, 16), bcast(pp(28), 2, 16)
            for ri in range(2):
                dve.tensor_tensor(bt[0], b_raw[:, ri], fre, ALU.mult)
                dve.tensor_tensor(bt[1], b_raw[:, 1 - ri], fim, ALU.mult)
                dve.drain()
                dve.tensor_tensor(bt[0], bt[0], bt[1], ALU.add if ri else ALU.subtract)
                dve.drain()
                for half in range(2):
                    dve.tensor_scalar(b_pad[:, ri, :, 16 * half:16 * half + 16], bt[0], par[:, half:half + 1], None, ALU.mult)
                dve.drain()
            dve.sem_inc(bpad_ready, 1)
            for ri in range(2):
                for half in range(2):
                    dve.tensor_scalar(c_pad[:, ri, :, ST * half:ST * half + ST], c_raw[:, ri], par[:, 2 + half:3 + half],
                                      (1.0, -1.0)[ri], ALU.mult, ALU.mult)
            dve.drain()
            dve.sem_inc(bpad_ready, 1)
            split_range(8, 16)
            for dst, n in ((PK_FH, 17), (PK_FL, 18), (PK_MAG, 5)):
                dve.tensor_copy(pack[:, :, dst:dst + 4], pp(n).rearrange("p (t j) -> p t j", j=4))
            dve.tensor_copy(pack[:, :, PK_D:PK_D + 1], vec[:, C_DS:C_DS + 8].rearrange("p (t a) -> p t a", a=1))
            dve.memset(pack[:, :, PK_D + 1:PKW], 0.0)
            dve.drain()
            dve.sem_inc(par_v, 1)
            split_range(16, 18)
            dve.tensor_scalar(neg_sel[:], ident[0:8, MH:2 * MH], -1.0, None, ALU.mult)
            dve.tensor_scalar(neg_bc[:], bcast(ident[0:MH, 0:MH], 2, P), -1.0, None, ALU.mult)
            dve.wait_ge(g8_a, 2)
            dve.tensor_scalar(gtmp[:, 0, :], gates8[:], 0.0, None, ALU.min)
            dve.drain()
            dve.tensor_tensor(gtmp[:, 0, :], gtmp[:, 0, :], gtmp[:, 2, :], ALU.subtract)
            dve.memset(gtmp[:, 1, :], 1.0)
            dve.drain()
            dve.tensor_tensor_scan(fcum[:], gtmp[:, 1, :], gtmp[:, 0, :], 0.0, ALU.mult, ALU.add).then_inc(g8_v, 1)
            dve.wait_ge(g8_p, 1)
            dve.tensor_copy(gaf[:], ps[0:MH, SPARE, :].rearrange("p (a t) -> p a t", a=2))
            dve.drain()
            dve.tensor_tensor_scan(gr[:, 0, :], gaf[:, 0, :], gaf[:, 0, :], 0.0, ALU.max, ALU.max)
            dve.drain()
            dve.tensor_tensor(gaf[:, 1, :], gaf[:, 1, :], gr[:, 0, :], ALU.add).then_inc(g8_v, 1)
            dve.wait_ge(g8_p, 2)
            for b in range(2):
                dve.tensor_copy(runmax_bc[:, 2 * b:2 * b + 2, :], ps[:, SPARE + b, :].rearrange("p (a t) -> p a t", a=2))
            dve.tensor_copy(acols[:], ps[:, SPARE + 2, 0:4 * MH].rearrange("p (a h) -> p a h", a=4))
            barrier(dve, 1)
            dve.memset(v_ext[:, :, :, 256:257], 1.0)

            def pair_in(n, j):
                dve.wait_ge(bu_ready, n * 4 + j + 1)
                dve.tensor_tensor(m1[:], ps[:, B_BU, :].rearrange("p (r t) -> p r t", r=2), bcast(c2[:, j % 2, :], 1, 2), ALU.mult)
                dve.tensor_tensor(m2[:], ps[:, B_BU, :].rearrange("p (r t) -> p r t", r=2), bcast(s2[:, j % 2, :], 1, 2),
                                  ALU.mult).then_inc(bu_free, 1)
                dve.drain()
                dve.tensor_tensor(zin[:, 0, :], m1[:, 0, :], m2[:, 1, :], ALU.add)
                dve.tensor_tensor(zin[:, 1, :], m1[:, 1, :], m2[:, 0, :], ALU.subtract)
                dve.drain()
                for ri in range(2):
                    last = dve.tensor_tensor_scan(m1[:, ri, :], bcast(s5s[:, PK_MAG + j:PK_MAG + j + 1], 1, TOK)[:, :, 0],
                                                  zin[:, ri, :], 0.0, ALU.mult, ALU.add)
                last.then_inc(z_ready, 1)

            def s5_unit(n, q):
                if q in (3, 10):
                    h = (3, 10).index(q)
                    dve.wait_ge(sins_ready, n * 2 + h + 1)
                    dve.scalar_tensor_tensor(s2[:], s2[:], -2.0, psi[:, 2 * h:2 * h + 2, :], ALU.mult, ALU.mult).then_inc(
                        s2_ready, 1)
                    dve.drain()
                if q in (4, 7, 11, 14):
                    j = (4, 7, 11, 14).index(q)
                    dve.wait_ge(rot_done, n * 4 + j + 1)
                    pair_in(n, j)
                if q == 17:
                    dve.wait_ge(y_done, n * 4 + 5)
                    y0, t0, t1 = zin[:, 0, :], zin[:, 1, :], m2[:, 0, :]
                    dve.scalar_tensor_tensor(y0, s5s[:, PK_U:PK_U + TOK], s5s[:, PK_D:PK_D + 1], ps[:, B_Y, 0:TOK],
                                             ALU.mult, ALU.add).then_inc(ys_ready, 1)
                    dve.drain()
                    chain(lambda: dve.tensor_tensor(t0, y0, y0, ALU.mult),
                          lambda: dve.tensor_scalar(t0, t0, 0.044715, 1.0, ALU.mult, ALU.add))
                    dve.tensor_tensor(t1, t0, y0, ALU.mult).then_inc(gelu_in, 1)
                    dve.wait_ge(gelu_sig, n + 1)
                    dve.tensor_tensor(y_s[:, bass.ds(n, 1), :].rearrange("p a t -> p (a t)"), y0, m2[:, 1, :],
                                      ALU.mult).then_inc(unit_done, 1)

            with dve.Fori(0, 2) as i:
                dve.tensor_copy(conv_s[:, 0:32].rearrange("p (j b c) -> p (j b) c", j=4, b=2),
                                vec[:, C_CW:C_CW + 64].rearrange("p (b c) -> p b c", c=8)[:, :, bass.ds(i * 4, 4)])
                dve.tensor_copy(conv_s[:, 32:40].rearrange("p (b c) -> p b c", b=2),
                                vec[:, C_CB:C_CB + 16].rearrange("p (b c) -> p b c", c=8)[:, :, bass.ds(i * 4, 4)])
                dve.tensor_copy(conv_s[:, 40:44], vec[:, bass.ds(i * 4 + C_MH, 4)])
                dve.tensor_copy(conv_s[:, 44:48].rearrange("p (t h) -> p t h", t=2), acols[:, 0:2, bass.ds(i * 2, 2)])
                dve.tensor_copy(small[:, 28:32].rearrange("p (t h) -> p t h", t=2), acols[:, 2:4, bass.ds(i * 2, 2)])
                dve.drain()

                def conv(b):
                    dve.wait_ge(conv_in, i * 2 + b + 1)

                    def tap(j, c):
                        return conv_s[:, j * 8 + b * 4 + c:j * 8 + b * 4 + c + 1]
                    for c in range(4):
                        dve.tensor_scalar(acc[:, c, :], qk_raw[:, c, :], tap(3, c), conv_s[:, 32 + b * 4 + c:33 + b * 4 + c],
                                          ALU.mult, ALU.add)
                    for j in (2, 1, 0):
                        dve.drain()
                        d = 3 - j
                        for c in range(4):
                            last = dve.scalar_tensor_tensor(acc[:, c, d:TOK], qk_raw[:, c, 0:TOK - d], tap(j, c),
                                                            acc[:, c, d:TOK], ALU.mult, ALU.add)
                    last.then_inc(conv_acc, 1)

                def silu(b):
                    dve.wait_ge(conv_sig, i * 2 + b + 1)
                    dve.scalar_tensor_tensor((qT, kT)[b][:], acc[:], (1.0, 1.0 / 16.0)[b], qk_raw[:], ALU.mult,
                                             ALU.mult).then_inc(qk_ready, 1)

                def head(h):
                    dve.wait_ge(num_ready, i * 2 + h + 2)
                    for t in range(TT):
                        dve.scalar_tensor_tensor(small[:, 14 + t:15 + t], ps[:, B_H[t], 256:257], -1.0,
                                                 small[:, 28 + 2 * t + h:29 + 2 * t + h], ALU.mult, ALU.max)
                    dve.drain()
                    for t in range(TT):
                        dve.tensor_tensor(small[:, 14 + t:15 + t], small[:, 14 + t:15 + t], ps[:, B_H[t], 256:257], ALU.max)
                    dve.drain()
                    dve.reciprocal(small[:, 10:12], small[:, 14:16]).then_inc(rec_ready, 1)
                    dve.wait_ge(hss_ready, i * 2 + h + 1)
                    dve.tensor_scalar(small[:, 14:16], small[:, 12:14], 1.0 / 256.0, EPS, ALU.mult, ALU.add)
                    dve.drain()
                    dve.reciprocal(small[:, 16:18], small[:, 14:16]).then_inc(hinv_ready, 1)
                    dve.wait_ge(hroot_ready, i * 2 + h + 1)
                    newton(small[:, 14:16], small[:, 18:20], small[:, 32:34], small[:, 20:22])
                    dve.tensor_tensor(small[:, 32:34], small[:, 32:34], small[:, 10:12], ALU.mult)
                    dve.drain()
                    for t in range(TT):
                        last = dve.tensor_scalar(hn[:, t, :], ps[:, B_H[t], 0:TOK], small[:, 32 + t:33 + t], None, ALU.mult)
                    last.then_inc(hn_ready, 1)

                def head_features(h):
                    dve.wait_ge(hT_ready, i * 2 + h + 1)
                    for e in range(2):
                        last = dve.tensor_scalar(y_a[:, bass.ds(i * 4 + (2 * h + e), 1), :].rearrange("p a t -> p (a t)"),
                                                 ps[:, B_H[0], e * TOK:(e + 1) * TOK],
                                                 conv_s[:, 40 + 2 * h + e:41 + 2 * h + e], None, ALU.mult)
                    last.then_inc(hT_copied, 1)

                for pos in range(32):
                    split_lo(dve, PA.piece + pos, 4 * i)
                    s5_unit(i, pos)
                    if pos == 5:
                        for h in range(2):
                            rm = runmax_bc[:, bass.ds(i * 2 + h, 1), :].rearrange("p a t -> p (a t)")
                            rm1 = runmax_bc[:, bass.ds(i * 2 + h, 1), P:TOK].rearrange("p a t -> p (a t)")
                            dve.tensor_tensor(wexp[:, h, 0:TOK], masks[:, 0:TOK], rm, ALU.add)
                            dve.tensor_tensor(wexp[:, h, TOK:384], masks[:, TOK:384], rm1, ALU.add).then_inc(wexp_in, 1)
                    if pos == 8:
                        conv(0)
                    if pos == 12:
                        silu(0)
                    if pos == 16:
                        conv(1)
                    if pos == 18:
                        silu(1)
                    if pos in (20, 21):
                        h = pos - 20
                        dve.wait_ge(sT_ready, i * 2 + h + 1)
                        if h == 0:
                            dve.wait_ge(wexp_ready, i * 2 + 2)
                        dve.tensor_tensor(pT[:, h, :], ps[:, B_H[h], 0:384], wexp[:, h, :], ALU.mult).then_inc(pT_ready, 1)
                    if pos in (26, 30):
                        head((26, 30).index(pos))
                    if pos == 28:
                        head_features(0)
                head_features(1)
                dve.drain()
                dve.wait_ge(o_ready, i + 1)
                ya = y_a[:, bass.ds(i * 4, 4), :]
                dve.tensor_tensor(ya, ya, o_sig[:], ALU.mult)
                dve.drain()
            barrier(dve, 2)

            with dve.Fori(0, 2) as i:
                for u in range(2):
                    slot = i * 4 + 2 * u

                    def logits(a):
                        dve.wait_ge(scored, slot + a + 2)
                        dve.wait_ge(rel_loaded, i * 64 + (2 * u + a + 1) * 16)
                        dve.wait_ge(probT_made, slot + a + 1)
                        sc = ps[:, B_SC1:B_SC1 + 2, :].rearrange("p b n -> p (b n)")
                        dve.scalar_tensor_tensor(prob[:, 0:NG * TOK], sc[:, 0:NG * TOK], P ** -0.5,
                                                 rel[:].rearrange("p g t -> p (g t)"), ALU.mult, ALU.add)
                        dve.scalar_tensor_tensor(prob[:, NG * TOK:].rearrange("p (g t) -> p g t", g=NG),
                                                 ps[:, B_SC0, 0:384].rearrange("p (g t) -> p g t", g=NG), P ** -0.5,
                                                 rel[:, :, P:TOK], ALU.mult, ALU.add)
                        dve.drain()
                        dve.tensor_reduce(small[:, 22:23], prob[:, 0:NG * TOK], AX_X, ALU.max, negate=True)
                        dve.tensor_reduce(small[:, 23:24], prob[:, NG * TOK:], AX_X, ALU.max, negate=True).then_inc(
                            logits_ready, 1)

                    def weights(a):
                        dve.wait_ge(exps_ready, slot + a + 1)
                        dve.reciprocal(small[:, 26:28], small[:, 24:26])
                        dve.drain()
                        dve.tensor_scalar(prob[:, 0:NG * TOK], prob[:, 0:NG * TOK], small[:, 26:27], None, ALU.mult)
                        dve.tensor_scalar(prob[:, NG * TOK:], prob[:, NG * TOK:], small[:, 27:28], None, ALU.mult).then_inc(
                            prob_ready, 1)

                    def head_copy(a):
                        dve.wait_ge(att_out, slot + a + 2)
                        dve.tensor_copy(y_b[:, bass.ds(i * 4 + (2 * u + a), 1), :].rearrange("p a t -> p (a t)"),
                                        ps[:, B_PV, 0:TOK]).then_inc(att_copied, 1)
                    for pos in range(36):
                        split_lo(dve, PB.piece + 36 * u + pos, 9 * i)
                        if u == 0 or pos < 18:
                            s5_unit(i * 3 + (2 + u), pos)
                        else:
                            s5_unit(i * 3 + 4, pos - 18)
                        if pos in (25, 30):
                            logits((25, 30).index(pos))
                        if pos in (26, 31):
                            weights((26, 31).index(pos))
                    head_copy(0)
                    head_copy(1)
            barrier(dve, 3)

            dve.wait_ge(z_split_a, 1)
            dve.tensor_tensor(z_lo[:], y_s[:], f(z_hi[:]), ALU.subtract).then_inc(z_split_v, 1)
            for b, y in enumerate((y_a, y_b)):
                dve.wait_ge(y_split_a, b + 1)
                dve.tensor_tensor(y_lo[:, b], y[:], f(y_hi[:, b]), ALU.subtract).then_inc(y_split_v, 1)
            with dve.Fori(0, 2) as i:
                for s in range(8):
                    split_lo(dve, PC.piece + s, i)
                dve.wait_ge(glu_in, i * 2 + 2)
                dve.tensor_tensor(y_s[:, bass.ds(i * 4, 4), :], z_lin[:], z_sig[:], ALU.mult).then_inc(glu_out, 1)
            dve.wait_ge(y_split_a, 3)
            dve.tensor_tensor(y_lo[:, 2], y_s[:], f(y_hi[:, 2]), ALU.subtract).then_inc(y_split_v, 1)

            with dve.Fori(0, 2) as i:
                for u in range(2):
                    for b in range(3):
                        s, blk = PD.piece + 36 * u + 12 * b, PD.block + 6 * u + 2 * b
                        for q in range(12):
                            split_lo(dve, s + q, 9 * i)
                        block_done(dve, s + 8, 4, 9 * i)
                        dve.wait_ge(gsig_ready, i * 6 + 3 * u + b + 1)
                        src = ps[:, 2 * ((blk + 1) % 2):2 * ((blk + 1) % 2) + 2, :].rearrange("p b (c t) -> p (b c) t", t=TOK)
                        dve.tensor_tensor((mix_t if b else mix)[:], src, gate_sig[:, b], ALU.mult).then_inc(
                            psum_free[(blk + 1) % 2], 1)
                        dve.drain()
                        if b:
                            add_op = dve.tensor_tensor(mix[:], mix[:], mix_t[:], ALU.add)
                            if b == 2:
                                add_op.then_inc(mix_ready, 1)
                            dve.drain()
                    dve.wait_ge(mixhi_ready, i * 2 + u + 1)
                    dst = bass.ds(i * 8 + 4 * u, 4)
                    dve.tensor_tensor(mix_lo[:, dst, :], mix[:], f(mix_hi[:, dst, :]), ALU.subtract).then_inc(mix_done, 1)
                    dve.drain()

            def add_to_x1(s, n, o8, blk, c0):
                block_done(dve, s, n, o8)
                dst = x1[:, :, bass.ds(c0, 512)]
                dve.tensor_tensor(dst, ps[:, 2 * (blk % 2):2 * (blk % 2) + 2, :], dst, ALU.add).then_inc(
                    psum_free[blk % 2], 1)
                dve.drain()
                dve.sem_inc(x1_done, 1)

            dve.wait_ge(x1_loaded, 16)
            with dve.Fori(0, 2) as i:
                for u in range(2):
                    for s in range(8):
                        split_lo(dve, PW.piece + 8 * u + s, 2 * i)
                    add_to_x1(PW.piece + 8 * u, 8, 2 * i, PW.block + u, i * 1024 + u * 512)
            inverse_rms(2, D)
            for t in range(TT):
                dve.tensor_scalar(hs[:, t, :], x1[:, t, :], small[:, 8 + t:9 + t], None, ALU.mult).then_inc(xs_ready, 1)
            features(8, xf2, C_N2)
            with dve.Fori(0, 2) as h:
                with dve.Fori(0, 4) as i:
                    for u in range(2):
                        for s in range(8):
                            split_lo(dve, PF.piece + 8 * u + s, h * 16 + i * 2)
                        dve.wait_ge(relu_ready, h * 8 + i * 2 + u + 1)
                        dve.tensor_tensor(relu2[:], relu[:], relu[:], ALU.mult)
                        dve.drain()
                        dve.wait_ge(hhi_ready, h * 8 + i * 2 + u + 1)
                        dst = bass.ds(i * 8 + 4 * u, 4)
                        dve.tensor_tensor(h_lo[:, dst, :], relu2[:].rearrange("p (c t) -> p c t", t=TOK),
                                          f(h_hi[:, dst, :]), ALU.subtract).then_inc(h_ready, 1)
                with dve.Fori(0, 2) as i:
                    for u in range(2):
                        for s in range(12 if u else 16):
                            split_lo(dve, PF.piece + 64 + 16 * u + s, h * 16 + i * 4)
                        if u:
                            split_unless_last(split_lo, dve, h, i)
                        add_to_x1(PF.piece + 64 + 16 * u, 16, h * 16 + i * 4, PF.block + 8 + u, i * 1024 + u * 512)
            inverse_rms(3, D)
            dve.wait_ge(fg_loaded, 16)
            for t in range(TT):
                last = dve.scalar_tensor_tensor(x1[:, t, :], x1[:, t, :], small[:, 8 + t:9 + t], fg_bc[:], ALU.mult, ALU.mult)
            last.then_inc(out_ready, 1)

        @block.gpsimd
        def _(gp):
            split_first(split_lo, gp)
            gp.wait_ge(cols_copied, 2)
            gp.dma_start(rel_rows, relval[:]).then_inc(rel_stored, 16)
            gp.wait_ge(rel_stored, 16)
            for g in range(NG):
                gp.dma_start(rel_tiles[:, :, g, :],
                             bass.AP(rel_rows.tensor, g * AH * 384 + P - 1, [[384, AH], [-1, P], [1, TOK]])).then_inc(
                    rel_spread, 16)
            for s in range(18):
                split_lo(gp, s, 0)
            barrier(gp, 1)

            def angles(n):
                gp.wait_ge(s5_staged, n + 1)
                gp.wait_ge(s2_ready, n * 2 + 1)
                gp.tensor_tensor(psi[:], bcast(iota_t, 1, 4), bcast(s5s[:, PK_FH:PK_FH + 4], 2, TOK), ALU.mult)
                gp.drain()
                for h in range(2):
                    ph = psi[:, 2 * h:2 * h + 2, :]
                    gp.tensor_scalar(kk2[:], ph, ROUND, ROUND, ALU.add, ALU.subtract)
                    gp.drain()
                    gp.tensor_tensor(ph, kk2[:], ph, ALU.subtract)
                    gp.drain()
                    gp.tensor_tensor(kk2[:], bcast(iota_t, 1, 2), bcast(s5s[:, PK_FL + 2 * h:PK_FL + 2 * h + 2], 2, TOK),
                                     ALU.mult)
                    gp.drain()
                    gp.tensor_tensor(ph, ph, kk2[:], ALU.add).then_inc(psi_ready, 1)
                    gp.drain()

            def s5_unit(n, q):
                if q == 0:
                    angles(n)
                if q in (5, 8, 12, 15):
                    j = (5, 8, 12, 15).index(q)
                    gp.wait_ge(z_ready, n * 4 + j + 1)
                    gp.wait_ge(y_done, n * 4 + j + 1)
                    gp.tensor_tensor(n1[:], m1[:], bcast(c2[:, j % 2, :], 1, 2), ALU.mult)
                    gp.tensor_tensor(n2[:], m1[:], bcast(s2[:, j % 2, :], 1, 2), ALU.mult)
                    gp.drain()
                    gp.sem_inc(rot_done, 1)
                    gp.tensor_tensor(n1[:, 0, :], n1[:, 0, :], n2[:, 1, :], ALU.subtract)
                    gp.tensor_tensor(n1[:, 1, :], n1[:, 1, :], n2[:, 0, :], ALU.add)
                    gp.drain()
                    gp.sem_inc(xr_ready, 1)

            with gp.Fori(0, 2) as i:
                for pos in range(32):
                    split_lo(gp, PA.piece + pos, 4 * i)
                    s5_unit(i, pos)
            gp.wait_ge(rel_spread, 16 * NG)
            barrier(gp, 2)
            with gp.Fori(0, 2) as i:
                for u in range(2):
                    slot = i * 4 + 2 * u
                    for pos in range(36):
                        split_lo(gp, PB.piece + 36 * u + pos, 9 * i)
                        if u == 0 or pos < 18:
                            s5_unit(i * 3 + (2 + u), pos)
                        else:
                            s5_unit(i * 3 + 4, pos - 18)
                        if pos in (1, 26):
                            a = (1, 26).index(pos)
                            gp.wait_ge(logits_ready, slot + a + 1)
                            gp.dma_start(rel[:], rel_tiles[bass.ds(i * 4 + (2 * u + a), 1)].rearrange(
                                "a p g t -> (a p) g t")).then_inc(rel_loaded, 16)
            barrier(gp, 3)
            with gp.Fori(0, 2) as i:
                for s in range(8):
                    split_lo(gp, PC.piece + s, i)
            with gp.Fori(0, 2) as i:
                for s in range(72):
                    split_lo(gp, PD.piece + s, 9 * i)
            gp.wait_ge(mix_done, 4)
            gp.dma_start(x1[:], x[0].rearrange("(t p) n -> p t n", p=P)).then_inc(x1_loaded, 16)
            with gp.Fori(0, 2) as i:
                for s in range(16):
                    split_lo(gp, PW.piece + s, i * 2)
            gp.wait_ge(xf_ready, 16)
            gp.dma_start(fg_bc[:], bass.AP(final_g.tensor, 0, [[0, P], [1, D]])).then_inc(fg_loaded, 16)
            with gp.Fori(0, 2) as h:
                with gp.Fori(0, 4) as i:
                    for s in range(16):
                        split_lo(gp, PF.piece + s, h * 16 + i * 2)
                with gp.Fori(0, 2) as i:
                    for s in range(28):
                        split_lo(gp, PF.piece + 64 + s, h * 16 + i * 4)
                    split_unless_last(split_lo, gp, h, i)


def t5_bucket(n):
    import numpy as np
    half = 16
    nf = np.maximum(n, half).astype(np.float32)
    large = half + (np.log(nf / np.float32(half)) / np.float32(math.log(2048 / half)) * np.float32(half)).astype(np.int32)
    return np.where(n < half, n, np.minimum(large, 31))


def shape_constants():
    import numpy as np
    p = np.arange(P)
    consts = np.zeros((P, 648), np.float32)
    causal = np.where(p[:, None] <= p[None, :], 0.0, NEG)
    consts[:, 0:P] = causal
    consts[:, 2 * P:3 * P] = causal
    consts[:, 384:640] = np.arange(TOK)
    consts[:, 640] = p < ST
    consts[:, 641] = p >= ST
    consts[:, 642] = p // 16 % 2 == 0
    consts[:, 643] = p // 16 % 2 == 1
    consts[:, 645] = math.pi / 2
    dist = 255 - np.arange(384)
    onehot = (t5_bucket(np.maximum(dist, 0))[None, :] == np.arange(32)[:, None]).astype(np.float32)
    seen = np.stack([(dist >= 0) & (dist <= 128), (dist >= 0) & (dist % 4 == 0), (dist >= 0) & (dist % 16 == 0)])
    relmask = np.repeat(np.where(seen, 0.0, NEG).astype(np.float32), AH, axis=0)
    return {"ident_c": np.eye(P, dtype=np.float32), "consts_c": consts, "onehot_c": onehot, "relmask_c": relmask}


_INS = ['x', 'norm1_g', 'w_in', 'conv_w', 'conv_b', 'b_igate', 'b_fgate', 'mh_norm_g', 'rel_bias', 'lam_re', 'lam_im',
        'log_dt', 'b_re', 'b_im', 'c_re', 'c_im', 'd_skip', 'w_glu', 'w_br_a', 'w_br_b', 'w_br_c', 'w_out', 'norm2_g',
        'w_ff1', 'w_ff2', 'final_g']


def kernel(**inputs):
    import numpy as _np
    import concourse.bacc as _bacc
    from concourse import mybir as _mybir
    from concourse.bass_utils import run_bass_kernel_spmd as _run

    nc = _bacc.Bacc("TRN2", target_bir_lowering=False, num_devices=1)
    arrays, args = {}, []
    values = {name: _np.ascontiguousarray(inputs[name]) for name in _INS}
    values.update(shape_constants())
    for name, a in values.items():
        arrays[f"in_{name}_dram"] = a
        args.append(nc.dram_tensor(f"in_{name}_dram", a.shape, _mybir.dt.from_np(a.dtype), kind="ExternalInput").ap())
    args.append(nc.dram_tensor("out_0_dram", (1, TOK, D), _mybir.dt.float32, kind="ExternalOutput").ap())
    trunk(nc, *args)
    r = _run(nc, [arrays], core_ids=[0])
    return r.results[0]["out_0_dram"]
```

```python
import math
from contextlib import ExitStack

import concourse.bass as bass
from concourse import mybir

F32 = mybir.dt.float32
F32R = mybir.dt.float32r
ACT = mybir.ActivationFunctionType
ALU = mybir.AluOpType
AX_X = mybir.AxisListType.X

P = 128
TOK = 256
TT = TOK // P
D = 2048
KD = D // P
EPS = 1e-6
MH, MW = 4, 1024
NG, AH = 3, 8
GW = 64
ST = 64
FF = 4 * D
Q_M, K_M, V_M, O_M, IF_M = 0, 1024, 2048, 3072, 4096
Q_A, K_A, V_A = 4104, 4104 + 3072, 4104 + 6144
U_S, GATE = 13320, 14344

LOADW, PIECEW, AHEAD = 2048, 1024, 4
C_LOADS = 16 * 10
SLOTS = 4
C_N1, C_N2, C_CW, C_CB, C_MH, C_DS = 0, 16, 32, 96, 112, 120
PK_B, PK_C, PK_U, PK_FH, PK_FL, PK_MAG, PK_D, PKW = 0, 256, 512, 768, 772, 776, 780, 784
S5_LEN, S5_IN, S5_OUT, S5_SINE = 24, (4, 9, 15, 19), (8, 13, 19, 23), (3, 13)
CONV_AT, SILU_AT = ((8, 10, 11, 12), (16, 17, 18, 20)), (14, 22)
NEG = -1.0e30
ROUND = 12582912.0
GRID16 = 192.0


def inv_two_pi():
    rest, parts = 1.0 / (2.0 * math.pi), []
    for _ in range(3):
        m, e = math.frexp(rest)
        part = math.ldexp(math.floor(m * 4096.0), e - 12)
        parts.append(part)
        rest -= part
    return parts


class Phase:
    def __init__(self, load, block):
        self.load, self.piece, self.block = load, 2 * load, block


LOADS_U, BLOCKS_U = 8, 2
LOADS_A, BLOCKS_A = 16, 4
LOADS_B, BLOCKS_B = 36, 18
LOADS_C, BLOCKS_C = 4, 2
LOADS_D, BLOCKS_D = 36, 12
LOADS_W, BLOCKS_W = 8, 2
LOADS_F1, BLOCKS_F1 = 8, 2
LOADS_F2, BLOCKS_F2 = 16, 2
HALF_LOADS, HALF_BLOCKS = 4 * LOADS_F1 + 2 * LOADS_F2, 4 * BLOCKS_F1 + 2 * BLOCKS_F2
PI = Phase(0, 0)
PU = Phase(PI.load + 1, PI.block + 1)
PA = Phase(PU.load + LOADS_U, PU.block + BLOCKS_U)
PB = Phase(PA.load + 2 * LOADS_A, PA.block + 2 * BLOCKS_A)
PC = Phase(PB.load + 2 * LOADS_B, PB.block + 2 * BLOCKS_B)
PD = Phase(PC.load + 2 * LOADS_C, PC.block + 2 * BLOCKS_C)
PW = Phase(PD.load + 2 * LOADS_D, PD.block + 2 * BLOCKS_D)
PF = Phase(PW.load + 2 * LOADS_W, PW.block + 2 * BLOCKS_W)
TOTAL_LOADS = PF.load + 2 * HALF_LOADS
TOTAL_PIECES = 2 * TOTAL_LOADS


def trunk(nc, x, norm1_g, w_in, conv_w, conv_b, b_igate, b_fgate, mh_norm_g, rel_bias, lam_re, lam_im,
          log_dt, b_re, b_im, c_re, c_im, d_skip, w_glu, w_br_a, w_br_b, w_br_c, w_out, norm2_g,
          w_ff1, w_ff2, final_g, ident_c, consts_c, onehot_c, relmask_c, out):
    ctx = ExitStack()
    with ctx:
        def sem(name):
            return ctx.enter_context(nc.semaphore(name))

        top = [(nc.sbuf_base + 31) // 32 * 32]

        def at(name, shape, off, dt=F32):
            return nc.alloc_sbuf_tensor_at(name, shape, dt, offset=off)

        def size(shape):
            n = 4
            for s in shape[1:]:
                n *= s
            return (n + 31) // 32 * 32

        def take(name, shape, dt=F32):
            t = at(name, shape, top[0], dt)
            top[0] += size(shape)
            return t

        def region(start, items):
            got = []
            for name, shape, dt in items:
                got.append(at(name, shape, start, dt))
                start += size(shape)
            assert start <= nc.sbuf_usable_end, (items[-1][0], start, nc.sbuf_usable_end)
            return got

        raw = take("raw", [P, SLOTS, LOADW])
        w_hi = take("w_hi", [P, SLOTS, PIECEW], F32R)
        w_lo = take("w_lo", [P, SLOTS, PIECEW], F32R)
        x_hi = take("x_hi", [P, KD, TOK], F32R)
        x_lo = take("x_lo", [P, KD, TOK], F32R)
        ident = take("ident", [P, P])
        vec = take("vec_cols", [P, P])
        consts = take("consts", [P, 384 + 256 + 8])
        masks = consts[:, 0:384]
        iota_t = consts[:, 384:640]
        par = consts[:, 640:648]
        half_pi, ones = par[:, 5:6], par[:, 4:5]
        runmax_bc = take("runmax_bc", [P, MH, TOK])
        acols = take("acols", [P, 4, MH])
        small = take("small", [P, 64])
        diag = take("diag", [P, TT, P])
        gate_bias = take("gate_bias", [8, 1])
        ldt = take("log_dt_pairs", [96, 2])
        conv_s = take("conv_s", [P, 48])
        y_base = top[0]
        y_a = take("y_a", [P, 8, TOK])
        y_b = take("y_b", [P, 8, TOK])
        y_s = take("y_s", [P, 8, TOK])
        r0 = top[0]
        pack, s5s, psi, kk2, c2, s2, m1, m2, zin, n1, n2 = region(r0, [
            ("pack", [P, 8, PKW], F32), ("s5_now", [P, PKW], F32), ("psi", [P, 4, TOK], F32),
            ("kk2", [P, 2, TOK], F32), ("cos2", [P, 2, TOK], F32), ("sin2", [P, 2, TOK], F32),
            ("m1", [P, 2, TOK], F32), ("m2", [P, 2, TOK], F32), ("zin", [P, 2, TOK], F32),
            ("n1", [P, 2, TOK], F32), ("n2", [P, 2, TOK], F32)])
        r_s5now = r0 + size([P, 8, PKW])
        r1 = r_s5now + size([P, PKW]) + 4096 + 8 * 2048
        (xs_junk,) = region(r0, [("xs_junk", [P, TT, D], F32)])
        (s5p,) = region(r_s5now, [("s5p", [P, 30, 32], F32)])
        (b_raw, c_raw, bb_t) = region(r_s5now + 3840, [
            ("b_raw", [P, 2, 32, 16], F32), ("c_raw", [P, 2, 8, 64], F32), ("bb_t", [P, 2, 32, 16], F32)])
        (xs,) = region(r1, [("xs", [P, TT, D], F32)])
        b_pad, c_pad = region(r1 + 12288, [("b_pad", [P, 2, 32, 32], F32), ("c_pad", [P, 2, 8, P], F32)])
        (vrows, srows, table, onehot, relmask, relval) = region(r_s5now + 3840 + 12288, [
            ("vrows", [P, P], F32), ("srows", [96, P], F32), ("table", [32, 24], F32),
            ("onehot", [32, 384], F32), ("relmask", [24, 384], F32), ("relval", [24, 384], F32)])
        (gates8, gtmp, fcum, gaf, gr, neg_sel, neg_bc) = region(y_base, [
            ("gates8", [8, TOK], F32), ("gtmp", [8, 4, TOK], F32), ("fcum", [8, TOK], F32),
            ("gaf", [MH, 2, TOK], F32), ("gr", [MH, 2, TOK], F32), ("neg_sel", [8, MH], F32),
            ("neg_bc", [MH, MH, P], F32)])
        (qk_raw, acc, qT, kT, v_m, o_sig, wexp, pT) = region(r1, [
            ("qk_raw", [P, 4, TOK], F32), ("acc", [P, 4, TOK], F32), ("qT", [P, 4, TOK], F32),
            ("kT", [P, 4, TOK], F32), ("v_m", [P, TT, 2, TOK], F32), ("o_sig", [P, 4, TOK], F32),
            ("wexp", [P, 2, 384], F32), ("pT", [P, 2, 384], F32)])
        (hn,) = region(r1 + 4096, [("hn", [P, TT, 2 * TOK], F32)])
        (aq, ak, av, rel, prob, probT) = region(r1, [
            ("aq", [P, 6, TOK], F32), ("ak", [P, 6, TOK], F32), ("av", [P, TT, NG, 2 * P], F32),
            ("rel", [P, NG, TOK], F32), ("prob", [P, NG * TOK + NG * P], F32), ("probT", [P, NG, 384], F32)])
        (mix_hi, mix_lo) = region(y_base, [("mix_hi", [P, KD, TOK], F32R), ("mix_lo", [P, KD, TOK], F32R)])
        r2 = y_base + 32768
        (y_hi, y_lo) = region(r2, [("y_hi", [P, 3, 8, TOK], F32R), ("y_lo", [P, 3, 8, TOK], F32R)])
        r3 = r2 + 49152
        (z_hi, z_lo) = region(r3, [("z_hi", [P, 8, TOK], F32R), ("z_lo", [P, 8, TOK], F32R)])
        (z_lin, z_sig) = region(y_base + 24576, [("z_lin", [P, 4, TOK], F32), ("z_sig", [P, 4, TOK], F32)])
        (gate_sig, mix, mix_t) = region(r3, [
            ("gate_sig", [P, NG, 4, TOK], F32), ("mix", [P, 4, TOK], F32), ("mix_t", [P, 4, TOK], F32)])
        (x1,) = region(r3, [("x1", [P, TT, D], F32)])
        (h_hi, h_lo) = region(y_base, [("h_hi", [P, 32, TOK], F32R), ("h_lo", [P, 32, TOK], F32R)])
        (relu, relu2) = region(y_base + 65536, [("relu", [P, PIECEW], F32), ("relu2", [P, PIECEW], F32)])
        (sq_junk,) = region(y_base, [("sq_junk", [P, TT, D], F32)])
        (fg_bc,) = region(y_base + 65536 + 8192, [("fg_bc", [P, D], F32)])
        assert y_base + 65536 + 16384 <= r3

        ps = ctx.enter_context(nc.psum_tensor("ps", [P, 8, 512], F32))
        SPARE = 4
        B_SC1, B_SC0, B_PV = 2, 4, 5
        B_H = (4, 5)
        B_Y, B_BU = 6, 7

        rel_rows = nc.dram_tensor("rel_rows", (24, 384), F32).ap()
        rel_tiles = nc.dram_tensor("rel_tiles", (AH, P, NG, TOK), F32).ap()

        raw_loaded = [sem(f"raw_loaded{i}") for i in range(SLOTS)]
        hi_ready, lo_ready = sem("hi_ready"), sem("lo_ready")
        piece_done = sem("piece_done")
        psum_free = [sem("psum_free0"), sem("psum_free1")]
        x_loaded, vrows_loaded, c_loaded, s5_loaded, srows_ready = (
            [sem("x_loaded0"), sem("x_loaded1")], sem("vrows_loaded"), sem("c_loaded"), sem("s5_loaded"), sem("srows_ready"))
        rel_stored, rel_spread = sem("rel_stored"), sem("rel_spread")
        sumsq_ready, inv_ready, root_ready, diag_ready = sem("sumsq_ready"), sem("inv_ready"), sem("root_ready"), sem("diag_ready")
        trans_ready, xhi_ready, xlo_ready = sem("trans_ready"), sem("xhi_ready"), sem("xlo_ready")
        cols_ready, cols_copied, relval_ready, relval_copied = sem("cols_ready"), sem("cols_copied"), sem("relval_ready"), sem("relval_copied")
        par_v, par_a = sem("par_v"), sem("par_a")
        rden_ready = sem("rden_ready")
        pad_ready, btr_ready, pack_ready = sem("pad_ready"), sem("btr_ready"), sem("pack_ready")
        g8_a, g8_v, g8_p = sem("g8_a"), sem("g8_v"), sem("g8_p")
        phase_done = sem("phase_done")
        conv_in, conv_acc, conv_sig, qk_ready = sem("conv_in"), sem("conv_acc"), sem("conv_sig"), sem("qk_ready")
        v_ready, o_ready, wexp_in, wexp_ready = sem("v_ready"), sem("o_ready"), sem("wexp_in"), sem("wexp_ready")
        sT_ready, pT_ready, num_ready, rec_ready, hss_ready, hinv_ready = (
            sem("sT_ready"), sem("pT_ready"), sem("num_ready"), sem("rec_ready"), sem("hss_ready"), sem("hinv_ready"))
        hroot_ready, hn_ready, hT_ready = sem("hroot_ready"), sem("hn_ready"), sem("hT_ready")
        s5_staged, psi_ready, sins_ready, s2_ready = sem("s5_staged"), sem("psi_ready"), sem("sins_ready"), sem("s2_ready")
        bu_ready, bu_free, z_ready, rot_done, xr_ready, y_done = (
            sem("bu_ready"), sem("bu_free"), sem("z_ready"), sem("rot_done"), sem("xr_ready"), sem("y_done"))
        ys_ready, gelu_in, gelu_sig, unit_done = sem("ys_ready"), sem("gelu_in"), sem("gelu_sig"), sem("unit_done")
        aq_ready, ak_ready, av_ready, rel_loaded = sem("aq_ready"), sem("ak_ready"), sem("av_ready"), sem("rel_loaded")
        scored, logits_ready, exps_ready, prob_ready = sem("scored"), sem("logits_ready"), sem("exps_ready"), sem("prob_ready")
        probT_made, probT_ready, att_out, att_copied = sem("probT_made"), sem("probT_ready"), sem("att_out"), sem("att_copied")
        z_split_a, z_split_v = sem("z_split_a"), sem("z_split_v")
        glu_in, glu_out, y_split_a, y_split_v = sem("glu_in"), sem("glu_out"), sem("y_split_a"), sem("y_split_v")
        gsig_ready, mix_ready, mixhi_ready, mix_done = sem("gsig_ready"), sem("mix_ready"), sem("mixhi_ready"), sem("mix_done")
        x1_loaded, x1_done = sem("x1_loaded"), sem("x1_done")
        relu_ready, hhi_ready, h_ready = sem("relu_ready"), sem("hhi_ready"), sem("h_ready")
        fg_loaded, out_ready, stored = sem("fg_loaded"), sem("out_ready"), sem("stored")

        def bcast(ap, pos, n):
            dims = [list(d) for d in ap.ap]
            return bass.AP(ap.tensor, ap.offset, dims[:pos] + [[0, n]] + dims[pos:])

        def f(ap):
            return ap.bitcast(F32)

        def barrier(eng, n):
            eng.drain()
            eng.sem_inc(phase_done, 1)
            eng.wait_ge(phase_done, n * 4)

        def split_hi(act, s, o8):
            s += AHEAD
            if not isinstance(o8, int) or s + 8 * o8 < TOTAL_PIECES:
                load = s // 2
                act.wait_ge(raw_loaded[load % SLOTS], 16 * (load // SLOTS + 1) + 16 * o8)
                if s >= SLOTS:
                    act.wait_ge(piece_done, s - SLOTS + 1 + 8 * o8)
                act.activation(w_hi[:, s % SLOTS, :], raw[:, load % SLOTS, s % 2 * PIECEW:(s % 2 + 1) * PIECEW],
                               ACT.Copy).then_inc(hi_ready, 1)

        def split_lo(dve, s, o8):
            s += AHEAD
            if not isinstance(o8, int) or s + 8 * o8 < TOTAL_PIECES:
                dve.wait_ge(hi_ready, s + 1 + 8 * o8)
                load = s // 2
                dve.tensor_tensor(w_lo[:, s % SLOTS, :], raw[:, load % SLOTS, s % 2 * PIECEW:(s % 2 + 1) * PIECEW],
                                  f(w_hi[:, s % SLOTS, :]), ALU.subtract).then_inc(lo_ready, 1)

        def split_first(do, eng):
            for s in range(AHEAD):
                do(eng, s - AHEAD, 0)

        def split_unless_last(do, eng, h, i):
            with eng.If(h * 2 + i < 3):
                for s in range(32 - AHEAD, 32):
                    do(eng, PF.piece + 64 + s, h * 16 + i * 4)

        def block_done(eng, s, n, o8):
            eng.wait_ge(piece_done, s + n + 8 * o8)

        def gemm(pe, s, o8, block, o2, cols, tokens, hi, lo, kk0=0, npieces=8, narrow=False, after=None, xs_wait=None):
            kts = PIECEW // cols
            free = block // 2
            if free > 0:
                pe.wait_ge(psum_free[block % 2], free + o2)
            bank0 = block % 2 if narrow else 2 * (block % 2)
            for q in range(npieces):
                pe.wait_ge(lo_ready, s + q + 1 + 8 * o8)
                if xs_wait is not None:
                    xs_wait(q)
                slot = (s + q) % SLOTS
                whi = w_hi[:, slot, :].rearrange("p (k n) -> p k n", k=kts)
                wlo = w_lo[:, slot, :].rearrange("p (k n) -> p k n", k=kts)
                for k in range(kts):
                    kk = q * kts + k
                    first, last = kk == 0, (q == npieces - 1 and k == kts - 1)
                    if tokens:
                        for t in range(TT):
                            o = ps[:, bank0, t * cols:(t + 1) * cols] if narrow else ps[:, bank0 + t, 0:cols]
                            tk = slice(t * P, (t + 1) * P)
                            st = first and (t == 0 or not narrow)
                            pe.matmul(o, hi[:, kk0 + kk, tk], whi[:, k, :], start=st, stop=False, skip_group_check=True)
                            pe.matmul(o, hi[:, kk0 + kk, tk], wlo[:, k, :], start=False, stop=False, skip_group_check=True)
                            mm = pe.matmul(o, lo[:, kk0 + kk, tk], whi[:, k, :], start=False, stop=last, skip_group_check=True)
                    else:
                        for c in range(cols // P):
                            o = ps[:, bank0 + c // 2, c % 2 * TOK:(c % 2 + 1) * TOK]
                            cs = slice(c * P, (c + 1) * P)
                            st = first and c % 2 == 0
                            pe.matmul(o, whi[:, k, cs], hi[:, kk0 + kk, :], start=st, stop=False, skip_group_check=True)
                            pe.matmul(o, whi[:, k, cs], lo[:, kk0 + kk, :], start=False, stop=False, skip_group_check=True)
                            mm = pe.matmul(o, wlo[:, k, cs], hi[:, kk0 + kk, :], start=False, stop=last, skip_group_check=True)
                mm.then_inc(piece_done, 1)
                if after is not None:
                    after(q)

        block = ctx.enter_context(nc.Block())

        @block.sync
        def _(sp):
            def load(s, o4, src):
                if s >= SLOTS:
                    sp.wait_ge(lo_ready, 2 * (s - SLOTS) + 2 + 8 * o4)
                sp.dma_start(raw[:, s % SLOTS, :].rearrange("p (k n) -> p k n", k=src.shape[1]),
                             src).then_inc(raw_loaded[s % SLOTS], 16)

            w_in_k = w_in[0].rearrange("(k p) n -> p k n", p=P)

            def cols(w, k0, kt, c0, n, turn=0):
                return w[:, k0:k0 + kt, c0:][:, :, bass.ds(turn, n)]

            for t in range(TT):
                sp.dma_start(xs[:, t, :], x[0, t * P:(t + 1) * P, :]).then_inc(x_loaded[t], 16)
            load(PI.load, 0, cols(w_in_k, 0, KD, IF_M, P))
            sp.wait_ge(c_loaded, C_LOADS)
            for j in range(2):
                for m in range(4):
                    load(PU.load + 4 * j + m, 0, cols(w_in_k, 4 * m, 4, U_S + 512 * j, 512))
            with sp.Fori(0, 2) as i:
                n = PA.load
                for base in (Q_M, K_M, V_M, O_M):
                    for m in range(4):
                        load(n, 4 * i, cols(w_in_k, 4 * m, 4, base, 512, i * 512))
                        n += 1
            with sp.Fori(0, 2) as i:
                n = PB.load
                for u in range(2):
                    for base in (Q_A, K_A, V_A):
                        for g in range(NG):
                            for m in range(2):
                                load(n, 9 * i, cols(w_in_k, 8 * m, 8, base + g * AH * P + u * 256, 256, i * 512))
                                n += 1
            w_glu_k = w_glu[0].rearrange("(k p) n -> p k n", p=P)
            with sp.Fori(0, 2) as i:
                n = PC.load
                for base in (0, 1024):
                    for m in range(2):
                        load(n, i, cols(w_glu_k, 4 * m, 4, base, 512, i * 512))
                        n += 1
            br_k = [w[0].rearrange("(k p) n -> p k n", p=P) for w in (w_br_a, w_br_b, w_br_c)]
            with sp.Fori(0, 2) as i:
                n = PD.load
                for u in range(2):
                    for b in range(3):
                        for m in range(4):
                            load(n, 9 * i, cols(w_in_k, 4 * m, 4, GATE + b * D + u * 512, 512, i * 1024))
                            n += 1
                        for m in range(2):
                            load(n, 9 * i, cols(br_k[b], 4 * m, 4, u * 512, 512, i * 512 * 2))
                            n += 1
            w_out_k = w_out[0].rearrange("(k p) n -> p k n", p=P)
            with sp.Fori(0, 2) as i:
                n = PW.load
                for u in range(2):
                    for m in range(4):
                        load(n, 2 * i, cols(w_out_k, 4 * m, 4, u * 512, 512, i * 1024))
                        n += 1
            ff1_k = w_ff1[0].rearrange("(k p) n -> p k n", p=P)
            ff2_k = w_ff2[0].rearrange("(h k p) n -> p h k n", p=P, h=2)
            with sp.Fori(0, 2) as h:
                with sp.Fori(0, 4) as i:
                    n = PF.load
                    for u in range(2):
                        for m in range(4):
                            load(n, 16 * h + 2 * i, cols(ff1_k, 4 * m, 4, u * 512, 512, h * 4096 + i * 1024))
                            n += 1
                with sp.Fori(0, 2) as i:
                    n = PF.load + 4 * LOADS_F1
                    for u in range(2):
                        for m in range(8):
                            load(n, 16 * h + 4 * i,
                                 ff2_k[:, :, :, u * 512:][:, bass.ds(h, 1), 4 * m:4 * m + 4, bass.ds(i * 1024, 512)].rearrange(
                                     "p h k n -> p (h k) n"))
                            n += 1
            for t in range(TT):
                sp.wait_ge(out_ready, t + 1)
                sp.dma_start(out[0, t * P:(t + 1) * P, :], x1[:, t, :]).then_inc(stored, 16)
            sp.wait_ge(stored, 16 * TT)

        @block.tensor
        def _(pe):
            def transposes(src, n0, batches=range(8)):
                for b in batches:
                    if b >= 4:
                        pe.wait_ge(xlo_ready, n0 + b - 3)
                    for k in range(2):
                        for t in range(TT):
                            mm = pe.matmul(ps[:, SPARE + b % 4, k * TOK + t * P:k * TOK + (t + 1) * P],
                                           src[:, t, (2 * b + k) * P:(2 * b + k + 1) * P], diag[:, t, :],
                                           start=True, stop=True)
                    mm.then_inc(trans_ready, 1)

            pe.wait_ge(vrows_loaded, 96)
            pe.wait_ge(srows_ready, 1)
            pe.transpose(ps[:, 0, 0:P], vrows[:], ident[:])
            pe.transpose(ps[:, 0, P:P + 96], srows[:], ident[0:96, 0:96])
            pe.matmul(ps[0:24, 1, 0:384], table[:], onehot[:], start=True, stop=True).then_inc(cols_ready, 1)
            pe.wait_ge(diag_ready, 1)
            transposes(xs, 0, range(4))
            pe.wait_ge(cols_copied, 2)

            def xn_wait(q):
                pe.wait_ge(xlo_ready, 4 * q + 4)

            def rest_of_xn(q):
                if q == 0:
                    transposes(xs, 0, range(4, 8))
            gemm(pe, PI.piece, 0, PI.block, 0, P, False, x_hi, x_lo, npieces=2, xs_wait=xn_wait, after=rest_of_xn)

            def setup_steps(pos):
                if pos == 3:
                    pe.wait_ge(g8_v, 1)
                    pe.matmul(ps[0:MH, SPARE, 0:TOK], ident[0:8, 0:MH], gates8[:], start=True, stop=False,
                              skip_group_check=True)
                    pe.matmul(ps[0:MH, SPARE, 0:TOK], neg_sel[:], fcum[:], start=False, stop=True, skip_group_check=True)
                    pe.matmul(ps[0:MH, SPARE, TOK:2 * TOK], ident[0:8, MH:2 * MH], fcum[:], start=False, stop=True,
                              skip_group_check=True).then_inc(g8_p, 1)
                if pos == 6:
                    pe.wait_ge(g8_v, 2)
                    pe.wait_ge(g8_a, 3)
                    for h in range(MH):
                        pe.matmul(ps[:, SPARE + h // 2, h % 2 * TOK:(h % 2 + 1) * TOK], neg_bc[:, h, :], gr[:, 0, :],
                                  start=h % 2 == 0, stop=True, skip_group_check=True)
                    for t in range(TT):
                        pe.transpose(ps[:, SPARE + 2, t * MH:(t + 1) * MH], gaf[:, 0, t * P:(t + 1) * P], ident[0:MH, 0:MH])
                        mm = pe.transpose(ps[:, SPARE + 2, (2 + t) * MH:(3 + t) * MH], gr[:, 1, t * P:(t + 1) * P],
                                          ident[0:MH, 0:MH])
                    mm.then_inc(g8_p, 1)
                if pos in (12, 14):
                    which = (12, 14).index(pos)
                    padded = (c_pad, b_pad)[which]
                    pe.wait_ge(pad_ready, which + 1)
                    pe.wait_ge(g8_v, 3)
                    for b in range(4):
                        if which:
                            pe.wait_ge(pack_ready, b + 1)
                        for h in range(2):
                            for ri in range(2):
                                t = 2 * b + h
                                src = (padded[:, ri, 4 * t:4 * t + 4, :].rearrange("p j c -> p (j c)") if which
                                       else padded[:, ri, t, :])
                                mm = pe.transpose(ps[:, SPARE + b, h * 256 + ri * P:h * 256 + (ri + 1) * P], src, ident[:])
                        mm.then_inc(btr_ready, 1)
            for j in range(2):
                gemm(pe, PU.piece + 8 * j, 0, PU.block + j, 0, 512, False, x_hi, x_lo,
                     after=lambda q, j=j: setup_steps(8 * j + q))
            barrier(pe, 1)

            def s5_unit(n, q):
                if q in S5_IN:
                    j = S5_IN.index(q)
                    if j == 0:
                        pe.wait_ge(s5_staged, n + 1)
                    pe.wait_ge(bu_free, n * 4 + j + 1)
                    rows = slice(32 * j, 32 * j + 32)
                    for ri in range(2):
                        mm = pe.matmul(ps[:, B_BU, ri * TOK:(ri + 1) * TOK],
                                       s5s[rows, PK_B + ri * P:PK_B + (ri + 1) * P], s5s[rows, PK_U:PK_U + TOK],
                                       start=ri == 0, stop=True, skip_group_check=True)
                    mm.then_inc(bu_ready, 1)
                if q in S5_OUT:
                    j = S5_OUT.index(q)
                    if j == 0:
                        pe.wait_ge(ys_ready, n + 1)
                    pe.wait_ge(xr_ready, n * 4 + j + 1)
                    for ri in range(2):
                        mm = pe.matmul(ps[32 * j:32 * j + 32, B_Y, 0:TOK],
                                       s5s[:, PK_C + ri * P + 32 * j:PK_C + ri * P + 32 * j + 32], n1[:, ri, :],
                                       start=ri == 0, stop=ri == 1, skip_group_check=True)
                    mm.then_inc(y_done, 1)

            with pe.Fori(0, 2) as i:
                def after(pos):
                    s5_unit(i, pos)
                    if pos in (23, 24):
                        h = pos - 23
                        if h == 0:
                            pe.wait_ge(qk_ready, i * 2 + 2)
                        for e in range(2):
                            pe.matmul(ps[:, B_H[h], 0:TOK], kT[:, 2 * h + e, 0:P], qT[:, 2 * h + e, :],
                                      start=e == 0, stop=e == 1, skip_group_check=True)
                        for e in range(2):
                            mm = pe.matmul(ps[:, B_H[h], TOK:TOK + P], kT[:, 2 * h + e, P:TOK],
                                           qT[:, 2 * h + e, P:TOK], start=False, stop=e == 1,
                                           skip_group_check=True)
                        mm.then_inc(sT_ready, 1)
                    if pos == 26:
                        pe.wait_ge(v_ready, i + 1)
                        pe.wait_ge(pT_ready, i * 2 + 2)
                        pe.wait_ge(bu_free, i * 4 + 5)
                        for h in range(2):
                            den = 2 * h
                            pe.matmul(ps[:, B_H[h], 0:TOK], pT[:, h, 0:P], v_m[:, 0, h, :], start=True, stop=True,
                                      skip_group_check=True)
                            pe.matmul(ps[:, B_H[h], TOK:2 * TOK], pT[:, h, P:TOK], v_m[:, 0, h, :], start=False,
                                      stop=False, skip_group_check=True)
                            pe.matmul(ps[:, B_H[h], TOK:2 * TOK], pT[:, h, TOK:384], v_m[:, 1, h, :], start=False,
                                      stop=True, skip_group_check=True)
                            pe.matmul(ps[:, B_BU, den:den + 1], pT[:, h, 0:P], ones, start=h == 0, stop=True,
                                      skip_group_check=True)
                            pe.matmul(ps[:, B_BU, den + 1:den + 2], pT[:, h, P:TOK], ones, start=False, stop=False,
                                      skip_group_check=True)
                            mm = pe.matmul(ps[:, B_BU, den + 1:den + 2], pT[:, h, TOK:384], ones, start=False,
                                           stop=True, skip_group_check=True)
                        mm.then_inc(num_ready, 1)
                    if pos == 31:
                        pe.wait_ge(hn_ready, i + 1)
                        for h in range(2):
                            for e in range(2):
                                for t in range(TT):
                                    mm = pe.transpose(ps[:, B_H[h], e * TOK + t * P:e * TOK + (t + 1) * P],
                                                      hn[:, t, h * TOK + e * P:h * TOK + (e + 1) * P], ident[:])
                        mm.then_inc(hT_ready, 1)
                for b in range(BLOCKS_A):
                    gemm(pe, PA.piece + 8 * b, 4 * i, PA.block + b, 2 * i, 512, b == 2, x_hi, x_lo,
                         after=lambda q, b=b: after(8 * b + q))
            barrier(pe, 2)
            with pe.Fori(0, 2) as i:
                for u in range(2):
                    def after(pos):
                        at_b = 36 * u + pos
                        s5_unit(i * 3 + (2 + at_b // S5_LEN), at_b % S5_LEN)
                        slot = i * 4 + 2 * u
                        if pos in (24, 30):
                            a = (24, 30).index(pos)
                            if a == 0:
                                pe.wait_ge(aq_ready, i * 6 + 3 * u + 3)
                                pe.wait_ge(ak_ready, i * 6 + 3 * u + 3)
                            else:
                                pe.wait_ge(probT_ready, slot + 1)
                            for g in range(NG):
                                c = 2 * g + a
                                o1 = ps[:, B_SC1 + g // 2, g % 2 * TOK:(g % 2 + 1) * TOK]
                                pe.matmul(o1, aq[:, c, P:TOK], ak[:, c, :], start=True, stop=True)
                                mm = pe.matmul(ps[:, B_SC0, g * P:(g + 1) * P], aq[:, c, 0:P], ak[:, c, 0:P],
                                               start=True, stop=True)
                            mm.then_inc(scored, 1)
                        if pos == 28:
                            prob_transposes(slot)
                        if pos == 35:
                            head_out(slot, 0)
                            prob_transposes(slot + 1)
                            head_out(slot + 1, 1)

                    def prob_transposes(slot):
                        pe.wait_ge(prob_ready, slot + 1)
                        for g in range(NG):
                            bank = B_SC1 + g
                            pe.transpose(ps[:, bank, 0:P], prob[:, NG * TOK + g * P:NG * TOK + (g + 1) * P], ident[:])
                            pe.transpose(ps[:, bank, P:2 * P], prob[:, g * TOK:g * TOK + P], ident[:])
                            mm = pe.transpose(ps[:, bank, 2 * P:3 * P], prob[:, g * TOK + P:(g + 1) * TOK], ident[:])
                        mm.then_inc(probT_made, 1)

                    def head_out(slot, a):
                        pe.wait_ge(probT_ready, slot + 1)
                        pe.wait_ge(att_copied, slot + 1)
                        for g in range(NG):
                            if a == 0:
                                pe.wait_ge(av_ready, i * 6 + 3 * u + g + 1)
                            pe.matmul(ps[:, B_PV, 0:TOK], av[:, 0, g, a * P:(a + 1) * P], probT[:, g, 0:TOK],
                                      start=g == 0, stop=False, skip_group_check=True)
                            mm = pe.matmul(ps[:, B_PV, P:TOK], av[:, 1, g, a * P:(a + 1) * P], probT[:, g, TOK:384],
                                           start=False, stop=g == 2, skip_group_check=True)
                        mm.then_inc(att_out, 1)
                    for b in range(9):
                        n = 9 * u + b
                        gemm(pe, PB.piece + n * 4, 9 * i, PB.block + n, 9 * i, 256, b >= 6, x_hi, x_lo, npieces=4,
                             narrow=True, after=lambda q, b=b: after(4 * b + q))
            barrier(pe, 3)
            def z_wait(q):
                pe.wait_ge(z_split_v, q + 1)
            with pe.Fori(0, 2) as i:
                for b in range(2):
                    gemm(pe, PC.piece + 4 * b, i, PC.block + b, i, 512, False, z_hi, z_lo, npieces=4,
                         xs_wait=None if b else z_wait)
            pe.wait_ge(y_split_v, 2)
            with pe.Fori(0, 2) as i:
                for u in range(2):
                    for b in range(3):
                        s, n = PD.piece + 36 * u + 12 * b, PD.block + 6 * u + 2 * b
                        gemm(pe, s, 9 * i, n, 6 * i, 512, False, x_hi, x_lo)
                        if b == 2:
                            pe.wait_ge(y_split_v, 3)
                        gemm(pe, s + 8, 9 * i, n + 1, 6 * i, 512, False, y_hi[:, b], y_lo[:, b], npieces=4)
            def mix_wait(q):
                if q in (0, 6):
                    pe.wait_ge(mix_done, 4 if q else 3)
            with pe.Fori(0, 2) as i:
                for u in range(2):
                    gemm(pe, PW.piece + 8 * u, 2 * i, PW.block + u, i, 512, True, mix_hi, mix_lo,
                         xs_wait=None if u else mix_wait)
            pe.wait_ge(diag_ready, 2)
            transposes(x1, 8)

            def hn_wait(q):
                pe.wait_ge(xlo_ready, 8 + q + 1)
            with pe.Fori(0, 2) as h:
                with pe.Fori(0, 4) as i:
                    for u in range(2):
                        gemm(pe, PF.piece + 8 * u, h * 16 + i * 2, PF.block + u, h * 6 + i, 512, False, x_hi, x_lo,
                             xs_wait=None if u else hn_wait)
                with pe.Fori(0, 2) as i:
                    def h_wait(q):
                        if q in (0, 14):
                            pe.wait_ge(h_ready, h * 8 + (9 if q else 8))
                    for u in range(2):
                        gemm(pe, PF.piece + 64 + 16 * u, h * 16 + i * 4, PF.block + 8 + u, h * 6 + i, 512, True,
                             h_hi, h_lo, npieces=16, xs_wait=None if u else h_wait)

        @block.scalar
        def _(act):
            def out_of_psum(dst, block, func=ACT.Copy, banks=2, width=512):
                act.activation(dst, ps[:, 2 * (block % 2):2 * (block % 2) + banks, 0:width], func).then_inc(
                    psum_free[block % 2], 1)

            def sum_of_squares(src, junk):
                act.activation(junk[:, 0, :], src[:, 0, :], ACT.Square, accum_out=small[:, 0:1]).then_inc(sumsq_ready, 1)

            def root(n):
                act.wait_ge(inv_ready, n)
                act.activation(small[:, 6:8], small[:, 4:6], ACT.Sqrt).then_inc(root_ready, 1)

            act.dma_start(ident[:], ident_c).then_inc(c_loaded, 16)
            act.dma_start(vrows[C_N1:C_N1 + 16, :], norm1_g.rearrange("a (k p) -> (a k) p", p=P)).then_inc(vrows_loaded, 16)
            act.dma_start(vrows[C_N2:C_N2 + 16, :], norm2_g.rearrange("a (k p) -> (a k) p", p=P)).then_inc(vrows_loaded, 16)
            act.dma_start(vrows[C_CW:C_CW + 64, :], conv_w[0].rearrange("j (k p) -> (j k) p", p=P)).then_inc(vrows_loaded, 16)
            act.dma_start(vrows[C_CB:C_CB + 16, :], conv_b.rearrange("a (k p) -> (a k) p", p=P)).then_inc(vrows_loaded, 16)
            act.dma_start(vrows[C_MH:C_MH + 8, :], mh_norm_g.rearrange("a (k p) -> (a k) p", p=P)).then_inc(vrows_loaded, 16)
            act.dma_start(vrows[C_DS:C_DS + 8, :], d_skip[0].rearrange("(k g) c -> k (g c)", k=8)).then_inc(vrows_loaded, 16)
            act.dma_start(consts[:], consts_c).then_inc(c_loaded, 16)
            act.dma_start(srows[0:32, :], lam_re[0].rearrange("(j q) s -> j (q s)", q=2)).then_inc(c_loaded, 16)
            act.dma_start(srows[32:64, :], lam_im[0].rearrange("(j q) s -> j (q s)", q=2)).then_inc(c_loaded, 16)
            act.dma_start(ldt[64:96, :], log_dt[0].rearrange("(j q) -> j q", q=2)).then_inc(c_loaded, 16)
            act.dma_start(gate_bias[0:4, :], b_igate[0].rearrange("(h a) -> h a", a=1)).then_inc(c_loaded, 16)
            act.dma_start(gate_bias[4:8, :], b_fgate[0].rearrange("(h a) -> h a", a=1)).then_inc(c_loaded, 16)
            act.dma_start(table[:], rel_bias).then_inc(c_loaded, 16)
            act.dma_start(onehot[:], onehot_c).then_inc(c_loaded, 16)
            act.dma_start(relmask[:], relmask_c).then_inc(c_loaded, 16)
            for ri, w in enumerate((b_re, b_im)):
                act.dma_start(b_raw[:, ri], w[0].rearrange("(j q) s c -> (q s) j c", q=2)).then_inc(s5_loaded, 16)
            for ri, w in enumerate((c_re, c_im)):
                act.dma_start(c_raw[:, ri], w[0].rearrange("(t g) c s -> (g c) t s", t=8)).then_inc(s5_loaded, 16)
            act.wait_ge(x_loaded[0], 16)
            sum_of_squares(xs, xs_junk)
            root(1)
            split_first(split_hi, act)

            def features_hi(n0, gcol):
                for b in range(8):
                    act.wait_ge(trans_ready, n0 + b + 1)
                    for k in range(2):
                        kk = 2 * b + k
                        last = act.activation(x_hi[:, kk, :], ps[:, SPARE + b % 4, k * TOK:(k + 1) * TOK], ACT.Copy,
                                              scale=vec[:, gcol + kk:gcol + kk + 1])
                    last.then_inc(xhi_ready, 1)
            act.wait_ge(cols_copied, 1)
            features_hi(0, C_N1)
            pack_u = pack[:, :, PK_U:PK_U + TOK]
            for s in range(2):
                split_hi(act, s, 0)
            act.wait_ge(c_loaded, C_LOADS)
            block_done(act, PI.piece, 2, 0)
            act.activation(gates8[:], ps[0:8, 0, 0:TOK], ACT.Identity, bias=gate_bias[:]).then_inc(psum_free[0], 1)
            act.drain()
            act.activation(gtmp[:, 0, :], gates8[:], ACT.Abs)
            act.drain()
            act.activation(gtmp[:, 1, :], gtmp[:, 0, :], ACT.Exp, scale=-1.0)
            act.wait_ge(cols_copied, 2)
            act.activation(s5p[:, 3, :], s5p[:, 2, :], ACT.Exp).then_inc(par_a, 1)
            act.drain()
            act.activation(gtmp[:, 2, :], gtmp[:, 1, :], ACT.Ln, bias=1.0).then_inc(g8_a, 2)
            for s in range(2, 4):
                split_hi(act, s, 0)
            act.wait_ge(par_v, 1)
            act.activation(s5p[:, 5, :], s5p[:, 4, :], ACT.Exp).then_inc(par_a, 1)
            act.activation(s5p[:, 7, :].bitcast(F32R), s5p[:, 6, :], ACT.Copy).then_inc(par_a, 1)
            for s in range(4, 6):
                split_hi(act, s, 0)
            act.wait_ge(g8_v, 2)
            act.activation(gr[:, 1, :], gaf[:, 1, :], ACT.Exp, scale=-1.0).then_inc(g8_a, 1)
            for s in range(6, 10):
                split_hi(act, s, 0)
            act.wait_ge(par_v, 2)
            act.activation(s5p[:, 20, :], s5p[:, 19, :], ACT.Sin, scale=math.pi)
            act.activation(s5p[:, 21, :], s5p[:, 19, :], ACT.Abs).then_inc(par_a, 1)
            act.wait_ge(par_a, 4)
            act.activation(s5p[:, 22, :], s5p[:, 21, :], ACT.Sin, bias=half_pi, scale=-math.pi)
            act.activation(s5p[:, 23, :], s5p[:, 21, :], ACT.Sin, bias=half_pi, scale=-2.0 * math.pi).then_inc(par_a, 1)
            block_done(act, PU.piece, 8, 0)
            act.activation(pack_u[:, 0:4, :], ps[:, 2:4, :].rearrange("p b (c t) -> p (b c) t", t=TOK),
                           ACT.Copy).then_inc(psum_free[1], 1)
            for s in range(10, 18):
                split_hi(act, s, 0)
                if s in (14, 16):
                    which = (14, 16).index(s)
                    for b in range(4):
                        act.wait_ge(btr_ready, 4 * which + b + 1)
                        col = PK_B if which else PK_C
                        act.activation(pack[:, 2 * b:2 * b + 2, col:col + 256],
                                       ps[:, SPARE + b, :].rearrange("p (t c) -> p t c", t=2), ACT.Copy).then_inc(pack_ready, 1)
            block_done(act, PU.piece + 8, 8, 0)
            act.activation(pack_u[:, 4:8, :], ps[:, 0:2, :].rearrange("p b (c t) -> p (b c) t", t=TOK),
                           ACT.Copy).then_inc(psum_free[0], 1)
            barrier(act, 1)

            def s5_unit(n, q):
                if q == 0:
                    act.wait_ge(unit_done, n + 1)
                    act.activation(s5s[:], pack[:, bass.ds(n, 1), :].rearrange("p a c -> p (a c)"), ACT.Copy).then_inc(
                        s5_staged, 1)
                if q in S5_SINE:
                    h = S5_SINE.index(q)
                    act.wait_ge(psi_ready, n * 2 + h + 1)
                    act.wait_ge(rot_done, n * 4 + 2 * h + 1)
                    ph = psi[:, 2 * h:2 * h + 2, :]
                    act.activation(s2[:], ph, ACT.Sin, scale=math.pi)
                    act.drain()
                    act.activation(ph, ph, ACT.Abs)
                    act.drain()
                    act.activation(c2[:], ph, ACT.Sin, bias=half_pi, scale=-2.0 * math.pi)
                    act.activation(ph, ph, ACT.Sin, bias=half_pi, scale=-math.pi).then_inc(sins_ready, 1)
                if q == S5_LEN - 1:
                    act.wait_ge(gelu_in, n + 1)
                    act.activation(m2[:, 1, :], m2[:, 0, :], ACT.Sigmoid, scale=2.0 * math.sqrt(2.0 / math.pi)).then_inc(
                        gelu_sig, 1)

            with act.Fori(0, 2) as i:
                def conv_copy(b):
                    s = PA.piece + 8 * b
                    block_done(act, s, 8, 4 * i)
                    if b:
                        act.wait_ge(qk_ready, i * 2 + 1)
                    act.activation(qk_raw[:], ps[:, 2 * ((PA.block + b) % 2):2 * ((PA.block + b) % 2) + 2, :],
                                   ACT.Copy).then_inc(psum_free[(PA.block + b) % 2], 1)
                    act.drain()
                    act.sem_inc(conv_in, 1)
                for pos in range(32):
                    split_hi(act, PA.piece + pos, 4 * i)
                    s5_unit(i, pos)
                    if pos == 7:
                        conv_copy(0)
                    if pos in SILU_AT:
                        b = SILU_AT.index(pos)
                        act.wait_ge(conv_acc, i * 2 + b + 1)
                        act.activation(qk_raw[:], acc[:], ACT.Sigmoid).then_inc(conv_sig, 1)
                    if pos == 15:
                        conv_copy(1)
                    if pos == 6:
                        for h in range(2):
                            act.wait_ge(wexp_in, i * 2 + h + 1)
                            act.activation(wexp[:, h, 0:TOK], wexp[:, h, 0:TOK], ACT.Exp, bias=conv_s[:, 44 + h:45 + h])
                            act.activation(wexp[:, h, TOK:384], wexp[:, h, TOK:384], ACT.Exp,
                                           bias=conv_s[:, 46 + h:47 + h]).then_inc(wexp_ready, 1)
                    if pos == 23:
                        s, blk = PA.piece + 16, PA.block + 2
                        block_done(act, s, 8, 4 * i)
                        act.wait_ge(num_ready, i + 1)
                        act.activation(v_m[:],
                                       ps[:, 2 * (blk % 2):2 * (blk % 2) + 2, :].rearrange("p t (h e) -> p t h e", h=2),
                                       ACT.Copy).then_inc(psum_free[blk % 2], 1)
                        act.drain()
                        act.sem_inc(v_ready, 1)
                    if pos == 28:
                        act.wait_ge(rec_ready, i + 1)
                        for m in range(4):
                            last = act.activation(qk_raw[:, m, :], ps[:, B_H[m // 2], m % 2 * TOK:(m % 2 + 1) * TOK],
                                                  ACT.Square, scale=small[:, 38 + m:39 + m],
                                                  accum_out=small[:, 42 + m:43 + m])
                        last.then_inc(hss_ready, 1)
                    if pos == 28:
                        act.wait_ge(hinv_ready, i + 1)
                        act.activation(small[:, 54:58], small[:, 50:54], ACT.Sqrt).then_inc(hroot_ready, 1)
                s, blk = PA.piece + 24, PA.block + 3
                block_done(act, s, 8, 4 * i)
                act.activation(o_sig[:], ps[:, 2 * (blk % 2):2 * (blk % 2) + 2, :], ACT.Sigmoid).then_inc(
                    psum_free[blk % 2], 1)
                act.drain()
                act.sem_inc(o_ready, 1)
            barrier(act, 2)

            with act.Fori(0, 2) as i:
                for u in range(2):
                    def bias_tiles(a):
                        act.wait_ge(logits_ready, i * 4 + 2 * u + a + 1)
                        act.dma_start(rel[:], rel_tiles[bass.ds(i * 4 + (2 * u + a), 1)].rearrange(
                            "a p g t -> (a p) g t")).then_inc(rel_loaded, 16)

                    for pos in range(36):
                        split_hi(act, PB.piece + 36 * u + pos, 9 * i)
                        slot = i * 4 + 2 * u
                        if pos % 4 == 3:
                            b = pos // 4
                            blk = PB.block + 9 * u + b
                            block_done(act, PB.piece + 36 * u + 4 * b, 4, 9 * i)
                            src = ps[:, blk % 2, :].rearrange("p (a t) -> p a t", a=2)
                            if b < 6:
                                dst = (aq if b < 3 else ak)[:, 2 * (b % 3):2 * (b % 3) + 2, :]
                                act.wait_ge(scored, slot + 1)
                            else:
                                dst = av[:, :, b - 6, :]
                                act.wait_ge(att_out, slot + 1)
                            act.activation(dst, src, ACT.Copy).then_inc(psum_free[blk % 2], 1)
                            act.drain()
                            act.sem_inc((aq_ready, ak_ready, av_ready)[b // 3], 1)
                        at_b = 36 * u + pos
                        s5_unit(i * 3 + (2 + at_b // S5_LEN), at_b % S5_LEN)
                        if pos == 14:
                            bias_tiles(0)
                        if pos in (26, 32):
                            a = (26, 32).index(pos)
                            act.wait_ge(logits_ready, slot + a + 2)
                            act.activation(prob[:, 0:NG * TOK], prob[:, 0:NG * TOK], ACT.Exp, bias=small[:, 22:23],
                                           accum_out=small[:, 24:25])
                            act.activation(prob[:, NG * TOK:], prob[:, NG * TOK:], ACT.Exp, bias=small[:, 23:24],
                                           accum_out=small[:, 25:26]).then_inc(exps_ready, 1)
                            if a == 0:
                                bias_tiles(1)
                        if pos == 29:
                            act.wait_ge(probT_made, slot + 2)
                            act.wait_ge(att_out, slot + 1)
                            act.activation(probT[:], ps[:, B_SC1:B_SC1 + 3, 0:384], ACT.Copy).then_inc(probT_ready, 1)
                    act.wait_ge(probT_made, slot + 3)
                    act.wait_ge(att_out, slot + 2)
                    act.activation(probT[:], ps[:, B_SC1:B_SC1 + 3, 0:384], ACT.Copy).then_inc(probT_ready, 1)
            barrier(act, 3)

            act.wait_ge(unit_done, 9)
            for q in range(4):
                act.activation(z_hi[:, 2 * q:2 * q + 2], y_s[:, 2 * q:2 * q + 2], ACT.Copy).then_inc(z_split_a, 1)
            for b, y in enumerate((y_a, y_b)):
                act.activation(y_hi[:, b], y[:], ACT.Copy).then_inc(y_split_a, 1)
            with act.Fori(0, 2) as i:
                for b in range(2):
                    s, blk = PC.piece + 4 * b, PC.block + b
                    for q in range(4):
                        split_hi(act, s + q, i)
                    block_done(act, s, 4, i)
                    act.wait_ge(glu_out, i + 1)
                    act.activation((z_lin, z_sig)[b][:], ps[:, 2 * (blk % 2):2 * (blk % 2) + 2, :],
                                   (ACT.Copy, ACT.Sigmoid)[b]).then_inc(psum_free[blk % 2], 1)
                    act.drain()
                    act.sem_inc(glu_in, 1)
            act.wait_ge(glu_out, 3)
            act.activation(y_hi[:, 2], y_s[:], ACT.Copy).then_inc(y_split_a, 1)

            with act.Fori(0, 2) as i:
                for u in range(2):
                    for b in range(3):
                        s, blk = PD.piece + 36 * u + 12 * b, PD.block + 6 * u + 2 * b
                        for q in range(8):
                            split_hi(act, s + q, 9 * i)
                        block_done(act, s, 8, 9 * i)
                        act.wait_ge(mix_ready, i * 2 + u + 1)
                        act.activation(gate_sig[:, b], ps[:, 2 * (blk % 2):2 * (blk % 2) + 2, :],
                                       ACT.Sigmoid).then_inc(psum_free[blk % 2], 1)
                        act.drain()
                        act.sem_inc(gsig_ready, 1)
                        for q in range(4):
                            split_hi(act, s + 8 + q, 9 * i)
                    act.wait_ge(mix_ready, i * 2 + u + 2)
                    act.activation(mix_hi[:, bass.ds(i * 8 + 4 * u, 4), :], mix[:], ACT.Copy).then_inc(mixhi_ready, 1)

            with act.Fori(0, 2) as i:
                for s in range(16):
                    split_hi(act, PW.piece + s, 2 * i)
            act.wait_ge(x1_done, 4)
            sum_of_squares(x1, sq_junk)
            root(2)
            features_hi(8, C_N2)

            def ff1(h, i):
                for u in range(2):
                    s, blk = PF.piece + 8 * u, PF.block + u
                    for q in range(8):
                        split_hi(act, s + q, 16 * h + 2 * i)
                    block_done(act, s, 8, 16 * h + 2 * i)
                    act.wait_ge(h_ready, h * 8 + i * 2 + u + 1)
                    act.activation(relu[:].rearrange("p (b n) -> p b n", b=2),
                                   ps[:, 2 * (blk % 2):2 * (blk % 2) + 2, :], ACT.Relu).then_inc(psum_free[blk % 2], 1)
                    act.drain()
                    act.sem_inc(relu_ready, 1)
                    act.activation(h_hi[:, bass.ds(i * 8 + 4 * u, 4), :], relu[:], ACT.Square).then_inc(hhi_ready, 1)
            with act.Fori(0, 2) as h:
                with act.Fori(0, 4) as i:
                    ff1(h, i)
                with act.Fori(0, 2) as i:
                    for s in range(28):
                        split_hi(act, PF.piece + 64 + s, 16 * h + 4 * i)
                    split_unless_last(split_hi, act, h, i)
            act.wait_ge(x1_done, 12)
            sum_of_squares(x1, sq_junk)
            root(3)

        @block.vector
        def _(dve):
            def chain(*ops):
                for op in ops:
                    op()
                    dve.drain()

            def inverse_rms(n, width, src, junk):
                dve.scalar_tensor_tensor(junk[:, 1, :], src[:, 1, :], 1.0, src[:, 1, :], ALU.mult, ALU.mult,
                                         accum_out=small[:, 1:2])
                dve.drain()
                dve.wait_ge(sumsq_ready, n)
                dve.tensor_scalar(small[:, 2:4], small[:, 0:2], 1.0 / width, EPS, ALU.mult, ALU.add)
                dve.drain()
                dve.reciprocal(small[:, 4:6], small[:, 2:4]).then_inc(inv_ready, 1)
                dve.wait_ge(root_ready, n)
                newton(small[:, 2:4], small[:, 6:8], small[:, 8:10], small[:, 20:22])

            def newton(v, r, dst, tmp):
                dve.tensor_tensor(tmp, r, r, ALU.mult)
                dve.drain()
                dve.tensor_tensor(tmp, tmp, v, ALU.mult)
                dve.drain()
                dve.tensor_scalar(tmp, tmp, -0.5, 1.5, ALU.mult, ALU.add)
                dve.drain()
                dve.tensor_tensor(dst, r, tmp, ALU.mult)
                dve.drain()

            def diagonals():
                for t in range(TT):
                    last = dve.tensor_scalar(diag[:, t, :], ident[:], small[:, 8 + t:9 + t], None, ALU.mult)
                last.then_inc(diag_ready, 1)

            def features_lo(n0, gcol, splits=()):
                for b in range(8):
                    dve.wait_ge(xhi_ready, n0 + b + 1)
                    for k in range(2):
                        kk = 2 * b + k
                        last = dve.scalar_tensor_tensor(x_lo[:, kk, :], ps[:, SPARE + b % 4, k * TOK:(k + 1) * TOK],
                                                        vec[:, gcol + kk:gcol + kk + 1], f(x_hi[:, kk, :]),
                                                        ALU.mult, ALU.subtract)
                    last.then_inc(xlo_ready, 1)
                    if b in splits:
                        split_lo(dve, splits[b] - AHEAD, 0)

            for s in (bu_free, ys_ready, unit_done, att_copied, glu_out, mix_ready, h_ready, rot_done, att_out,
                      scored, num_ready, s2_ready, y_done, logits_ready, probT_made):
                dve.sem_inc(s, 1)
            dve.wait_ge(x_loaded[1], 16)
            inverse_rms(1, D, xs, xs_junk)
            dve.wait_ge(c_loaded, C_LOADS)
            diagonals()
            dve.tensor_copy(srows[64:96, :].rearrange("p (q s) -> p q s", q=2), bcast(ldt[64:96, :], 2, ST)).then_inc(
                srows_ready, 1)
            dve.tensor_scalar(neg_sel[:], ident[0:8, MH:2 * MH], -1.0, None, ALU.mult)
            dve.tensor_scalar(neg_bc[:], bcast(ident[0:MH, 0:MH], 2, P), -1.0, None, ALU.mult)
            dve.wait_ge(cols_ready, 1)
            dve.tensor_copy(vec[:], ps[:, 0, 0:P]).then_inc(cols_copied, 1)
            dve.tensor_copy(s5p[:, 0:3, :], ps[:, 0, P:P + 96].rearrange("p (a b) -> p a b", a=3))
            dve.tensor_tensor(relval[:], ps[0:24, 1, 0:384], relmask[:], ALU.add)
            dve.drain()
            dve.sem_inc(cols_copied, 1)
            dve.tensor_tensor(s5p[:, 15:17, :], s5p[:, 0:2, :], s5p[:, 0:2, :], ALU.mult)
            dve.drain()
            dve.tensor_tensor(s5p[:, 16, :], s5p[:, 15, :], s5p[:, 16, :], ALU.add)
            dve.drain()
            dve.reciprocal(s5p[:, 16, :], s5p[:, 16, :]).then_inc(rden_ready, 1)
            split_lo(dve, 0 - AHEAD, 0)
            split_lo(dve, 1 - AHEAD, 0)
            features_lo(0, C_N1, {3: 2, 7: 3})

            def split_range(a, b):
                for s in range(a, b):
                    split_lo(dve, s, 0)
            split_range(0, 2)
            dve.memset(gtmp[:, 3, :], 1.0)
            dve.wait_ge(g8_a, 2)
            dve.tensor_scalar(gtmp[:, 0, :], gates8[:], 0.0, None, ALU.min)
            dve.drain()
            dve.tensor_tensor(gtmp[:, 0, :], gtmp[:, 0, :], gtmp[:, 2, :], ALU.subtract)
            dve.drain()
            dve.tensor_tensor_scan(fcum[:], gtmp[:, 3, :], gtmp[:, 0, :], 0.0, ALU.mult, ALU.add).then_inc(g8_v, 1)
            split_range(2, 5)
            dve.wait_ge(g8_p, 1)
            dve.tensor_copy(gaf[:], ps[0:MH, SPARE, :].rearrange("p (a t) -> p a t", a=2))
            dve.drain()
            dve.tensor_tensor_scan(gr[:, 0, :], gaf[:, 0, :], gaf[:, 0, :], 0.0, ALU.max, ALU.max)
            dve.drain()
            dve.tensor_tensor(gaf[:, 1, :], gaf[:, 1, :], gr[:, 0, :], ALU.add).then_inc(g8_v, 1)
            split_range(5, 10)
            dve.wait_ge(g8_p, 2)
            for b in range(2):
                dve.tensor_copy(runmax_bc[:, 2 * b:2 * b + 2, :], ps[:, SPARE + b, :].rearrange("p (a t) -> p a t", a=2))
            dve.tensor_copy(acols[:], ps[:, SPARE + 2, 0:4 * MH].rearrange("p (a h) -> p a h", a=4)).then_inc(g8_v, 1)
            split_range(10, 18)
            barrier(dve, 1)

            def pair_in(n, j):
                dve.wait_ge(bu_ready, n * 4 + j + 1)
                dve.tensor_tensor(m1[:], ps[:, B_BU, :].rearrange("p (r t) -> p r t", r=2), bcast(c2[:, j % 2, :], 1, 2), ALU.mult)
                dve.tensor_tensor(m2[:], ps[:, B_BU, :].rearrange("p (r t) -> p r t", r=2), bcast(s2[:, j % 2, :], 1, 2),
                                  ALU.mult).then_inc(bu_free, 1)
                dve.drain()
                dve.tensor_tensor(zin[:, 0, :], m1[:, 0, :], m2[:, 1, :], ALU.add)
                dve.tensor_tensor(zin[:, 1, :], m1[:, 1, :], m2[:, 0, :], ALU.subtract)
                dve.drain()
                for ri in range(2):
                    last = dve.tensor_tensor_scan(m1[:, ri, :], bcast(s5s[:, PK_MAG + j:PK_MAG + j + 1], 1, TOK)[:, :, 0],
                                                  zin[:, ri, :], 0.0, ALU.mult, ALU.add)
                last.then_inc(z_ready, 1)

            def s5_unit(n, q):
                if q in S5_SINE:
                    h = S5_SINE.index(q)
                    dve.wait_ge(sins_ready, n * 2 + h + 1)
                    dve.scalar_tensor_tensor(s2[:], s2[:], -2.0, psi[:, 2 * h:2 * h + 2, :], ALU.mult, ALU.mult).then_inc(
                        s2_ready, 1)
                    dve.drain()
                if q in S5_IN:
                    j = S5_IN.index(q)
                    dve.wait_ge(rot_done, n * 4 + j + 1)
                    pair_in(n, j)
                if q == S5_LEN - 1:
                    dve.wait_ge(y_done, n * 4 + 5)
                    y0, t0, t1 = zin[:, 0, :], zin[:, 1, :], m2[:, 0, :]
                    dve.scalar_tensor_tensor(y0, s5s[:, PK_U:PK_U + TOK], s5s[:, PK_D:PK_D + 1], ps[:, B_Y, 0:TOK],
                                             ALU.mult, ALU.add).then_inc(ys_ready, 1)
                    dve.drain()
                    chain(lambda: dve.tensor_tensor(t0, y0, y0, ALU.mult),
                          lambda: dve.tensor_scalar(t0, t0, 0.044715, 1.0, ALU.mult, ALU.add))
                    dve.tensor_tensor(t1, t0, y0, ALU.mult).then_inc(gelu_in, 1)
                    dve.wait_ge(gelu_sig, n + 1)
                    dve.tensor_tensor(y_s[:, bass.ds(n, 1), :].rearrange("p a t -> p (a t)"), y0, m2[:, 1, :],
                                      ALU.mult).then_inc(unit_done, 1)

            with dve.Fori(0, 2) as i:
                dve.tensor_copy(conv_s[:, 0:32].rearrange("p (j b c) -> p (j b) c", j=4, b=2),
                                vec[:, C_CW:C_CW + 64].rearrange("p (b c) -> p b c", c=8)[:, :, bass.ds(i * 4, 4)])
                dve.tensor_copy(conv_s[:, 32:40].rearrange("p (b c) -> p b c", b=2),
                                vec[:, C_CB:C_CB + 16].rearrange("p (b c) -> p b c", c=8)[:, :, bass.ds(i * 4, 4)])
                dve.tensor_copy(conv_s[:, 40:44], vec[:, bass.ds(i * 4 + C_MH, 4)])
                dve.tensor_copy(conv_s[:, 44:48].rearrange("p (t h) -> p t h", t=2), acols[:, 0:2, bass.ds(i * 2, 2)])
                dve.tensor_copy(small[:, 28:32].rearrange("p (h t) -> p t h", t=2), acols[:, 2:4, bass.ds(i * 2, 2)])
                dve.drain()

                def conv(b, j):
                    if j == 3:
                        dve.wait_ge(conv_in, i * 2 + b + 1)
                    d = 3 - j
                    for c in range(4):
                        tap = conv_s[:, j * 8 + b * 4 + c:j * 8 + b * 4 + c + 1]
                        if j == 3:
                            dve.tensor_scalar(acc[:, c, :], qk_raw[:, c, :], tap,
                                              conv_s[:, 32 + b * 4 + c:33 + b * 4 + c], ALU.mult, ALU.add)
                        else:
                            last = dve.scalar_tensor_tensor(acc[:, c, d:TOK], qk_raw[:, c, 0:TOK - d], tap,
                                                            acc[:, c, d:TOK], ALU.mult, ALU.add)
                    if j == 0:
                        last.then_inc(conv_acc, 1)
                    else:
                        dve.drain()

                def silu(b):
                    dve.wait_ge(conv_sig, i * 2 + b + 1)
                    dve.scalar_tensor_tensor((qT, kT)[b][:], acc[:], (1.0, 1.0 / 16.0)[b], qk_raw[:], ALU.mult,
                                             ALU.mult).then_inc(qk_ready, 1)

                def denominators():
                    dve.wait_ge(num_ready, i + 2)
                    dve.scalar_tensor_tensor(small[:, 34:38], ps[:, B_BU, 0:4], -1.0, small[:, 28:32], ALU.mult, ALU.max)
                    dve.drain()
                    dve.tensor_tensor(small[:, 34:38], small[:, 34:38], ps[:, B_BU, 0:4], ALU.max)
                    dve.drain()
                    dve.reciprocal(small[:, 38:42], small[:, 34:38]).then_inc(rec_ready, 1)

                def head_mean_squares():
                    dve.wait_ge(hss_ready, i + 1)
                    dve.tensor_scalar(small[:, 46:50], small[:, 42:46], 1.0 / 256.0, EPS, ALU.mult, ALU.add)
                    dve.drain()
                    dve.reciprocal(small[:, 50:54], small[:, 46:50]).then_inc(hinv_ready, 1)

                def head_norms():
                    dve.wait_ge(hroot_ready, i + 1)
                    newton(small[:, 46:50], small[:, 54:58], small[:, 58:62], small[:, 14:18])
                    dve.tensor_tensor(small[:, 58:62], small[:, 58:62], small[:, 38:42], ALU.mult)
                    dve.drain()
                    for m in range(4):
                        last = dve.tensor_scalar(hn[:, m % 2, m // 2 * TOK:(m // 2 + 1) * TOK],
                                                 ps[:, B_H[m // 2], m % 2 * TOK:(m % 2 + 1) * TOK],
                                                 small[:, 58 + m:59 + m], None, ALU.mult)
                    last.then_inc(hn_ready, 1)

                for pos in range(32):
                    split_lo(dve, PA.piece + pos, 4 * i)
                    s5_unit(i, pos)
                    if pos == 5:
                        for h in range(2):
                            rm = runmax_bc[:, bass.ds(i * 2 + h, 1), :].rearrange("p a t -> p (a t)")
                            rm1 = runmax_bc[:, bass.ds(i * 2 + h, 1), P:TOK].rearrange("p a t -> p (a t)")
                            dve.tensor_tensor(wexp[:, h, 0:TOK], masks[:, 0:TOK], rm, ALU.add)
                            dve.tensor_tensor(wexp[:, h, TOK:384], masks[:, TOK:384], rm1, ALU.add).then_inc(wexp_in, 1)
                    if pos in CONV_AT[0]:
                        conv(0, 3 - CONV_AT[0].index(pos))
                    if pos in CONV_AT[1]:
                        conv(1, 3 - CONV_AT[1].index(pos))
                    if pos in SILU_AT:
                        silu(SILU_AT.index(pos))
                    if pos in (24, 25):
                        h = pos - 24
                        dve.wait_ge(sT_ready, i * 2 + h + 1)
                        if h == 0:
                            dve.wait_ge(wexp_ready, i * 2 + 2)
                        dve.tensor_tensor(pT[:, h, :], ps[:, B_H[h], 0:384], wexp[:, h, :], ALU.mult).then_inc(pT_ready, 1)
                    if pos == 27:
                        denominators()
                    if pos == 28:
                        head_mean_squares()
                    if pos == 29:
                        head_norms()
                dve.wait_ge(hT_ready, i + 1)
                dve.wait_ge(o_ready, i + 1)
                for c in range(4):
                    dve.scalar_tensor_tensor(y_a[:, bass.ds(i * 4 + c, 1), :].rearrange("p a t -> p (a t)"),
                                             ps[:, B_H[c // 2], c % 2 * TOK:(c % 2 + 1) * TOK],
                                             conv_s[:, 40 + c:41 + c], o_sig[:, c, :], ALU.mult, ALU.mult)
                dve.drain()
            barrier(dve, 2)

            with dve.Fori(0, 2) as i:
                for u in range(2):
                    slot = i * 4 + 2 * u

                    def logits(a):
                        dve.wait_ge(scored, slot + a + 2)
                        dve.wait_ge(rel_loaded, i * 64 + (2 * u + a + 1) * 16)
                        dve.wait_ge(probT_made, slot + a + 1)
                        sc = ps[:, B_SC1:B_SC1 + 2, :].rearrange("p b n -> p (b n)")
                        dve.scalar_tensor_tensor(prob[:, 0:NG * TOK], sc[:, 0:NG * TOK], P ** -0.5,
                                                 rel[:].rearrange("p g t -> p (g t)"), ALU.mult, ALU.add)
                        dve.scalar_tensor_tensor(prob[:, NG * TOK:].rearrange("p (g t) -> p g t", g=NG),
                                                 ps[:, B_SC0, 0:384].rearrange("p (g t) -> p g t", g=NG), P ** -0.5,
                                                 rel[:, :, P:TOK], ALU.mult, ALU.add)
                        dve.drain()
                        dve.tensor_reduce(small[:, 22:23], prob[:, 0:NG * TOK], AX_X, ALU.max, negate=True)
                        dve.tensor_reduce(small[:, 23:24], prob[:, NG * TOK:], AX_X, ALU.max, negate=True).then_inc(
                            logits_ready, 1)

                    def weights(a):
                        dve.wait_ge(exps_ready, slot + a + 1)
                        dve.reciprocal(small[:, 26:28], small[:, 24:26])
                        dve.drain()
                        dve.tensor_scalar(prob[:, 0:NG * TOK], prob[:, 0:NG * TOK], small[:, 26:27], None, ALU.mult)
                        dve.tensor_scalar(prob[:, NG * TOK:], prob[:, NG * TOK:], small[:, 27:28], None, ALU.mult).then_inc(
                            prob_ready, 1)

                    def head_copy(a):
                        dve.wait_ge(att_out, slot + a + 2)
                        dve.tensor_copy(y_b[:, bass.ds(i * 4 + (2 * u + a), 1), :].rearrange("p a t -> p (a t)"),
                                        ps[:, B_PV, 0:TOK]).then_inc(att_copied, 1)
                    for pos in range(36):
                        split_lo(dve, PB.piece + 36 * u + pos, 9 * i)
                        at_b = 36 * u + pos
                        s5_unit(i * 3 + (2 + at_b // S5_LEN), at_b % S5_LEN)
                        if pos in (25, 31):
                            logits((25, 31).index(pos))
                        if pos in (26, 32):
                            weights((26, 32).index(pos))
                    head_copy(0)
                    head_copy(1)
            barrier(dve, 3)

            for q in range(4):
                dve.wait_ge(z_split_a, q + 1)
                dve.tensor_tensor(z_lo[:, 2 * q:2 * q + 2], y_s[:, 2 * q:2 * q + 2], f(z_hi[:, 2 * q:2 * q + 2]),
                                  ALU.subtract).then_inc(z_split_v, 1)
            for b, y in enumerate((y_a, y_b)):
                dve.wait_ge(y_split_a, b + 1)
                dve.tensor_tensor(y_lo[:, b], y[:], f(y_hi[:, b]), ALU.subtract).then_inc(y_split_v, 1)
            with dve.Fori(0, 2) as i:
                for s in range(8):
                    split_lo(dve, PC.piece + s, i)
                dve.wait_ge(glu_in, i * 2 + 2)
                dve.tensor_tensor(y_s[:, bass.ds(i * 4, 4), :], z_lin[:], z_sig[:], ALU.mult).then_inc(glu_out, 1)
            dve.wait_ge(y_split_a, 3)
            dve.tensor_tensor(y_lo[:, 2], y_s[:], f(y_hi[:, 2]), ALU.subtract).then_inc(y_split_v, 1)

            with dve.Fori(0, 2) as i:
                for u in range(2):
                    for b in range(3):
                        s, blk = PD.piece + 36 * u + 12 * b, PD.block + 6 * u + 2 * b
                        for q in range(12):
                            split_lo(dve, s + q, 9 * i)
                        block_done(dve, s + 8, 4, 9 * i)
                        dve.wait_ge(gsig_ready, i * 6 + 3 * u + b + 1)
                        src = ps[:, 2 * ((blk + 1) % 2):2 * ((blk + 1) % 2) + 2, :].rearrange("p b (c t) -> p (b c) t", t=TOK)
                        dve.tensor_tensor((mix_t if b else mix)[:], src, gate_sig[:, b], ALU.mult).then_inc(
                            psum_free[(blk + 1) % 2], 1)
                        dve.drain()
                        if b:
                            add_op = dve.tensor_tensor(mix[:], mix[:], mix_t[:], ALU.add)
                            if b == 2:
                                add_op.then_inc(mix_ready, 1)
                            dve.drain()
                    dve.wait_ge(mixhi_ready, i * 2 + u + 1)
                    dst = bass.ds(i * 8 + 4 * u, 4)
                    dve.tensor_tensor(mix_lo[:, dst, :], mix[:], f(mix_hi[:, dst, :]), ALU.subtract).then_inc(mix_done, 1)
                    dve.drain()

            def add_to_x1(s, n, o8, blk, c0):
                block_done(dve, s, n, o8)
                dst = x1[:, :, bass.ds(c0, 512)]
                dve.tensor_tensor(dst, ps[:, 2 * (blk % 2):2 * (blk % 2) + 2, :], dst, ALU.add).then_inc(
                    psum_free[blk % 2], 1)
                dve.drain()
                dve.sem_inc(x1_done, 1)

            with dve.Fori(0, 2) as i:
                for u in range(2):
                    for s in range(8):
                        split_lo(dve, PW.piece + 8 * u + s, 2 * i)
                    dve.wait_ge(x1_loaded, 16)
                    add_to_x1(PW.piece + 8 * u, 8, 2 * i, PW.block + u, i * 1024 + u * 512)
            inverse_rms(2, D, x1, sq_junk)
            diagonals()
            features_lo(8, C_N2)
            with dve.Fori(0, 2) as h:
                with dve.Fori(0, 4) as i:
                    for u in range(2):
                        for s in range(8):
                            split_lo(dve, PF.piece + 8 * u + s, h * 16 + i * 2)
                        dve.wait_ge(relu_ready, h * 8 + i * 2 + u + 1)
                        dve.tensor_tensor(relu2[:], relu[:], relu[:], ALU.mult)
                        dve.drain()
                        dve.wait_ge(hhi_ready, h * 8 + i * 2 + u + 1)
                        dst = bass.ds(i * 8 + 4 * u, 4)
                        dve.tensor_tensor(h_lo[:, dst, :], relu2[:].rearrange("p (c t) -> p c t", t=TOK),
                                          f(h_hi[:, dst, :]), ALU.subtract).then_inc(h_ready, 1)
                with dve.Fori(0, 2) as i:
                    for u in range(2):
                        for s in range(12 if u else 16):
                            split_lo(dve, PF.piece + 64 + 16 * u + s, h * 16 + i * 4)
                        if u:
                            split_unless_last(split_lo, dve, h, i)
                        add_to_x1(PF.piece + 64 + 16 * u, 16, h * 16 + i * 4, PF.block + 8 + u, i * 1024 + u * 512)
            inverse_rms(3, D, x1, sq_junk)
            dve.wait_ge(fg_loaded, 16)
            for t in range(TT):
                dve.scalar_tensor_tensor(x1[:, t, :], x1[:, t, :], small[:, 8 + t:9 + t], fg_bc[:], ALU.mult,
                                         ALU.mult).then_inc(out_ready, 1)

        @block.gpsimd
        def _(gp):
            gp.wait_ge(c_loaded, C_LOADS)
            gp.wait_ge(s5_loaded, 64)
            gp.wait_ge(xlo_ready, 8)
            for ri in range(2):
                for half in range(2):
                    gp.tensor_scalar(c_pad[:, ri, :, ST * half:ST * half + ST], c_raw[:, ri], par[:, 2 + half:3 + half],
                                     (1.0, -1.0)[ri], ALU.mult, ALU.mult)
            gp.drain()
            gp.sem_inc(pad_ready, 1)
            gp.wait_ge(cols_copied, 2)
            gp.dma_start(rel_rows, relval[:]).then_inc(rel_stored, 16)
            gp.wait_ge(rel_stored, 16)
            for g in range(NG):
                gp.dma_start(rel_tiles[:, :, g, :],
                             bass.AP(rel_rows.tensor, g * AH * 384 + P - 1, [[384, AH], [-1, P], [1, TOK]])).then_inc(
                    rel_spread, 16)

            def pp(n):
                return s5p[:, n, :]

            def mul(o, a, b):
                gp.tensor_tensor(pp(o), pp(a), pp(b), ALU.mult)
                gp.drain()

            def add(o, a, b, op=ALU.add):
                gp.tensor_tensor(pp(o), pp(a), pp(b), op)
                gp.drain()

            def scaled(o, a, c):
                gp.tensor_scalar(pp(o), pp(a), c, None, ALU.mult)
                gp.drain()

            def whole(o, a, big=ROUND):
                gp.tensor_scalar(pp(o), pp(a), big, big, ALU.add, ALU.subtract)
                gp.drain()
            inv1, inv2, inv3 = inv_two_pi()
            gp.wait_ge(par_a, 1)
            mul(4, 0, 3)
            mul(6, 1, 3)
            gp.sem_inc(par_v, 1)
            gp.wait_ge(par_a, 3)
            add(8, 6, 7, ALU.subtract)
            scaled(9, 7, inv1)
            whole(10, 9)
            add(9, 9, 10, ALU.subtract)
            scaled(11, 7, inv2)
            whole(10, 11)
            add(11, 11, 10, ALU.subtract)
            scaled(12, 8, inv1)
            whole(10, 12)
            add(12, 12, 10, ALU.subtract)
            scaled(13, 8, inv2)
            scaled(14, 7, inv3)
            add(13, 13, 14)
            add(14, 9, 11)
            add(14, 14, 12)
            add(14, 14, 13)
            whole(10, 14)
            add(9, 9, 10, ALU.subtract)
            add(14, 14, 10, ALU.subtract)
            whole(17, 14, GRID16)
            add(15, 9, 17, ALU.subtract)
            add(15, 15, 11)
            add(15, 15, 12)
            add(15, 15, 13)
            scaled(18, 15, -1.0)
            add(19, 17, 15)
            gp.sem_inc(par_v, 1)
            gp.wait_ge(par_a, 5)
            mul(24, 20, 22)
            scaled(24, 24, 2.0)
            mul(25, 5, 23)
            gp.tensor_scalar(pp(25), pp(25), -1.0, None, ALU.add)
            gp.drain()
            mul(26, 5, 24)
            mul(21, 25, 0)
            mul(22, 26, 1)
            add(21, 21, 22)
            gp.wait_ge(rden_ready, 1)
            mul(27, 21, 16)
            mul(21, 26, 0)
            mul(22, 25, 1)
            add(21, 21, 22, ALU.subtract)
            mul(28, 21, 16)
            bt = [bb_t[:, n] for n in range(2)]
            fre, fim = bcast(pp(27), 2, 16), bcast(pp(28), 2, 16)
            for ri in range(2):
                gp.tensor_tensor(bt[0], b_raw[:, ri], fre, ALU.mult)
                gp.tensor_tensor(bt[1], b_raw[:, 1 - ri], fim, ALU.mult)
                gp.drain()
                gp.tensor_tensor(bt[0], bt[0], bt[1], ALU.add if ri else ALU.subtract)
                gp.drain()
                for half in range(2):
                    gp.tensor_scalar(b_pad[:, ri, :, 16 * half:16 * half + 16], bt[0], par[:, half:half + 1], None, ALU.mult)
                gp.drain()
            gp.sem_inc(pad_ready, 1)
            for dst, n in ((PK_FH, 17), (PK_FL, 18), (PK_MAG, 5)):
                gp.tensor_copy(pack[:, :, dst:dst + 4], pp(n).rearrange("p (t j) -> p t j", j=4))
            gp.tensor_copy(pack[:, :, PK_D:PK_D + 1], vec[:, C_DS:C_DS + 8].rearrange("p (t a) -> p t a", a=1))
            gp.memset(pack[:, :, PK_D + 1:PKW], 0.0)
            barrier(gp, 1)

            def angles(n, h):
                ph = psi[:, 2 * h:2 * h + 2, :]
                gp.tensor_tensor(ph, bcast(iota_t, 1, 2), bcast(s5s[:, PK_FH + 2 * h:PK_FH + 2 * h + 2], 2, TOK), ALU.mult)
                gp.drain()
                gp.tensor_scalar(kk2[:], ph, ROUND, ROUND, ALU.add, ALU.subtract)
                gp.drain()
                gp.tensor_tensor(ph, kk2[:], ph, ALU.subtract)
                gp.drain()
                gp.tensor_tensor(kk2[:], bcast(iota_t, 1, 2), bcast(s5s[:, PK_FL + 2 * h:PK_FL + 2 * h + 2], 2, TOK),
                                 ALU.mult)
                gp.drain()
                gp.tensor_tensor(ph, ph, kk2[:], ALU.add).then_inc(psi_ready, 1)
                gp.drain()

            def rotate_back(n, j):
                gp.wait_ge(z_ready, n * 4 + j + 1)
                gp.wait_ge(y_done, n * 4 + j + 1)
                gp.tensor_tensor(n1[:], m1[:], bcast(c2[:, j % 2, :], 1, 2), ALU.mult)
                gp.tensor_tensor(n2[:], m1[:], bcast(s2[:, j % 2, :], 1, 2), ALU.mult)
                gp.drain()
                gp.sem_inc(rot_done, 1)
                gp.tensor_tensor(n1[:, 0, :], n1[:, 0, :], n2[:, 1, :], ALU.subtract)
                gp.tensor_tensor(n1[:, 1, :], n1[:, 1, :], n2[:, 0, :], ALU.add)
                gp.drain()
                gp.sem_inc(xr_ready, 1)

            def s5_unit(n):
                gp.wait_ge(s5_staged, n + 1)
                gp.wait_ge(s2_ready, n * 2 + 1)
                for h in range(2):
                    angles(n, h)
                for j in range(4):
                    rotate_back(n, j)

            with gp.Fori(0, 2) as i:
                s5_unit(i)
            gp.wait_ge(rel_spread, 16 * NG)
            barrier(gp, 2)
            with gp.Fori(0, 2) as i:
                for unit in range(3):
                    s5_unit(i * 3 + (2 + unit))
            barrier(gp, 3)
            gp.wait_ge(mix_done, 4)
            gp.dma_start(x1[:], x[0].rearrange("(t p) n -> p t n", p=P)).then_inc(x1_loaded, 16)
            gp.dma_start(fg_bc[:], bass.AP(final_g.tensor, 0, [[0, P], [1, D]])).then_inc(fg_loaded, 16)


def t5_bucket(n):
    import numpy as np
    half = 16
    nf = np.maximum(n, half).astype(np.float32)
    large = half + (np.log(nf / np.float32(half)) / np.float32(math.log(2048 / half)) * np.float32(half)).astype(np.int32)
    return np.where(n < half, n, np.minimum(large, 31))


def shape_constants():
    import numpy as np
    p = np.arange(P)
    consts = np.zeros((P, 648), np.float32)
    causal = np.where(p[:, None] <= p[None, :], 0.0, NEG)
    consts[:, 0:P] = causal
    consts[:, 2 * P:3 * P] = causal
    consts[:, 384:640] = np.arange(TOK)
    consts[:, 640] = p < ST
    consts[:, 641] = p >= ST
    consts[:, 642] = p // 16 % 2 == 0
    consts[:, 643] = p // 16 % 2 == 1
    consts[:, 644] = 1.0
    consts[:, 645] = math.pi / 2
    dist = 255 - np.arange(384)
    onehot = (t5_bucket(np.maximum(dist, 0))[None, :] == np.arange(32)[:, None]).astype(np.float32)
    seen = np.stack([(dist >= 0) & (dist <= 128), (dist >= 0) & (dist % 4 == 0), (dist >= 0) & (dist % 16 == 0)])
    relmask = np.repeat(np.where(seen, 0.0, NEG).astype(np.float32), AH, axis=0)
    return {"ident_c": np.eye(P, dtype=np.float32), "consts_c": consts, "onehot_c": onehot, "relmask_c": relmask}


_INS = ['x', 'norm1_g', 'w_in', 'conv_w', 'conv_b', 'b_igate', 'b_fgate', 'mh_norm_g', 'rel_bias', 'lam_re', 'lam_im',
        'log_dt', 'b_re', 'b_im', 'c_re', 'c_im', 'd_skip', 'w_glu', 'w_br_a', 'w_br_b', 'w_br_c', 'w_out', 'norm2_g',
        'w_ff1', 'w_ff2', 'final_g']


def kernel(**inputs):
    import numpy as _np
    import concourse.bacc as _bacc
    from concourse import mybir as _mybir
    from concourse.bass_utils import run_bass_kernel_spmd as _run

    nc = _bacc.Bacc("TRN2", target_bir_lowering=False, num_devices=1)
    arrays, args = {}, []
    values = {name: _np.ascontiguousarray(inputs[name]) for name in _INS}
    values.update(shape_constants())
    for name, a in values.items():
        arrays[f"in_{name}_dram"] = a
        args.append(nc.dram_tensor(f"in_{name}_dram", a.shape, _mybir.dt.from_np(a.dtype), kind="ExternalInput").ap())
    args.append(nc.dram_tensor("out_0_dram", (1, TOK, D), _mybir.dt.float32, kind="ExternalOutput").ap())
    trunk(nc, *args)
    r = _run(nc, [arrays], core_ids=[0])
    return r.results[0]["out_0_dram"]
```

```python
import math
from contextlib import ExitStack

import concourse.bass as bass
from concourse import mybir

F32 = mybir.dt.float32
F32R = mybir.dt.float32r
ACT = mybir.ActivationFunctionType
ALU = mybir.AluOpType
AX_X = mybir.AxisListType.X

P = 128
TOK = 256
TT = TOK // P
D = 2048
KD = D // P
EPS = 1e-6
MH, MW = 4, 1024
NG, AH = 3, 8
GW = 64
ST = 64
Q_M, K_M, V_M, O_M, IF_M = 0, 1024, 2048, 3072, 4096
Q_A, K_A, V_A = 4104, 4104 + 3072, 4104 + 6144
U_S, GATE = 13320, 14344

LOADW, PIECEW, AHEAD = 2048, 1024, 4
C_LOADS, G_LOADS = 16 * 5, 16 * 5
SLOTS = 4
C_N1, C_N2, C_CW, C_CB, C_MH, C_DS = 0, 16, 32, 96, 112, 120
PK_B, PK_C, PK_U, PK_MAG, PK_D, PKW = 0, 256, 512, 768, 772, 776
S5_LEN, S5_IN, S5_OUT, S5_SINE = 24, (3, 8, 14, 18), (7, 12, 18, 22), (1, 12)
CONV_AT, SILU_AT = ((9, 10, 11, 12), (16, 17, 19, 20)), (13, 22)
SCORE_AT, LOGIT_AT, EXP_AT, WEIGHT_AT, TRANS_AT, PROBT_AT = (24, 30), (25, 31), (26, 32), (26, 32), 28, 29
NEG = -1.0e30
ROUND = 12582912.0
GRID16 = 192.0


def inv_two_pi():
    rest, parts = 1.0 / (2.0 * math.pi), []
    for _ in range(3):
        m, e = math.frexp(rest)
        part = math.ldexp(math.floor(m * 4096.0), e - 12)
        parts.append(part)
        rest -= part
    return parts


class Phase:
    def __init__(self, load, block):
        self.load, self.piece, self.block = load, 2 * load, block


LOADS_U, BLOCKS_U = 8, 2
LOADS_A, BLOCKS_A = 16, 4
LOADS_B, BLOCKS_B = 36, 18
LOADS_C, BLOCKS_C = 4, 2
LOADS_D, BLOCKS_D = 36, 12
LOADS_W, BLOCKS_W = 8, 2
LOADS_F1, BLOCKS_F1 = 8, 2
LOADS_F2, BLOCKS_F2 = 16, 2
HALF_LOADS, HALF_BLOCKS = 4 * LOADS_F1 + 2 * LOADS_F2, 4 * BLOCKS_F1 + 2 * BLOCKS_F2
PI = Phase(0, 0)
PU = Phase(PI.load + 1, PI.block + 1)
PA = Phase(PU.load + LOADS_U, PU.block + BLOCKS_U)
PB = Phase(PA.load + 2 * LOADS_A, PA.block + 2 * BLOCKS_A)
PC = Phase(PB.load + 2 * LOADS_B, PB.block + 2 * BLOCKS_B)
PD = Phase(PC.load + 2 * LOADS_C, PC.block + 2 * BLOCKS_C)
PW = Phase(PD.load + 2 * LOADS_D, PD.block + 2 * BLOCKS_D)
PF = Phase(PW.load + 2 * LOADS_W, PW.block + 2 * BLOCKS_W)
TOTAL_LOADS = PF.load + 2 * HALF_LOADS
TOTAL_PIECES = 2 * TOTAL_LOADS


def trunk(nc, x, norm1_g, w_in, conv_w, conv_b, b_igate, b_fgate, mh_norm_g, rel_bias, lam_re, lam_im,
          log_dt, b_re, b_im, c_re, c_im, d_skip, w_glu, w_br_a, w_br_b, w_br_c, w_out, norm2_g,
          w_ff1, w_ff2, final_g, ident_c, consts_c, onehot_c, relmask_c, out):
    ctx = ExitStack()
    with ctx:
        def sem(name):
            return ctx.enter_context(nc.semaphore(name))

        top = [(nc.sbuf_base + 31) // 32 * 32]

        def at(name, shape, off, dt=F32):
            return nc.alloc_sbuf_tensor_at(name, shape, dt, offset=off)

        def size(shape):
            n = 4
            for s in shape[1:]:
                n *= s
            return (n + 31) // 32 * 32

        def take(name, shape, dt=F32):
            t = at(name, shape, top[0], dt)
            top[0] += size(shape)
            return t

        def region(start, items):
            got = []
            for name, shape, dt in items:
                got.append(at(name, shape, start, dt))
                start += size(shape)
            assert start <= nc.sbuf_usable_end, (items[-1][0], start, nc.sbuf_usable_end)
            return got

        raw = take("raw", [P, SLOTS, LOADW])
        w_hi = take("w_hi", [P, SLOTS, PIECEW], F32R)
        w_lo = take("w_lo", [P, SLOTS, PIECEW], F32R)
        x_hi = take("x_hi", [P, KD, TOK], F32R)
        x_lo = take("x_lo", [P, KD, TOK], F32R)
        ident = take("ident", [P, P])
        vec = take("vec_cols", [P, P])
        consts = take("consts", [P, 384 + 256 + 8])
        masks = consts[:, 0:384]
        iota_t = consts[:, 384:640]
        par = consts[:, 640:648]
        half_pi, ones, minus_half, eps_256 = par[:, 5:6], par[:, 4:5], par[:, 6:7], par[:, 7:8]
        runmax_bc = take("runmax_bc", [P, MH, TOK])
        acols = take("acols", [P, 4, MH])
        small = take("small", [P, 64])
        diag = take("diag", [P, TT, P])
        gate_bias = take("gate_bias", [8, 1])
        ldt = take("log_dt_pairs", [96, 2])
        theta = take("theta", [P, GW // 8 + 1, 8])
        conv_s = take("conv_s", [P, 48])
        y_base = top[0]
        y_a = take("y_a", [P, 8, TOK])
        y_b = take("y_b", [P, 8, TOK])
        y_s = take("y_s", [P, 8, TOK])
        r0 = top[0]
        pack, s5s, psi, kk2, c2, s2, m1, m2, zin, n1, n2 = region(r0, [
            ("pack", [P, 8, PKW], F32), ("s5_now", [P, PKW], F32), ("psi", [P, 4, TOK], F32),
            ("kk2", [P, 2, TOK], F32), ("cos2", [P, 2, TOK], F32), ("sin2", [P, 2, TOK], F32),
            ("m1", [P, 2, TOK], F32), ("m2", [P, 2, TOK], F32), ("zin", [P, 2, TOK], F32),
            ("n1", [P, 2, TOK], F32), ("n2", [P, 2, TOK], F32)])
        r_s5now = r0 + size([P, 8, PKW])
        r1 = r_s5now + size([P, PKW]) + 4096 + 8 * 2048
        (xs_junk,) = region(r0, [("xs_junk", [P, TT, D], F32)])
        (s5p,) = region(r_s5now, [("s5p", [P, 30, 32], F32)])
        (b_raw, c_raw, bb_t) = region(r_s5now + 3840, [
            ("b_raw", [P, 2, 32, 16], F32), ("c_raw", [P, 2, 8, 64], F32), ("bb_t", [P, 2, 32, 16], F32)])
        (xs,) = region(r1, [("xs", [P, TT, D], F32)])
        b_pad, c_pad = region(r1 + 12288, [("b_pad", [P, 2, 32, 32], F32), ("c_pad", [P, 2, 8, P], F32)])
        (vrows, srows, table, onehot, relmask, relval) = region(r_s5now + 3840 + 12288, [
            ("vrows", [P, P], F32), ("srows", [96, P], F32), ("table", [32, 24], F32),
            ("onehot", [32, 384], F32), ("relmask", [24, 384], F32), ("relval", [24, 384], F32)])
        (gates8, gtmp, fcum, gaf, gr, neg_sel, neg_bc) = region(y_base, [
            ("gates8", [8, TOK], F32), ("gtmp", [8, 4, TOK], F32), ("fcum", [8, TOK], F32),
            ("gaf", [MH, 2, TOK], F32), ("gr", [MH, 2, TOK], F32), ("neg_sel", [8, MH], F32),
            ("neg_bc", [MH, MH, P], F32)])
        (qk_raw, acc, qT, kT, v_m, o_sig, wexp, pT) = region(r1, [
            ("qk_raw", [P, 4, TOK], F32), ("acc", [P, 4, TOK], F32), ("qT", [P, 4, TOK], F32),
            ("kT", [P, 4, TOK], F32), ("v_m", [P, TT, 2, TOK], F32), ("o_sig", [P, 4, TOK], F32),
            ("wexp", [P, 2, 384], F32), ("pT", [P, 2, 384], F32)])
        (hn,) = region(r1 + 4096, [("hn", [P, TT, 2 * TOK], F32)])
        (aq, ak, av, rel, prob, probT) = region(r1, [
            ("aq", [P, 6, TOK], F32), ("ak", [P, 6, TOK], F32), ("av", [P, TT, NG, 2 * P], F32),
            ("rel", [P, NG, TOK], F32), ("prob", [P, NG * TOK + NG * P], F32), ("probT", [P, NG, 384], F32)])
        (mix_hi, mix_lo) = region(y_base, [("mix_hi", [P, KD, TOK], F32R), ("mix_lo", [P, KD, TOK], F32R)])
        r2 = y_base + 32768
        (y_hi, y_lo) = region(r2, [("y_hi", [P, 3, 8, TOK], F32R), ("y_lo", [P, 3, 8, TOK], F32R)])
        r3 = r2 + 49152
        (z_hi, z_lo) = region(r3, [("z_hi", [P, 8, TOK], F32R), ("z_lo", [P, 8, TOK], F32R)])
        (z_lin, z_sig) = region(y_base + 24576, [("z_lin", [P, 4, TOK], F32), ("z_sig", [P, 4, TOK], F32)])
        (gate_sig, mix, mix_t) = region(r3, [
            ("gate_sig", [P, NG, 4, TOK], F32), ("mix", [P, 4, TOK], F32), ("mix_t", [P, 4, TOK], F32)])
        (x1,) = region(r3, [("x1", [P, TT, D], F32)])
        (h_hi, h_lo) = region(y_base, [("h_hi", [P, 32, TOK], F32R), ("h_lo", [P, 32, TOK], F32R)])
        (relu, relu2) = region(y_base + 65536, [("relu", [P, PIECEW], F32), ("relu2", [P, PIECEW], F32)])
        (sq_junk,) = region(y_base, [("sq_junk", [P, TT, D], F32)])
        (fg_bc,) = region(y_base + 65536 + 8192, [("fg_bc", [P, D], F32)])
        assert y_base + 65536 + 16384 <= r3

        ps = ctx.enter_context(nc.psum_tensor("ps", [P, 8, 512], F32))
        SPARE = 4
        B_SC1, B_SC0, B_PV = 2, 4, 5
        B_H = (4, 5)
        B_Y, B_BU = 6, 7

        rel_rows = nc.dram_tensor("rel_rows", (24, 384), F32).ap()
        rel_tiles = nc.dram_tensor("rel_tiles", (AH, P, NG, TOK), F32).ap()

        raw_loaded = [sem(f"raw_loaded{i}") for i in range(SLOTS)]
        hi_ready, lo_ready = sem("hi_ready"), sem("lo_ready")
        piece_done = sem("piece_done")
        psum_free = [sem("psum_free0"), sem("psum_free1")]
        x_loaded, vrows_loaded, c_loaded = [sem("x_loaded0"), sem("x_loaded1")], sem("vrows_loaded"), sem("c_loaded")
        g_loaded, s5_loaded, srows_ready = sem("g_loaded"), sem("s5_loaded"), sem("srows_ready")
        rel_stored, rel_spread = sem("rel_stored"), sem("rel_spread")
        sumsq_ready, sumsq_v_ready, inv_ready = sem("sumsq_ready"), sem("sumsq_v_ready"), sem("inv_ready")
        diag_ready, trans_ready = sem("diag_ready"), sem("trans_ready")
        xhi_ready, xlo_ready = sem("xhi_ready"), sem("xlo_ready")
        cols_ready, cols_copied = sem("cols_ready"), sem("cols_copied")
        par_v, par_a, rden_ready = sem("par_v"), sem("par_a"), sem("rden_ready")
        pad_ready, btr_ready, pack_ready = sem("pad_ready"), sem("btr_ready"), sem("pack_ready")
        g8_a, g8_v, g8_p = sem("g8_a"), sem("g8_v"), sem("g8_p")
        phase_done = sem("phase_done")
        conv_in, conv_acc, conv_sig, qk_ready = sem("conv_in"), sem("conv_acc"), sem("conv_sig"), sem("qk_ready")
        v_ready, o_ready, wexp_in, wexp_ready = sem("v_ready"), sem("o_ready"), sem("wexp_in"), sem("wexp_ready")
        sT_ready, pT_ready, num_ready, rec_ready = sem("sT_ready"), sem("pT_ready"), sem("num_ready"), sem("rec_ready")
        hss_ready, hinv_ready, hn_ready, hT_ready = sem("hss_ready"), sem("hinv_ready"), sem("hn_ready"), sem("hT_ready")
        s5_staged, psi_ready, sins_ready, s2_ready = sem("s5_staged"), sem("psi_ready"), sem("sins_ready"), sem("s2_ready")
        bu_ready, bu_free, z_ready, rot_done, xr_ready, y_done = (
            sem("bu_ready"), sem("bu_free"), sem("z_ready"), sem("rot_done"), sem("xr_ready"), sem("y_done"))
        ys_ready, gelu_in, gelu_sig, unit_done = sem("ys_ready"), sem("gelu_in"), sem("gelu_sig"), sem("unit_done")
        aq_ready, ak_ready, av_ready, rel_loaded = sem("aq_ready"), sem("ak_ready"), sem("av_ready"), sem("rel_loaded")
        scored, logits_ready, exps_ready, prob_ready = sem("scored"), sem("logits_ready"), sem("exps_ready"), sem("prob_ready")
        probT_made, probT_ready, att_out, att_copied = sem("probT_made"), sem("probT_ready"), sem("att_out"), sem("att_copied")
        z_split_a, z_split_v = sem("z_split_a"), sem("z_split_v")
        glu_in, glu_out, y_split_a, y_split_v = sem("glu_in"), sem("glu_out"), sem("y_split_a"), sem("y_split_v")
        gsig_ready, mix_ready, mixhi_ready, mix_done = sem("gsig_ready"), sem("mix_ready"), sem("mixhi_ready"), sem("mix_done")
        x1_loaded, x1_done = sem("x1_loaded"), sem("x1_done")
        relu_ready, hhi_ready, h_ready = sem("relu_ready"), sem("hhi_ready"), sem("h_ready")
        fg_loaded, out_ready, stored = sem("fg_loaded"), sem("out_ready"), sem("stored")

        def bcast(ap, pos, n):
            dims = [list(d) for d in ap.ap]
            return bass.AP(ap.tensor, ap.offset, dims[:pos] + [[0, n]] + dims[pos:])

        def f(ap):
            return ap.bitcast(F32)

        def end_of_phase(eng, n, wait=False):
            eng.drain()
            eng.sem_inc(phase_done, 1)
            if wait:
                eng.wait_ge(phase_done, n * 4)

        def split_hi(act, s, o8):
            s += AHEAD
            if not isinstance(o8, int) or s + 8 * o8 < TOTAL_PIECES:
                load = s // 2
                act.wait_ge(raw_loaded[load % SLOTS], 16 * (load // SLOTS + 1) + 16 * o8)
                if s >= SLOTS:
                    act.wait_ge(piece_done, s - SLOTS + 1 + 8 * o8)
                act.activation(w_hi[:, s % SLOTS, :], raw[:, load % SLOTS, s % 2 * PIECEW:(s % 2 + 1) * PIECEW],
                               ACT.Copy).then_inc(hi_ready, 1)

        def split_lo(dve, s, o8):
            s += AHEAD
            if not isinstance(o8, int) or s + 8 * o8 < TOTAL_PIECES:
                dve.wait_ge(hi_ready, s + 1 + 8 * o8)
                load = s // 2
                dve.tensor_tensor(w_lo[:, s % SLOTS, :], raw[:, load % SLOTS, s % 2 * PIECEW:(s % 2 + 1) * PIECEW],
                                  f(w_hi[:, s % SLOTS, :]), ALU.subtract).then_inc(lo_ready, 1)

        def split_unless_last(do, eng, h, i):
            with eng.If(h * 2 + i < 3):
                for s in range(32 - AHEAD, 32):
                    do(eng, PF.piece + 64 + s, h * 16 + i * 4)

        FIRST_SPLITS = {3: 2, 7: 3}

        def block_done(eng, s, n, o8):
            eng.wait_ge(piece_done, s + n + 8 * o8)

        def gemm(pe, s, o8, block, o2, cols, tokens, hi, lo, npieces=8, narrow=False, after=None, xs_wait=None):
            kts = PIECEW // cols
            free = block // 2
            if free > 0:
                pe.wait_ge(psum_free[block % 2], free + o2)
            bank0 = block % 2 if narrow else 2 * (block % 2)
            for q in range(npieces):
                pe.wait_ge(lo_ready, s + q + 1 + 8 * o8)
                if xs_wait is not None:
                    xs_wait(q)
                slot = (s + q) % SLOTS
                whi = w_hi[:, slot, :].rearrange("p (k n) -> p k n", k=kts)
                wlo = w_lo[:, slot, :].rearrange("p (k n) -> p k n", k=kts)
                for k in range(kts):
                    kk = q * kts + k
                    first, last = kk == 0, (q == npieces - 1 and k == kts - 1)
                    if tokens:
                        for t in range(TT):
                            o = ps[:, bank0, t * cols:(t + 1) * cols] if narrow else ps[:, bank0 + t, 0:cols]
                            tk = slice(t * P, (t + 1) * P)
                            st = first and (t == 0 or not narrow)
                            pe.matmul(o, hi[:, kk, tk], whi[:, k, :], start=st, stop=False, skip_group_check=True)
                            pe.matmul(o, hi[:, kk, tk], wlo[:, k, :], start=False, stop=False, skip_group_check=True)
                            mm = pe.matmul(o, lo[:, kk, tk], whi[:, k, :], start=False, stop=last, skip_group_check=True)
                    else:
                        for c in range(cols // P):
                            o = ps[:, bank0 + c // 2, c % 2 * TOK:(c % 2 + 1) * TOK]
                            cs = slice(c * P, (c + 1) * P)
                            st = first and c % 2 == 0
                            pe.matmul(o, whi[:, k, cs], hi[:, kk, :], start=st, stop=False, skip_group_check=True)
                            pe.matmul(o, whi[:, k, cs], lo[:, kk, :], start=False, stop=False, skip_group_check=True)
                            mm = pe.matmul(o, wlo[:, k, cs], hi[:, kk, :], start=False, stop=last, skip_group_check=True)
                mm.then_inc(piece_done, 1)
                if after is not None:
                    after(q)

        block = ctx.enter_context(nc.Block())

        @block.sync
        def _(sp):
            def load(s, o4, src):
                if s >= SLOTS:
                    sp.wait_ge(lo_ready, 2 * (s - SLOTS) + 2 + 8 * o4)
                sp.dma_start(raw[:, s % SLOTS, :].rearrange("p (k n) -> p k n", k=src.shape[1]),
                             src).then_inc(raw_loaded[s % SLOTS], 16)

            w_in_k = w_in[0].rearrange("(k p) n -> p k n", p=P)

            def cols(w, k0, kt, c0, n, turn=0):
                return w[:, k0:k0 + kt, c0:][:, :, bass.ds(turn, n)]

            for t in range(TT):
                sp.dma_start(xs[:, t, :], x[0, t * P:(t + 1) * P, :]).then_inc(x_loaded[t], 16)
            sp.dma_start(vrows[C_N1:C_N1 + 16, :], norm1_g.rearrange("a (k p) -> (a k) p", p=P)).then_inc(vrows_loaded, 16)
            sp.dma_start(vrows[C_N2:C_N2 + 16, :], norm2_g.rearrange("a (k p) -> (a k) p", p=P)).then_inc(vrows_loaded, 16)
            sp.dma_start(vrows[C_CW:C_CW + 64, :], conv_w[0].rearrange("j (k p) -> (j k) p", p=P)).then_inc(vrows_loaded, 16)
            sp.dma_start(vrows[C_CB:C_CB + 16, :], conv_b.rearrange("a (k p) -> (a k) p", p=P)).then_inc(vrows_loaded, 16)
            sp.dma_start(vrows[C_MH:C_MH + 8, :], mh_norm_g.rearrange("a (k p) -> (a k) p", p=P)).then_inc(vrows_loaded, 16)
            sp.dma_start(vrows[C_DS:C_DS + 8, :], d_skip[0].rearrange("(k g) c -> k (g c)", k=8)).then_inc(vrows_loaded, 16)
            load(PI.load, 0, cols(w_in_k, 0, KD, IF_M, P))
            sp.wait_ge(c_loaded, C_LOADS)
            for j in range(2):
                for m in range(4):
                    load(PU.load + 4 * j + m, 0, cols(w_in_k, 4 * m, 4, U_S + 512 * j, 512))
            with sp.Fori(0, 2) as i:
                n = PA.load
                for base in (Q_M, K_M, V_M, O_M):
                    for m in range(4):
                        load(n, 4 * i, cols(w_in_k, 4 * m, 4, base, 512, i * 512))
                        n += 1
            with sp.Fori(0, 2) as i:
                n = PB.load
                for u in range(2):
                    for base in (Q_A, K_A, V_A):
                        for g in range(NG):
                            for m in range(2):
                                load(n, 9 * i, cols(w_in_k, 8 * m, 8, base + g * AH * P + u * 256, 256, i * 512))
                                n += 1
            w_glu_k = w_glu[0].rearrange("(k p) n -> p k n", p=P)
            with sp.Fori(0, 2) as i:
                n = PC.load
                for base in (0, 1024):
                    for m in range(2):
                        load(n, i, cols(w_glu_k, 4 * m, 4, base, 512, i * 512))
                        n += 1
            br_k = [w[0].rearrange("(k p) n -> p k n", p=P) for w in (w_br_a, w_br_b, w_br_c)]
            with sp.Fori(0, 2) as i:
                n = PD.load
                for u in range(2):
                    for b in range(3):
                        for m in range(4):
                            load(n, 9 * i, cols(w_in_k, 4 * m, 4, GATE + b * D + u * 512, 512, i * 1024))
                            n += 1
                        for m in range(2):
                            load(n, 9 * i, cols(br_k[b], 4 * m, 4, u * 512, 512, i * 512 * 2))
                            n += 1
            w_out_k = w_out[0].rearrange("(k p) n -> p k n", p=P)
            with sp.Fori(0, 2) as i:
                n = PW.load
                for u in range(2):
                    for m in range(4):
                        load(n, 2 * i, cols(w_out_k, 4 * m, 4, u * 512, 512, i * 1024))
                        n += 1
            ff1_k = w_ff1[0].rearrange("(k p) n -> p k n", p=P)
            ff2_k = w_ff2[0].rearrange("(h k p) n -> p h k n", p=P, h=2)
            with sp.Fori(0, 2) as h:
                with sp.Fori(0, 4) as i:
                    n = PF.load
                    for u in range(2):
                        for m in range(4):
                            load(n, 16 * h + 2 * i, cols(ff1_k, 4 * m, 4, u * 512, 512, h * 4096 + i * 1024))
                            n += 1
                with sp.Fori(0, 2) as i:
                    n = PF.load + 4 * LOADS_F1
                    for u in range(2):
                        for m in range(8):
                            load(n, 16 * h + 4 * i,
                                 ff2_k[:, :, :, u * 512:][:, bass.ds(h, 1), 4 * m:4 * m + 4, bass.ds(i * 1024, 512)].rearrange(
                                     "p h k n -> p (h k) n"))
                            n += 1
            for t in range(TT):
                for n, half in enumerate((slice(0, D // 2), slice(D // 2, D))):
                    sp.wait_ge(out_ready, 2 * t + n + 1)
                    sp.dma_start(out[0, t * P:(t + 1) * P, half], x1[:, t, half]).then_inc(stored, 16)
            sp.wait_ge(stored, 16 * 2 * TT)

        @block.tensor
        def _(pe):
            def transposes(src, n0, batches=range(8)):
                for b in batches:
                    if b >= 4:
                        pe.wait_ge(xlo_ready, n0 + b - 3)
                    for k in range(2):
                        for t in range(TT):
                            mm = pe.matmul(ps[:, SPARE + b % 4, k * TOK + t * P:k * TOK + (t + 1) * P],
                                           src[:, t, (2 * b + k) * P:(2 * b + k + 1) * P], diag[:, t, :],
                                           start=True, stop=True)
                    mm.then_inc(trans_ready, 1)

            pe.wait_ge(vrows_loaded, 96)
            pe.wait_ge(c_loaded, C_LOADS)
            pe.wait_ge(srows_ready, 1)
            pe.transpose(ps[:, 0, 0:P], vrows[:], ident[:])
            pe.transpose(ps[:, 0, P:P + 96], srows[:], ident[0:96, 0:96])
            pe.matmul(ps[0:24, 1, 0:384], table[:], onehot[:], start=True, stop=True).then_inc(cols_ready, 1)
            pe.wait_ge(diag_ready, 1)
            transposes(xs, 0, range(4))
            pe.wait_ge(cols_copied, 2)

            def xn_wait(q):
                pe.wait_ge(xlo_ready, 4 * q + 4)

            def rest_of_xn(q):
                if q == 0:
                    transposes(xs, 0, range(4, 8))
            gemm(pe, PI.piece, 0, PI.block, 0, P, False, x_hi, x_lo, npieces=2, xs_wait=xn_wait, after=rest_of_xn)

            def setup_steps(pos):
                if pos == 3:
                    pe.wait_ge(g8_v, 1)
                    pe.matmul(ps[0:MH, SPARE, 0:TOK], ident[0:8, 0:MH], gates8[:], start=True, stop=False,
                              skip_group_check=True)
                    pe.matmul(ps[0:MH, SPARE, 0:TOK], neg_sel[:], fcum[:], start=False, stop=True, skip_group_check=True)
                    pe.matmul(ps[0:MH, SPARE, TOK:2 * TOK], ident[0:8, MH:2 * MH], fcum[:], start=False, stop=True,
                              skip_group_check=True).then_inc(g8_p, 1)
                if pos == 6:
                    pe.wait_ge(g8_v, 2)
                    pe.wait_ge(g8_a, 3)
                    for h in range(MH):
                        pe.matmul(ps[:, SPARE + h // 2, h % 2 * TOK:(h % 2 + 1) * TOK], neg_bc[:, h, :], gr[:, 0, :],
                                  start=h % 2 == 0, stop=True, skip_group_check=True)
                    for t in range(TT):
                        pe.transpose(ps[:, SPARE + 2, t * MH:(t + 1) * MH], gaf[:, 0, t * P:(t + 1) * P], ident[0:MH, 0:MH])
                        mm = pe.transpose(ps[:, SPARE + 2, (2 + t) * MH:(3 + t) * MH], gr[:, 1, t * P:(t + 1) * P],
                                          ident[0:MH, 0:MH])
                    mm.then_inc(g8_p, 1)
                if pos in (12, 15):
                    which = (12, 15).index(pos)
                    padded = (c_pad, b_pad)[which]
                    pe.wait_ge(pad_ready, which + 1)
                    pe.wait_ge(g8_v, 3)
                    for b in range(4):
                        if which:
                            pe.wait_ge(pack_ready, b + 1)
                        for h in range(2):
                            for ri in range(2):
                                t = 2 * b + h
                                src = (padded[:, ri, 4 * t:4 * t + 4, :].rearrange("p j c -> p (j c)") if which
                                       else padded[:, ri, t, :])
                                mm = pe.transpose(ps[:, SPARE + b, h * 256 + ri * P:h * 256 + (ri + 1) * P], src, ident[:])
                        mm.then_inc(btr_ready, 1)
            for j in range(2):
                gemm(pe, PU.piece + 8 * j, 0, PU.block + j, 0, 512, False, x_hi, x_lo,
                     after=lambda q, j=j: setup_steps(8 * j + q))
            end_of_phase(pe, 1)

            def s5_unit(n, q):
                if q in S5_IN:
                    j = S5_IN.index(q)
                    if j == 0:
                        pe.wait_ge(s5_staged, n + 1)
                    pe.wait_ge(bu_free, n * 4 + j + 1)
                    rows = slice(32 * j, 32 * j + 32)
                    for ri in range(2):
                        mm = pe.matmul(ps[:, B_BU, ri * TOK:(ri + 1) * TOK],
                                       s5s[rows, PK_B + ri * P:PK_B + (ri + 1) * P], s5s[rows, PK_U:PK_U + TOK],
                                       start=ri == 0, stop=True, skip_group_check=True)
                    mm.then_inc(bu_ready, 1)
                if q in S5_OUT:
                    j = S5_OUT.index(q)
                    if j == 0:
                        pe.wait_ge(ys_ready, n + 1)
                    pe.wait_ge(xr_ready, n * 4 + j + 1)
                    for ri in range(2):
                        mm = pe.matmul(ps[32 * j:32 * j + 32, B_Y, 0:TOK],
                                       s5s[:, PK_C + ri * P + 32 * j:PK_C + ri * P + 32 * j + 32], n1[:, ri, :],
                                       start=ri == 0, stop=ri == 1, skip_group_check=True)
                    mm.then_inc(y_done, 1)

            with pe.Fori(0, 2) as i:
                def after(pos):
                    s5_unit(i, pos)
                    if pos in (23, 24):
                        h = pos - 23
                        if h == 0:
                            pe.wait_ge(qk_ready, i * 2 + 2)
                        for e in range(2):
                            pe.matmul(ps[:, B_H[h], 0:TOK], kT[:, 2 * h + e, 0:P], qT[:, 2 * h + e, :],
                                      start=e == 0, stop=e == 1, skip_group_check=True)
                        for e in range(2):
                            mm = pe.matmul(ps[:, B_H[h], TOK:TOK + P], kT[:, 2 * h + e, P:TOK],
                                           qT[:, 2 * h + e, P:TOK], start=False, stop=e == 1,
                                           skip_group_check=True)
                        mm.then_inc(sT_ready, 1)
                    if pos == 26:
                        pe.wait_ge(v_ready, i + 1)
                        pe.wait_ge(pT_ready, i * 2 + 2)
                        pe.wait_ge(bu_free, i * 4 + 5)
                        for h in range(2):
                            den = 2 * h
                            pe.matmul(ps[:, B_H[h], 0:TOK], pT[:, h, 0:P], v_m[:, 0, h, :], start=True, stop=True,
                                      skip_group_check=True)
                            pe.matmul(ps[:, B_H[h], TOK:2 * TOK], pT[:, h, P:TOK], v_m[:, 0, h, :], start=False,
                                      stop=False, skip_group_check=True)
                            pe.matmul(ps[:, B_H[h], TOK:2 * TOK], pT[:, h, TOK:384], v_m[:, 1, h, :], start=False,
                                      stop=True, skip_group_check=True)
                            pe.matmul(ps[:, B_BU, den:den + 1], pT[:, h, 0:P], ones, start=h == 0, stop=True,
                                      skip_group_check=True)
                            pe.matmul(ps[:, B_BU, den + 1:den + 2], pT[:, h, P:TOK], ones, start=False, stop=False,
                                      skip_group_check=True)
                            mm = pe.matmul(ps[:, B_BU, den + 1:den + 2], pT[:, h, TOK:384], ones, start=False,
                                           stop=True, skip_group_check=True)
                        mm.then_inc(num_ready, 1)
                    if pos == 31:
                        pe.wait_ge(hn_ready, i + 1)
                        for h in range(2):
                            for e in range(2):
                                for t in range(TT):
                                    mm = pe.transpose(ps[:, B_H[h], e * TOK + t * P:e * TOK + (t + 1) * P],
                                                      hn[:, t, h * TOK + e * P:h * TOK + (e + 1) * P], ident[:])
                        mm.then_inc(hT_ready, 1)
                for b in range(BLOCKS_A):
                    gemm(pe, PA.piece + 8 * b, 4 * i, PA.block + b, 2 * i, 512, b == 2, x_hi, x_lo,
                         after=lambda q, b=b: after(8 * b + q))
            end_of_phase(pe, 2)
            pe.wait_ge(psum_free[(PB.block - 1) % 2], (PB.block + 1) // 2)
            with pe.Fori(0, 2) as i:
                for u in range(2):
                    def after(pos):
                        at_b = 36 * u + pos
                        s5_unit(i * 3 + (2 + at_b // S5_LEN), at_b % S5_LEN)
                        slot = i * 4 + 2 * u
                        if pos in SCORE_AT:
                            a = SCORE_AT.index(pos)
                            if a == 0:
                                pe.wait_ge(aq_ready, i * 6 + 3 * u + 3)
                                pe.wait_ge(ak_ready, i * 6 + 3 * u + 3)
                            else:
                                pe.wait_ge(probT_ready, slot * NG + NG)
                            for g in range(NG):
                                c = 2 * g + a
                                o1 = ps[:, B_SC1 + g // 2, g % 2 * TOK:(g % 2 + 1) * TOK]
                                pe.matmul(o1, aq[:, c, P:TOK], ak[:, c, :], start=True, stop=True)
                                mm = pe.matmul(ps[:, B_SC0, g * P:(g + 1) * P], aq[:, c, 0:P], ak[:, c, 0:P],
                                               start=True, stop=True)
                            mm.then_inc(scored, 1)
                        if pos == TRANS_AT:
                            prob_transposes(slot)
                        if pos == 35:
                            head_out(slot, 0)
                            prob_transposes(slot + 1)
                            head_out(slot + 1, 1)

                    def prob_transposes(slot):
                        pe.wait_ge(prob_ready, slot + 1)
                        for g in range(NG):
                            bank = B_SC1 + g
                            pe.transpose(ps[:, bank, 0:P], prob[:, NG * TOK + g * P:NG * TOK + (g + 1) * P], ident[:])
                            pe.transpose(ps[:, bank, P:2 * P], prob[:, g * TOK:g * TOK + P], ident[:])
                            mm = pe.transpose(ps[:, bank, 2 * P:3 * P], prob[:, g * TOK + P:(g + 1) * TOK], ident[:])
                        mm.then_inc(probT_made, 1)

                    def head_out(slot, a):
                        pe.wait_ge(att_copied, slot + 1)
                        for g in range(NG):
                            pe.wait_ge(probT_ready, slot * NG + (g + 1))
                            if a == 0:
                                pe.wait_ge(av_ready, i * 6 + 3 * u + g + 1)
                            pe.matmul(ps[:, B_PV, 0:TOK], av[:, 0, g, a * P:(a + 1) * P], probT[:, g, 0:TOK],
                                      start=g == 0, stop=False, skip_group_check=True)
                            mm = pe.matmul(ps[:, B_PV, P:TOK], av[:, 1, g, a * P:(a + 1) * P], probT[:, g, TOK:384],
                                           start=False, stop=g == 2, skip_group_check=True)
                        mm.then_inc(att_out, 1)
                    for b in range(9):
                        n = 9 * u + b
                        gemm(pe, PB.piece + n * 4, 9 * i, PB.block + n, 9 * i, 256, b >= 6, x_hi, x_lo, npieces=4,
                             narrow=True, after=lambda q, b=b: after(4 * b + q))
            end_of_phase(pe, 3)
            def z_wait(q):
                pe.wait_ge(z_split_v, q + 1)
            with pe.Fori(0, 2) as i:
                for b in range(2):
                    gemm(pe, PC.piece + 4 * b, i, PC.block + b, i, 512, False, z_hi, z_lo, npieces=4,
                         xs_wait=None if b else z_wait)
            pe.wait_ge(y_split_v, 2)
            with pe.Fori(0, 2) as i:
                for u in range(2):
                    for b in range(3):
                        s, n = PD.piece + 36 * u + 12 * b, PD.block + 6 * u + 2 * b
                        gemm(pe, s, 9 * i, n, 6 * i, 512, False, x_hi, x_lo)
                        if b == 2:
                            pe.wait_ge(y_split_v, 3)
                        gemm(pe, s + 8, 9 * i, n + 1, 6 * i, 512, False, y_hi[:, b], y_lo[:, b], npieces=4)
            def mix_wait(q):
                if q in (0, 6):
                    pe.wait_ge(mix_done, 4 if q else 3)
            with pe.Fori(0, 2) as i:
                for u in range(2):
                    gemm(pe, PW.piece + 8 * u, 2 * i, PW.block + u, i, 512, True, mix_hi, mix_lo,
                         xs_wait=None if u else mix_wait)
            pe.wait_ge(diag_ready, 2)
            transposes(x1, 8)

            def hn_wait(q):
                pe.wait_ge(xlo_ready, 8 + q + 1)
            with pe.Fori(0, 2) as h:
                with pe.Fori(0, 4) as i:
                    for u in range(2):
                        gemm(pe, PF.piece + 8 * u, h * 16 + i * 2, PF.block + u, h * 6 + i, 512, False, x_hi, x_lo,
                             xs_wait=None if u else hn_wait)
                with pe.Fori(0, 2) as i:
                    def h_wait(q):
                        if q in (0, 14):
                            pe.wait_ge(h_ready, h * 8 + (9 if q else 8))
                    for u in range(2):
                        gemm(pe, PF.piece + 64 + 16 * u, h * 16 + i * 4, PF.block + 8 + u, h * 6 + i, 512, True,
                             h_hi, h_lo, npieces=16, xs_wait=None if u else h_wait)

        @block.scalar
        def _(act):
            def out_of_psum(dst, block, func=ACT.Copy, banks=2, width=512):
                act.activation(dst, ps[:, 2 * (block % 2):2 * (block % 2) + banks, 0:width], func).then_inc(
                    psum_free[block % 2], 1)

            def sum_of_squares(src, junk):
                act.activation(junk[:, 0, :], src[:, 0, :], ACT.Square, accum_out=small[:, 0:1]).then_inc(sumsq_ready, 1)

            act.dma_start(ident[:], ident_c).then_inc(c_loaded, 16)
            act.dma_start(srows[0:32, :], lam_re[0].rearrange("(j q) s -> j (q s)", q=2)).then_inc(c_loaded, 16)
            act.dma_start(srows[32:64, :], lam_im[0].rearrange("(j q) s -> j (q s)", q=2)).then_inc(c_loaded, 16)
            act.dma_start(table[:], rel_bias).then_inc(c_loaded, 16)
            act.dma_start(consts[:], consts_c).then_inc(c_loaded, 16)
            act.wait_ge(x_loaded[0], 16)
            sum_of_squares(xs, xs_junk)
            split_hi(act, 0 - AHEAD, 0)
            split_hi(act, 1 - AHEAD, 0)

            def features_hi(n0, gcol, splits={}):
                for b in range(8):
                    act.wait_ge(trans_ready, n0 + b + 1)
                    for k in range(2):
                        kk = 2 * b + k
                        last = act.activation(x_hi[:, kk, :], ps[:, SPARE + b % 4, k * TOK:(k + 1) * TOK], ACT.Copy,
                                              scale=vec[:, gcol + kk:gcol + kk + 1])
                    last.then_inc(xhi_ready, 1)
                    if b in splits:
                        split_hi(act, splits[b] - AHEAD, 0)
            act.wait_ge(cols_copied, 1)
            features_hi(0, C_N1, FIRST_SPLITS)
            pack_u = pack[:, :, PK_U:PK_U + TOK]
            for s in range(2):
                split_hi(act, s, 0)
            act.wait_ge(g_loaded, G_LOADS)
            block_done(act, PI.piece, 2, 0)
            act.activation(gates8[:], ps[0:8, 0, 0:TOK], ACT.Identity, bias=gate_bias[:]).then_inc(psum_free[0], 1)
            act.drain()
            act.activation(gtmp[:, 0, :], gates8[:], ACT.Abs)
            act.drain()
            act.activation(gtmp[:, 1, :], gtmp[:, 0, :], ACT.Exp, scale=-1.0)
            act.wait_ge(cols_copied, 2)
            act.activation(s5p[:, 3, :], s5p[:, 2, :], ACT.Exp).then_inc(par_a, 1)
            act.drain()
            act.activation(gtmp[:, 2, :], gtmp[:, 1, :], ACT.Ln, bias=1.0).then_inc(g8_a, 2)
            for s in range(2, 4):
                split_hi(act, s, 0)
            act.wait_ge(par_v, 1)
            act.activation(s5p[:, 5, :], s5p[:, 4, :], ACT.Exp).then_inc(par_a, 1)
            act.activation(s5p[:, 7, :].bitcast(F32R), s5p[:, 6, :], ACT.Copy).then_inc(par_a, 1)
            for s in range(4, 6):
                split_hi(act, s, 0)
            act.wait_ge(g8_v, 2)
            act.activation(gr[:, 1, :], gaf[:, 1, :], ACT.Exp, scale=-1.0).then_inc(g8_a, 1)
            for s in range(6, 10):
                split_hi(act, s, 0)
            act.wait_ge(par_v, 2)
            act.activation(s5p[:, 20, :], s5p[:, 19, :], ACT.Sin, scale=math.pi)
            act.activation(s5p[:, 21, :], s5p[:, 19, :], ACT.Abs).then_inc(par_a, 1)
            act.wait_ge(par_a, 4)
            act.activation(s5p[:, 22, :], s5p[:, 21, :], ACT.Sin, bias=half_pi, scale=-math.pi)
            act.activation(s5p[:, 23, :], s5p[:, 21, :], ACT.Sin, bias=half_pi, scale=-2.0 * math.pi).then_inc(par_a, 1)
            block_done(act, PU.piece, 8, 0)
            act.activation(pack_u[:, 0:4, :], ps[:, 2:4, :].rearrange("p b (c t) -> p (b c) t", t=TOK),
                           ACT.Copy).then_inc(psum_free[1], 1)
            for s in range(10, 18):
                split_hi(act, s, 0)
                if s in (14, 17):
                    which = (14, 17).index(s)
                    for b in range(4):
                        act.wait_ge(btr_ready, 4 * which + b + 1)
                        col = PK_B if which else PK_C
                        act.activation(pack[:, 2 * b:2 * b + 2, col:col + 256],
                                       ps[:, SPARE + b, :].rearrange("p (t c) -> p t c", t=2), ACT.Copy).then_inc(pack_ready, 1)
            block_done(act, PU.piece + 8, 8, 0)
            act.activation(pack_u[:, 4:8, :], ps[:, 0:2, :].rearrange("p b (c t) -> p (b c) t", t=TOK),
                           ACT.Copy).then_inc(psum_free[0], 1)
            end_of_phase(act, 1, wait=True)

            def s5_unit(n, q):
                if q == 0:
                    act.wait_ge(unit_done, n + 1)
                    act.activation(s5s[:], pack[:, bass.ds(n, 1), :].rearrange("p a c -> p (a c)"), ACT.Copy).then_inc(
                        s5_staged, 1)
                if q in S5_SINE:
                    h = S5_SINE.index(q)
                    act.wait_ge(psi_ready, n * 2 + h + 1)
                    act.wait_ge(rot_done, n * 4 + 2 * h + 1)
                    ph = psi[:, 2 * h:2 * h + 2, :]
                    act.activation(s2[:], ph, ACT.Sin, scale=math.pi)
                    act.drain()
                    act.activation(ph, ph, ACT.Abs)
                    act.drain()
                    act.activation(c2[:], ph, ACT.Sin, bias=half_pi, scale=-2.0 * math.pi)
                    act.activation(ph, ph, ACT.Sin, bias=half_pi, scale=-math.pi).then_inc(sins_ready, 1)
                if q == S5_LEN - 1:
                    act.wait_ge(gelu_in, n + 1)
                    act.activation(m2[:, 1, :], m2[:, 0, :], ACT.Sigmoid, scale=2.0 * math.sqrt(2.0 / math.pi)).then_inc(
                        gelu_sig, 1)

            with act.Fori(0, 2) as i:
                def conv_copy(b):
                    s = PA.piece + 8 * b
                    block_done(act, s, 8, 4 * i)
                    if b:
                        act.wait_ge(qk_ready, i * 2 + 1)
                    act.activation(qk_raw[:], ps[:, 2 * ((PA.block + b) % 2):2 * ((PA.block + b) % 2) + 2, :],
                                   ACT.Copy).then_inc(psum_free[(PA.block + b) % 2], 1)
                    act.drain()
                    act.sem_inc(conv_in, 1)
                for pos in range(32):
                    split_hi(act, PA.piece + pos, 4 * i)
                    s5_unit(i, pos)
                    if pos == 7:
                        conv_copy(0)
                    if pos in SILU_AT:
                        b = SILU_AT.index(pos)
                        act.wait_ge(conv_acc, i * 2 + b + 1)
                        act.activation(qk_raw[:], acc[:], ACT.Sigmoid).then_inc(conv_sig, 1)
                    if pos == 15:
                        conv_copy(1)
                    if pos == 6:
                        for h in range(2):
                            act.wait_ge(wexp_in, i * 2 + h + 1)
                            act.activation(wexp[:, h, 0:TOK], wexp[:, h, 0:TOK], ACT.Exp, bias=conv_s[:, 44 + h:45 + h])
                            act.activation(wexp[:, h, TOK:384], wexp[:, h, TOK:384], ACT.Exp,
                                           bias=conv_s[:, 46 + h:47 + h]).then_inc(wexp_ready, 1)
                    if pos == 23:
                        s, blk = PA.piece + 16, PA.block + 2
                        block_done(act, s, 8, 4 * i)
                        act.wait_ge(num_ready, i + 1)
                        act.activation(v_m[:],
                                       ps[:, 2 * (blk % 2):2 * (blk % 2) + 2, :].rearrange("p t (h e) -> p t h e", h=2),
                                       ACT.Copy).then_inc(psum_free[blk % 2], 1)
                        act.drain()
                        act.sem_inc(v_ready, 1)
                    if pos == 28:
                        act.wait_ge(rec_ready, i + 1)
                        for m in range(4):
                            last = act.activation(qk_raw[:, m, :], ps[:, B_H[m // 2], m % 2 * TOK:(m % 2 + 1) * TOK],
                                                  ACT.Square, scale=small[:, 38 + m:39 + m],
                                                  accum_out=small[:, 42 + m:43 + m])
                        last.then_inc(hss_ready, 1)
                s, blk = PA.piece + 24, PA.block + 3
                block_done(act, s, 8, 4 * i)
                act.activation(o_sig[:], ps[:, 2 * (blk % 2):2 * (blk % 2) + 2, :], ACT.Sigmoid).then_inc(
                    psum_free[blk % 2], 1)
                act.drain()
                act.sem_inc(o_ready, 1)
            end_of_phase(act, 2, wait=True)

            with act.Fori(0, 2) as i:
                for u in range(2):
                    def bias_tiles(a):
                        act.wait_ge(logits_ready, i * 4 + 2 * u + a + 1)
                        act.dma_start(rel[:], rel_tiles[bass.ds(i * 4 + (2 * u + a), 1)].rearrange(
                            "a p g t -> (a p) g t")).then_inc(rel_loaded, 16)

                    def copy_probT():
                        for g in range(NG):
                            act.activation(probT[:, g, :], ps[:, B_SC1 + g, 0:384], ACT.Copy).then_inc(probT_ready, 1)

                    for pos in range(36):
                        split_hi(act, PB.piece + 36 * u + pos, 9 * i)
                        slot = i * 4 + 2 * u
                        if pos % 4 == 3:
                            b = pos // 4
                            blk = PB.block + 9 * u + b
                            block_done(act, PB.piece + 36 * u + 4 * b, 4, 9 * i)
                            src = ps[:, blk % 2, :].rearrange("p (a t) -> p a t", a=2)
                            if b < 6:
                                dst = (aq if b < 3 else ak)[:, 2 * (b % 3):2 * (b % 3) + 2, :]
                                act.wait_ge(scored, slot + 1)
                            else:
                                dst = av[:, :, b - 6, :]
                                act.wait_ge(att_out, slot + 1)
                            act.activation(dst, src, ACT.Copy).then_inc(psum_free[blk % 2], 1)
                            act.drain()
                            act.sem_inc((aq_ready, ak_ready, av_ready)[b // 3], 1)
                        at_b = 36 * u + pos
                        s5_unit(i * 3 + (2 + at_b // S5_LEN), at_b % S5_LEN)
                        if pos == 14:
                            bias_tiles(0)
                        if pos in EXP_AT:
                            a = EXP_AT.index(pos)
                            act.wait_ge(logits_ready, slot + a + 2)
                            act.activation(prob[:, 0:NG * TOK], prob[:, 0:NG * TOK], ACT.Exp, bias=small[:, 22:23],
                                           accum_out=small[:, 24:25])
                            act.activation(prob[:, NG * TOK:], prob[:, NG * TOK:], ACT.Exp, bias=small[:, 23:24],
                                           accum_out=small[:, 25:26]).then_inc(exps_ready, 1)
                            if a == 0:
                                bias_tiles(1)
                        if pos == PROBT_AT:
                            act.wait_ge(probT_made, slot + 2)
                            act.wait_ge(att_out, slot + 1)
                            copy_probT()
                    act.wait_ge(probT_made, slot + 3)
                    act.wait_ge(att_out, slot + 2)
                    copy_probT()
            end_of_phase(act, 3, wait=True)

            act.wait_ge(unit_done, 9)
            for q in range(4):
                act.activation(z_hi[:, 2 * q:2 * q + 2], y_s[:, 2 * q:2 * q + 2], ACT.Copy).then_inc(z_split_a, 1)
            for b, y in enumerate((y_a, y_b)):
                act.activation(y_hi[:, b], y[:], ACT.Copy).then_inc(y_split_a, 1)
            with act.Fori(0, 2) as i:
                for b in range(2):
                    s, blk = PC.piece + 4 * b, PC.block + b
                    for q in range(4):
                        split_hi(act, s + q, i)
                    block_done(act, s, 4, i)
                    act.wait_ge(glu_out, i + 1)
                    act.activation((z_lin, z_sig)[b][:], ps[:, 2 * (blk % 2):2 * (blk % 2) + 2, :],
                                   (ACT.Copy, ACT.Sigmoid)[b]).then_inc(psum_free[blk % 2], 1)
                    act.drain()
                    act.sem_inc(glu_in, 1)
            act.wait_ge(glu_out, 3)
            act.activation(y_hi[:, 2], y_s[:], ACT.Copy).then_inc(y_split_a, 1)

            with act.Fori(0, 2) as i:
                for u in range(2):
                    for b in range(3):
                        s, blk = PD.piece + 36 * u + 12 * b, PD.block + 6 * u + 2 * b
                        for q in range(8):
                            split_hi(act, s + q, 9 * i)
                        block_done(act, s, 8, 9 * i)
                        act.wait_ge(mix_ready, i * 2 + u + 1)
                        act.activation(gate_sig[:, b], ps[:, 2 * (blk % 2):2 * (blk % 2) + 2, :],
                                       ACT.Sigmoid).then_inc(psum_free[blk % 2], 1)
                        act.drain()
                        act.sem_inc(gsig_ready, 1)
                        for q in range(4):
                            split_hi(act, s + 8 + q, 9 * i)
                    act.wait_ge(mix_ready, i * 2 + u + 2)
                    act.activation(mix_hi[:, bass.ds(i * 8 + 4 * u, 4), :], mix[:], ACT.Copy).then_inc(mixhi_ready, 1)

            with act.Fori(0, 2) as i:
                for s in range(16):
                    split_hi(act, PW.piece + s, 2 * i)
            act.wait_ge(x1_done, 4)
            sum_of_squares(x1, sq_junk)
            features_hi(8, C_N2)

            def ff1(h, i):
                for u in range(2):
                    s, blk = PF.piece + 8 * u, PF.block + u
                    for q in range(8):
                        split_hi(act, s + q, 16 * h + 2 * i)
                    block_done(act, s, 8, 16 * h + 2 * i)
                    act.wait_ge(h_ready, h * 8 + i * 2 + u + 1)
                    act.activation(relu[:].rearrange("p (b n) -> p b n", b=2),
                                   ps[:, 2 * (blk % 2):2 * (blk % 2) + 2, :], ACT.Relu).then_inc(psum_free[blk % 2], 1)
                    act.drain()
                    act.sem_inc(relu_ready, 1)
                    act.activation(h_hi[:, bass.ds(i * 8 + 4 * u, 4), :], relu[:], ACT.Square).then_inc(hhi_ready, 1)
            with act.Fori(0, 2) as h:
                with act.Fori(0, 4) as i:
                    ff1(h, i)
                with act.Fori(0, 2) as i:
                    for s in range(28):
                        split_hi(act, PF.piece + 64 + s, 16 * h + 4 * i)
                    split_unless_last(split_hi, act, h, i)
            act.wait_ge(x1_done, 12)
            sum_of_squares(x1, sq_junk)

        @block.vector
        def _(dve):
            def chain(*ops):
                for op in ops:
                    op()
                    dve.drain()

            def sum_of_squares(src, junk):
                dve.scalar_tensor_tensor(junk[:, 1, :], src[:, 1, :], 1.0, src[:, 1, :], ALU.mult, ALU.mult,
                                         accum_out=small[:, 1:2]).then_inc(sumsq_v_ready, 1)

            def diagonals(n):
                dve.wait_ge(inv_ready, n)
                for t in range(TT):
                    last = dve.tensor_scalar(diag[:, t, :], ident[:], small[:, 4 + t:5 + t], None, ALU.mult)
                last.then_inc(diag_ready, 1)

            def features_lo(n0, gcol, splits={}):
                for b in range(8):
                    dve.wait_ge(xhi_ready, n0 + b + 1)
                    for k in range(2):
                        kk = 2 * b + k
                        last = dve.scalar_tensor_tensor(x_lo[:, kk, :], ps[:, SPARE + b % 4, k * TOK:(k + 1) * TOK],
                                                        vec[:, gcol + kk:gcol + kk + 1], f(x_hi[:, kk, :]),
                                                        ALU.mult, ALU.subtract)
                    last.then_inc(xlo_ready, 1)
                    if b in splits:
                        split_lo(dve, splits[b] - AHEAD, 0)

            for s in (bu_free, ys_ready, unit_done, att_copied, glu_out, mix_ready, h_ready, rot_done, att_out,
                      scored, num_ready, y_done, logits_ready, probT_made):
                dve.sem_inc(s, 1)
            dve.wait_ge(g_loaded, G_LOADS)
            dve.tensor_copy(srows[64:96, :].rearrange("p (q s) -> p q s", q=2), bcast(ldt[64:96, :], 2, ST)).then_inc(
                srows_ready, 1)
            dve.wait_ge(x_loaded[1], 16)
            sum_of_squares(xs, xs_junk)
            dve.wait_ge(cols_ready, 1)
            dve.tensor_copy(vec[:], ps[:, 0, 0:P]).then_inc(cols_copied, 1)
            dve.tensor_copy(s5p[:, 0:3, :], ps[:, 0, P:P + 96].rearrange("p (a b) -> p a b", a=3))
            diagonals(1)
            dve.tensor_scalar(neg_sel[:], ident[0:8, MH:2 * MH], -1.0, None, ALU.mult)
            dve.tensor_scalar(neg_bc[:], bcast(ident[0:MH, 0:MH], 2, P), -1.0, None, ALU.mult)
            split_lo(dve, 0 - AHEAD, 0)
            dve.tensor_tensor(relval[:], ps[0:24, 1, 0:384], relmask[:], ALU.add)
            dve.drain()
            dve.sem_inc(cols_copied, 1)
            dve.tensor_tensor(s5p[:, 15:17, :], s5p[:, 0:2, :], s5p[:, 0:2, :], ALU.mult)
            dve.drain()
            dve.tensor_tensor(s5p[:, 16, :], s5p[:, 15, :], s5p[:, 16, :], ALU.add)
            dve.drain()
            dve.reciprocal(s5p[:, 16, :], s5p[:, 16, :]).then_inc(rden_ready, 1)
            split_lo(dve, 1 - AHEAD, 0)
            features_lo(0, C_N1, FIRST_SPLITS)

            def split_range(a, b):
                for s in range(a, b):
                    split_lo(dve, s, 0)
            split_range(0, 2)
            dve.memset(gtmp[:, 3, :], 1.0)
            dve.wait_ge(g8_a, 2)
            dve.tensor_scalar(gtmp[:, 0, :], gates8[:], 0.0, None, ALU.min)
            dve.drain()
            dve.tensor_tensor(gtmp[:, 0, :], gtmp[:, 0, :], gtmp[:, 2, :], ALU.subtract)
            dve.drain()
            dve.tensor_tensor_scan(fcum[:], gtmp[:, 3, :], gtmp[:, 0, :], 0.0, ALU.mult, ALU.add).then_inc(g8_v, 1)
            split_range(2, 5)
            dve.wait_ge(g8_p, 1)
            dve.tensor_copy(gaf[:], ps[0:MH, SPARE, :].rearrange("p (a t) -> p a t", a=2))
            dve.drain()
            dve.tensor_tensor_scan(gr[:, 0, :], gaf[:, 0, :], gaf[:, 0, :], 0.0, ALU.max, ALU.max)
            dve.drain()
            dve.tensor_tensor(gaf[:, 1, :], gaf[:, 1, :], gr[:, 0, :], ALU.add).then_inc(g8_v, 1)
            split_range(5, 10)
            dve.wait_ge(g8_p, 2)
            for b in range(2):
                dve.tensor_copy(runmax_bc[:, 2 * b:2 * b + 2, :], ps[:, SPARE + b, :].rearrange("p (a t) -> p a t", a=2))
            dve.tensor_copy(acols[:], ps[:, SPARE + 2, 0:4 * MH].rearrange("p (a h) -> p a h", a=4)).then_inc(g8_v, 1)
            split_range(10, 18)
            end_of_phase(dve, 1)

            def pair_in(n, j):
                dve.wait_ge(bu_ready, n * 4 + j + 1)
                bu = ps[:, B_BU, :].rearrange("p (r t) -> p r t", r=2)
                dve.tensor_tensor(m1[:], bu, bcast(c2[:, j % 2, :], 1, 2), ALU.mult)
                dve.tensor_tensor(m2[:], bu, bcast(s2[:, j % 2, :], 1, 2), ALU.mult).then_inc(bu_free, 1)
                dve.drain()
                dve.tensor_tensor(zin[:, 0, :], m1[:, 0, :], m2[:, 1, :], ALU.add)
                dve.tensor_tensor(zin[:, 1, :], m1[:, 1, :], m2[:, 0, :], ALU.subtract)
                dve.drain()
                for ri in range(2):
                    last = dve.tensor_tensor_scan(m1[:, ri, :], bcast(s5s[:, PK_MAG + j:PK_MAG + j + 1], 1, TOK)[:, :, 0],
                                                  zin[:, ri, :], 0.0, ALU.mult, ALU.add)
                last.then_inc(z_ready, 1)

            def s5_unit(n, q):
                if q in S5_SINE:
                    h = S5_SINE.index(q)
                    dve.wait_ge(sins_ready, n * 2 + h + 1)
                    dve.scalar_tensor_tensor(s2[:], s2[:], -2.0, psi[:, 2 * h:2 * h + 2, :], ALU.mult, ALU.mult).then_inc(
                        s2_ready, 1)
                    dve.drain()
                if q in S5_IN:
                    j = S5_IN.index(q)
                    dve.wait_ge(rot_done, n * 4 + j + 1)
                    pair_in(n, j)
                if q == S5_LEN - 1:
                    dve.wait_ge(y_done, n * 4 + 5)
                    y0, t0, t1 = zin[:, 0, :], zin[:, 1, :], m2[:, 0, :]
                    dve.scalar_tensor_tensor(y0, s5s[:, PK_U:PK_U + TOK], s5s[:, PK_D:PK_D + 1], ps[:, B_Y, 0:TOK],
                                             ALU.mult, ALU.add).then_inc(ys_ready, 1)
                    dve.drain()
                    chain(lambda: dve.tensor_tensor(t0, y0, y0, ALU.mult),
                          lambda: dve.tensor_scalar(t0, t0, 0.044715, 1.0, ALU.mult, ALU.add))
                    dve.tensor_tensor(t1, t0, y0, ALU.mult).then_inc(gelu_in, 1)
                    dve.wait_ge(gelu_sig, n + 1)
                    dve.tensor_tensor(y_s[:, bass.ds(n, 1), :].rearrange("p a t -> p (a t)"), y0, m2[:, 1, :],
                                      ALU.mult).then_inc(unit_done, 1)

            with dve.Fori(0, 2) as i:
                dve.tensor_copy(conv_s[:, 0:32].rearrange("p (j b c) -> p (j b) c", j=4, b=2),
                                vec[:, C_CW:C_CW + 64].rearrange("p (b c) -> p b c", c=8)[:, :, bass.ds(i * 4, 4)])
                dve.tensor_copy(conv_s[:, 32:40].rearrange("p (b c) -> p b c", b=2),
                                vec[:, C_CB:C_CB + 16].rearrange("p (b c) -> p b c", c=8)[:, :, bass.ds(i * 4, 4)])
                dve.tensor_copy(conv_s[:, 40:44], vec[:, bass.ds(i * 4 + C_MH, 4)])
                dve.tensor_copy(conv_s[:, 44:48].rearrange("p (t h) -> p t h", t=2), acols[:, 0:2, bass.ds(i * 2, 2)])
                dve.tensor_copy(small[:, 28:32].rearrange("p (h t) -> p t h", t=2), acols[:, 2:4, bass.ds(i * 2, 2)])
                dve.drain()

                def conv(b, j):
                    if j == 3:
                        dve.wait_ge(conv_in, i * 2 + b + 1)
                    d = 3 - j
                    for c in range(4):
                        tap = conv_s[:, j * 8 + b * 4 + c:j * 8 + b * 4 + c + 1]
                        if j == 3:
                            dve.tensor_scalar(acc[:, c, :], qk_raw[:, c, :], tap,
                                              conv_s[:, 32 + b * 4 + c:33 + b * 4 + c], ALU.mult, ALU.add)
                        else:
                            last = dve.scalar_tensor_tensor(acc[:, c, d:TOK], qk_raw[:, c, 0:TOK - d], tap,
                                                            acc[:, c, d:TOK], ALU.mult, ALU.add)
                    if j == 0:
                        last.then_inc(conv_acc, 1)
                    else:
                        dve.drain()

                def silu(b):
                    dve.wait_ge(conv_sig, i * 2 + b + 1)
                    dve.scalar_tensor_tensor((qT, kT)[b][:], acc[:], (1.0, 1.0 / 16.0)[b], qk_raw[:], ALU.mult,
                                             ALU.mult).then_inc(qk_ready, 1)

                def denominators():
                    dve.wait_ge(num_ready, i + 2)
                    dve.scalar_tensor_tensor(small[:, 34:38], ps[:, B_BU, 0:4], -1.0, small[:, 28:32], ALU.mult, ALU.max)
                    dve.drain()
                    dve.tensor_tensor(small[:, 34:38], small[:, 34:38], ps[:, B_BU, 0:4], ALU.max)
                    dve.drain()
                    dve.reciprocal(small[:, 38:42], small[:, 34:38]).then_inc(rec_ready, 1)

                def head_norms():
                    dve.wait_ge(hinv_ready, i + 1)
                    dve.scalar_tensor_tensor(small[:, 58:62], small[:, 50:54], 16.0, small[:, 38:42], ALU.mult, ALU.mult)
                    dve.drain()
                    for m in range(4):
                        last = dve.tensor_scalar(hn[:, m % 2, m // 2 * TOK:(m // 2 + 1) * TOK],
                                                 ps[:, B_H[m // 2], m % 2 * TOK:(m % 2 + 1) * TOK],
                                                 small[:, 58 + m:59 + m], None, ALU.mult)
                    last.then_inc(hn_ready, 1)

                for pos in range(32):
                    split_lo(dve, PA.piece + pos, 4 * i)
                    s5_unit(i, pos)
                    if pos == 5:
                        for h in range(2):
                            rm = runmax_bc[:, bass.ds(i * 2 + h, 1), :].rearrange("p a t -> p (a t)")
                            rm1 = runmax_bc[:, bass.ds(i * 2 + h, 1), P:TOK].rearrange("p a t -> p (a t)")
                            dve.tensor_tensor(wexp[:, h, 0:TOK], masks[:, 0:TOK], rm, ALU.add)
                            dve.tensor_tensor(wexp[:, h, TOK:384], masks[:, TOK:384], rm1, ALU.add).then_inc(wexp_in, 1)
                    if pos in CONV_AT[0]:
                        conv(0, 3 - CONV_AT[0].index(pos))
                    if pos in CONV_AT[1]:
                        conv(1, 3 - CONV_AT[1].index(pos))
                    if pos in SILU_AT:
                        silu(SILU_AT.index(pos))
                    if pos in (24, 25):
                        h = pos - 24
                        dve.wait_ge(sT_ready, i * 2 + h + 1)
                        if h == 0:
                            dve.wait_ge(wexp_ready, i * 2 + 2)
                        dve.tensor_tensor(pT[:, h, :], ps[:, B_H[h], 0:384], wexp[:, h, :], ALU.mult).then_inc(pT_ready, 1)
                    if pos == 27:
                        denominators()
                    if pos == 28:
                        head_norms()
                dve.wait_ge(hT_ready, i + 1)
                dve.wait_ge(o_ready, i + 1)
                for c in range(4):
                    dve.scalar_tensor_tensor(y_a[:, bass.ds(i * 4 + c, 1), :].rearrange("p a t -> p (a t)"),
                                             ps[:, B_H[c // 2], c % 2 * TOK:(c % 2 + 1) * TOK],
                                             conv_s[:, 40 + c:41 + c], o_sig[:, c, :], ALU.mult, ALU.mult)
                dve.drain()
            end_of_phase(dve, 2)

            with dve.Fori(0, 2) as i:
                for u in range(2):
                    slot = i * 4 + 2 * u

                    def logits(a):
                        dve.wait_ge(scored, slot + a + 2)
                        dve.wait_ge(rel_loaded, i * 64 + (2 * u + a + 1) * 16)
                        dve.wait_ge(probT_made, slot + a + 1)
                        sc = ps[:, B_SC1:B_SC1 + 2, :].rearrange("p b n -> p (b n)")
                        dve.scalar_tensor_tensor(prob[:, 0:NG * TOK], sc[:, 0:NG * TOK], P ** -0.5,
                                                 rel[:].rearrange("p g t -> p (g t)"), ALU.mult, ALU.add)
                        dve.scalar_tensor_tensor(prob[:, NG * TOK:].rearrange("p (g t) -> p g t", g=NG),
                                                 ps[:, B_SC0, 0:384].rearrange("p (g t) -> p g t", g=NG), P ** -0.5,
                                                 rel[:, :, P:TOK], ALU.mult, ALU.add)
                        dve.drain()
                        dve.tensor_reduce(small[:, 22:23], prob[:, 0:NG * TOK], AX_X, ALU.max, negate=True)
                        dve.tensor_reduce(small[:, 23:24], prob[:, NG * TOK:], AX_X, ALU.max, negate=True).then_inc(
                            logits_ready, 1)

                    def weights(a):
                        dve.wait_ge(exps_ready, slot + a + 1)
                        dve.reciprocal(small[:, 26:28], small[:, 24:26])
                        dve.drain()
                        dve.tensor_scalar(prob[:, 0:NG * TOK], prob[:, 0:NG * TOK], small[:, 26:27], None, ALU.mult)
                        dve.tensor_scalar(prob[:, NG * TOK:], prob[:, NG * TOK:], small[:, 27:28], None, ALU.mult).then_inc(
                            prob_ready, 1)

                    def head_copy(a):
                        dve.wait_ge(att_out, slot + a + 2)
                        dve.tensor_copy(y_b[:, bass.ds(i * 4 + (2 * u + a), 1), :].rearrange("p a t -> p (a t)"),
                                        ps[:, B_PV, 0:TOK]).then_inc(att_copied, 1)
                    for pos in range(36):
                        split_lo(dve, PB.piece + 36 * u + pos, 9 * i)
                        if pos in WEIGHT_AT:
                            weights(WEIGHT_AT.index(pos))
                        at_b = 36 * u + pos
                        s5_unit(i * 3 + (2 + at_b // S5_LEN), at_b % S5_LEN)
                        if pos in LOGIT_AT:
                            logits(LOGIT_AT.index(pos))
                    head_copy(0)
                    head_copy(1)
            end_of_phase(dve, 3)

            for q in range(4):
                dve.wait_ge(z_split_a, q + 1)
                dve.tensor_tensor(z_lo[:, 2 * q:2 * q + 2], y_s[:, 2 * q:2 * q + 2], f(z_hi[:, 2 * q:2 * q + 2]),
                                  ALU.subtract).then_inc(z_split_v, 1)
            for b, y in enumerate((y_a, y_b)):
                dve.wait_ge(y_split_a, b + 1)
                dve.tensor_tensor(y_lo[:, b], y[:], f(y_hi[:, b]), ALU.subtract).then_inc(y_split_v, 1)
            with dve.Fori(0, 2) as i:
                for s in range(8):
                    split_lo(dve, PC.piece + s, i)
                dve.wait_ge(glu_in, i * 2 + 2)
                dve.tensor_tensor(y_s[:, bass.ds(i * 4, 4), :], z_lin[:], z_sig[:], ALU.mult).then_inc(glu_out, 1)
            dve.wait_ge(y_split_a, 3)
            dve.tensor_tensor(y_lo[:, 2], y_s[:], f(y_hi[:, 2]), ALU.subtract).then_inc(y_split_v, 1)

            with dve.Fori(0, 2) as i:
                for u in range(2):
                    for b in range(3):
                        s, blk = PD.piece + 36 * u + 12 * b, PD.block + 6 * u + 2 * b
                        for q in range(12):
                            split_lo(dve, s + q, 9 * i)
                        block_done(dve, s + 8, 4, 9 * i)
                        dve.wait_ge(gsig_ready, i * 6 + 3 * u + b + 1)
                        src = ps[:, 2 * ((blk + 1) % 2):2 * ((blk + 1) % 2) + 2, :].rearrange("p b (c t) -> p (b c) t", t=TOK)
                        dve.tensor_tensor((mix_t if b else mix)[:], src, gate_sig[:, b], ALU.mult).then_inc(
                            psum_free[(blk + 1) % 2], 1)
                        dve.drain()
                        if b:
                            add_op = dve.tensor_tensor(mix[:], mix[:], mix_t[:], ALU.add)
                            if b == 2:
                                add_op.then_inc(mix_ready, 1)
                            dve.drain()
                    dve.wait_ge(mixhi_ready, i * 2 + u + 1)
                    dst = bass.ds(i * 8 + 4 * u, 4)
                    dve.tensor_tensor(mix_lo[:, dst, :], mix[:], f(mix_hi[:, dst, :]), ALU.subtract).then_inc(mix_done, 1)
                    dve.drain()

            def add_to_x1(s, n, o8, blk, c0):
                block_done(dve, s, n, o8)
                dst = x1[:, :, bass.ds(c0, 512)]
                dve.tensor_tensor(dst, ps[:, 2 * (blk % 2):2 * (blk % 2) + 2, :], dst, ALU.add).then_inc(
                    psum_free[blk % 2], 1)
                dve.drain()
                dve.sem_inc(x1_done, 1)

            with dve.Fori(0, 2) as i:
                for u in range(2):
                    for s in range(8):
                        split_lo(dve, PW.piece + 8 * u + s, 2 * i)
                    dve.wait_ge(x1_loaded, 16)
                    add_to_x1(PW.piece + 8 * u, 8, 2 * i, PW.block + u, i * 1024 + u * 512)
            sum_of_squares(x1, sq_junk)
            diagonals(2)
            features_lo(8, C_N2)
            with dve.Fori(0, 2) as h:
                with dve.Fori(0, 4) as i:
                    for u in range(2):
                        for s in range(8):
                            split_lo(dve, PF.piece + 8 * u + s, h * 16 + i * 2)
                        dve.wait_ge(relu_ready, h * 8 + i * 2 + u + 1)
                        dve.tensor_tensor(relu2[:], relu[:], relu[:], ALU.mult)
                        dve.drain()
                        dve.wait_ge(hhi_ready, h * 8 + i * 2 + u + 1)
                        dst = bass.ds(i * 8 + 4 * u, 4)
                        dve.tensor_tensor(h_lo[:, dst, :], relu2[:].rearrange("p (c t) -> p c t", t=TOK),
                                          f(h_hi[:, dst, :]), ALU.subtract).then_inc(h_ready, 1)
                with dve.Fori(0, 2) as i:
                    for u in range(2):
                        for s in range(12 if u else 16):
                            split_lo(dve, PF.piece + 64 + 16 * u + s, h * 16 + i * 4)
                        if u:
                            split_unless_last(split_lo, dve, h, i)
                        add_to_x1(PF.piece + 64 + 16 * u, 16, h * 16 + i * 4, PF.block + 8 + u, i * 1024 + u * 512)
            sum_of_squares(x1, sq_junk)
            dve.wait_ge(inv_ready, 3)
            dve.wait_ge(fg_loaded, 16)
            for t in range(TT):
                for half in (slice(0, D // 2), slice(D // 2, D)):
                    dve.scalar_tensor_tensor(x1[:, t, half], x1[:, t, half], small[:, 4 + t:5 + t], fg_bc[:, half],
                                             ALU.mult, ALU.mult).then_inc(out_ready, 1)

        @block.gpsimd
        def _(gp):
            gp.dma_start(ldt[64:96, :], log_dt[0].rearrange("(j q) -> j q", q=2)).then_inc(g_loaded, 16)
            gp.dma_start(onehot[:], onehot_c).then_inc(g_loaded, 16)
            gp.dma_start(relmask[:], relmask_c).then_inc(g_loaded, 16)
            gp.dma_start(gate_bias[0:4, :], b_igate[0].rearrange("(h a) -> h a", a=1)).then_inc(g_loaded, 16)
            gp.dma_start(gate_bias[4:8, :], b_fgate[0].rearrange("(h a) -> h a", a=1)).then_inc(g_loaded, 16)

            def inverse_root(mean, inv, done):
                gp.drain()
                gp.tensor_tensor(inv, mean, bcast(minus_half, 1, mean.shape[-1])[:, :, 0], ALU.pow).then_inc(done, 1)

            def token_inverse_rms(n):
                gp.wait_ge(sumsq_ready, n)
                gp.wait_ge(sumsq_v_ready, n)
                gp.tensor_scalar(small[:, 2:4], small[:, 0:2], 1.0 / D, EPS, ALU.mult, ALU.add)
                inverse_root(small[:, 2:4], small[:, 4:6], inv_ready)
            gp.wait_ge(c_loaded, C_LOADS)
            token_inverse_rms(1)
            for ri, w in enumerate((c_re, c_im)):
                gp.dma_start(c_raw[:, ri], w[0].rearrange("(t g) c s -> (g c) t s", t=8)).then_inc(s5_loaded, 16)
            for ri, w in enumerate((b_re, b_im)):
                gp.dma_start(b_raw[:, ri], w[0].rearrange("(j q) s c -> (q s) j c", q=2)).then_inc(s5_loaded, 16)
            gp.wait_ge(c_loaded, C_LOADS)
            gp.wait_ge(s5_loaded, 64)
            gp.wait_ge(xlo_ready, 8)
            for ri in range(2):
                for half in range(2):
                    gp.tensor_scalar(c_pad[:, ri, :, ST * half:ST * half + ST], c_raw[:, ri], par[:, 2 + half:3 + half],
                                     (1.0, -1.0)[ri], ALU.mult, ALU.mult)
            gp.drain()
            gp.sem_inc(pad_ready, 1)
            gp.wait_ge(cols_copied, 2)
            gp.dma_start(rel_rows, relval[:]).then_inc(rel_stored, 16)
            gp.wait_ge(rel_stored, 16)
            for g in range(NG):
                gp.dma_start(rel_tiles[:, :, g, :],
                             bass.AP(rel_rows.tensor, g * AH * 384 + P - 1, [[384, AH], [-1, P], [1, TOK]])).then_inc(
                    rel_spread, 16)

            def pp(n):
                return s5p[:, n, :]

            def mul(o, a, b):
                gp.tensor_tensor(pp(o), pp(a), pp(b), ALU.mult)
                gp.drain()

            def add(o, a, b, op=ALU.add):
                gp.tensor_tensor(pp(o), pp(a), pp(b), op)
                gp.drain()

            def scaled(o, a, c):
                gp.tensor_scalar(pp(o), pp(a), c, None, ALU.mult)
                gp.drain()

            def whole(o, a, big=ROUND):
                gp.tensor_scalar(pp(o), pp(a), big, big, ALU.add, ALU.subtract)
                gp.drain()
            inv1, inv2, inv3 = inv_two_pi()
            gp.wait_ge(par_a, 1)
            mul(4, 0, 3)
            mul(6, 1, 3)
            gp.sem_inc(par_v, 1)
            gp.wait_ge(par_a, 3)
            add(8, 6, 7, ALU.subtract)
            scaled(9, 7, inv1)
            whole(10, 9)
            add(9, 9, 10, ALU.subtract)
            scaled(11, 7, inv2)
            whole(10, 11)
            add(11, 11, 10, ALU.subtract)
            scaled(12, 8, inv1)
            whole(10, 12)
            add(12, 12, 10, ALU.subtract)
            scaled(13, 8, inv2)
            scaled(14, 7, inv3)
            add(13, 13, 14)
            add(14, 9, 11)
            add(14, 14, 12)
            add(14, 14, 13)
            whole(10, 14)
            add(9, 9, 10, ALU.subtract)
            add(14, 14, 10, ALU.subtract)
            whole(17, 14, GRID16)
            add(15, 9, 17, ALU.subtract)
            add(15, 15, 11)
            add(15, 15, 12)
            add(15, 15, 13)
            scaled(18, 15, -1.0)
            add(19, 17, 15)
            gp.sem_inc(par_v, 1)
            gp.wait_ge(par_a, 5)
            mul(24, 20, 22)
            scaled(24, 24, 2.0)
            mul(25, 5, 23)
            gp.tensor_scalar(pp(25), pp(25), -1.0, None, ALU.add)
            gp.drain()
            mul(26, 5, 24)
            mul(21, 25, 0)
            mul(22, 26, 1)
            add(21, 21, 22)
            gp.wait_ge(rden_ready, 1)
            mul(27, 21, 16)
            mul(21, 26, 0)
            mul(22, 25, 1)
            add(21, 21, 22, ALU.subtract)
            mul(28, 21, 16)
            bt = [bb_t[:, n] for n in range(2)]
            fre, fim = bcast(pp(27), 2, 16), bcast(pp(28), 2, 16)
            for ri in range(2):
                gp.tensor_tensor(bt[0], b_raw[:, ri], fre, ALU.mult)
                gp.tensor_tensor(bt[1], b_raw[:, 1 - ri], fim, ALU.mult)
                gp.drain()
                gp.tensor_tensor(bt[0], bt[0], bt[1], ALU.add if ri else ALU.subtract)
                gp.drain()
                for half in range(2):
                    gp.tensor_scalar(b_pad[:, ri, :, 16 * half:16 * half + 16], bt[0], par[:, half:half + 1], None, ALU.mult)
                gp.drain()
            gp.sem_inc(pad_ready, 1)
            for dst, n in ((theta[:, 0:8, 0:4], 17), (theta[:, 0:8, 4:8], 18), (pack[:, :, PK_MAG:PK_MAG + 4], 5)):
                gp.tensor_copy(dst, pp(n).rearrange("p (t j) -> p t j", j=4))
            gp.memset(theta[:, 8, :], 0.0)
            gp.tensor_copy(pack[:, :, PK_D:PK_D + 1], vec[:, C_DS:C_DS + 8].rearrange("p (t a) -> p t a", a=1))
            gp.memset(pack[:, :, PK_D + 1:PKW], 0.0)
            end_of_phase(gp, 1)

            def angles(n, h):
                ph = psi[:, 2 * h:2 * h + 2, :]

                def part(lo):
                    at_n = theta[:, bass.ds(n, 1), 4 * lo + 2 * h:4 * lo + 2 * h + 2].rearrange("p a j -> p (a j)")
                    return bcast(at_n, 2, TOK)
                gp.tensor_tensor(ph, bcast(iota_t, 1, 2), part(0), ALU.mult)
                gp.drain()
                gp.tensor_scalar(kk2[:], ph, ROUND, ROUND, ALU.add, ALU.subtract)
                gp.drain()
                gp.tensor_tensor(ph, kk2[:], ph, ALU.subtract)
                gp.drain()
                gp.tensor_tensor(kk2[:], bcast(iota_t, 1, 2), part(1), ALU.mult)
                gp.drain()
                gp.tensor_tensor(ph, ph, kk2[:], ALU.add).then_inc(psi_ready, 1)
                gp.drain()

            def rotate_back(n, j):
                gp.wait_ge(z_ready, n * 4 + j + 1)
                gp.wait_ge(y_done, n * 4 + j + 1)
                gp.tensor_tensor(n1[:], m1[:], bcast(c2[:, j % 2, :], 1, 2), ALU.mult)
                gp.tensor_tensor(n2[:], m1[:], bcast(s2[:, j % 2, :], 1, 2), ALU.mult)
                gp.drain()
                gp.sem_inc(rot_done, 1)
                gp.tensor_tensor(n1[:, 0, :], n1[:, 0, :], n2[:, 1, :], ALU.subtract)
                gp.tensor_tensor(n1[:, 1, :], n1[:, 1, :], n2[:, 0, :], ALU.add)
                gp.drain()
                gp.sem_inc(xr_ready, 1)

            def s5_unit(n):
                rotate_back(n, 0)
                for h in range(2):
                    rotate_back(n, 1 + h)
                    gp.wait_ge(s2_ready, n * 2 + (h + 1))
                    angles(n + 1, h)
                rotate_back(n, 3)

            for h in range(2):
                angles(0, h)
            with gp.Fori(0, 2) as i:
                s5_unit(i)
                gp.wait_ge(hss_ready, i + 1)
                gp.tensor_tensor(small[:, 46:50], small[:, 42:46], bcast(eps_256, 1, 4)[:, :, 0], ALU.add)
                inverse_root(small[:, 46:50], small[:, 50:54], hinv_ready)
            gp.wait_ge(rel_spread, 16 * NG)
            end_of_phase(gp, 2)
            with gp.Fori(0, 2) as i:
                for unit in range(3):
                    s5_unit(i * 3 + (2 + unit))
            end_of_phase(gp, 3)
            gp.wait_ge(mix_done, 4)
            gp.dma_start(x1[:], x[0].rearrange("(t p) n -> p t n", p=P)).then_inc(x1_loaded, 16)
            gp.dma_start(fg_bc[:], bass.AP(final_g.tensor, 0, [[0, P], [1, D]])).then_inc(fg_loaded, 16)
            token_inverse_rms(2)
            token_inverse_rms(3)


def t5_bucket(n):
    import numpy as np
    half = 16
    nf = np.maximum(n, half).astype(np.float32)
    large = half + (np.log(nf / np.float32(half)) / np.float32(math.log(2048 / half)) * np.float32(half)).astype(np.int32)
    return np.where(n < half, n, np.minimum(large, 31))


def shape_constants():
    import numpy as np
    p = np.arange(P)
    consts = np.zeros((P, 648), np.float32)
    causal = np.where(p[:, None] <= p[None, :], 0.0, NEG)
    consts[:, 0:P] = causal
    consts[:, 2 * P:3 * P] = causal
    consts[:, 384:640] = np.arange(TOK)
    consts[:, 640] = p < ST
    consts[:, 641] = p >= ST
    consts[:, 642] = p // 16 % 2 == 0
    consts[:, 643] = p // 16 % 2 == 1
    consts[:, 644] = 1.0
    consts[:, 646] = -0.5
    consts[:, 647] = 256 * EPS
    consts[:, 645] = math.pi / 2
    dist = 255 - np.arange(384)
    onehot = (t5_bucket(np.maximum(dist, 0))[None, :] == np.arange(32)[:, None]).astype(np.float32)
    seen = np.stack([(dist >= 0) & (dist <= 128), (dist >= 0) & (dist % 4 == 0), (dist >= 0) & (dist % 16 == 0)])
    relmask = np.repeat(np.where(seen, 0.0, NEG).astype(np.float32), AH, axis=0)
    return {"ident_c": np.eye(P, dtype=np.float32), "consts_c": consts, "onehot_c": onehot, "relmask_c": relmask}


_INS = ['x', 'norm1_g', 'w_in', 'conv_w', 'conv_b', 'b_igate', 'b_fgate', 'mh_norm_g', 'rel_bias', 'lam_re', 'lam_im',
        'log_dt', 'b_re', 'b_im', 'c_re', 'c_im', 'd_skip', 'w_glu', 'w_br_a', 'w_br_b', 'w_br_c', 'w_out', 'norm2_g',
        'w_ff1', 'w_ff2', 'final_g']


def kernel(**inputs):
    import numpy as _np
    import concourse.bacc as _bacc
    from concourse import mybir as _mybir
    from concourse.bass_utils import run_bass_kernel_spmd as _run

    nc = _bacc.Bacc("TRN2", target_bir_lowering=False, num_devices=1)
    arrays, args = {}, []
    values = {name: _np.ascontiguousarray(inputs[name]) for name in _INS}
    values.update(shape_constants())
    for name, a in values.items():
        arrays[f"in_{name}_dram"] = a
        args.append(nc.dram_tensor(f"in_{name}_dram", a.shape, _mybir.dt.from_np(a.dtype), kind="ExternalInput").ap())
    args.append(nc.dram_tensor("out_0_dram", (1, TOK, D), _mybir.dt.float32, kind="ExternalOutput").ap())
    trunk(nc, *args)
    r = _run(nc, [arrays], core_ids=[0])
    return r.results[0]["out_0_dram"]
```
